# Optimizing a Trainium2 kernel written in Bass

```python
import jax
import jax.numpy as jnp
from jax import lax
import numpy as np

D_MODEL = 1024
BATCH = 1
SEQ = 512
DEPTH = 1
DEC_BATCH = 8
DEC_SEQ = 1
PAST_LEN = 2048
PAGE_SIZE = 128

NSA_HEADS = 8
NSA_KV_HEADS = 2
NSA_HD = 64
NSA_GROUP = NSA_HEADS // NSA_KV_HEADS
NSA_SCALE = NSA_HD ** -0.5
CMP_BLOCK = 32
CMP_STRIDE = 16
CMP_HID = 128
SEL_BLOCK = 64
SEL_TOP = 16
WINDOW = 512
SEL_Q_BLOCK = 64
WIN_Q_BLOCK = 128
FORCE_SCORE = 1e9
GDN_HEADS = 4
GDN_DK = 128
GDN_DV = 128
CONV_W = 4
GDN_CHUNK = 64
MEM_TOKENS = 256
MEM_HEADS = 4
MEM_HD = 128
MEM_SCALE = MEM_HD ** -0.5
D_FF = 4 * D_MODEL
ROPE_THETA = 10000.0
EPS = 1e-6

Q_NSA = NSA_HEADS * NSA_HD
KV_NSA = NSA_KV_HEADS * NSA_HD
GDN_QK = GDN_HEADS * GDN_DK
GDN_V = GDN_HEADS * GDN_DV
CONV_DIM = 2 * GDN_QK + GDN_V
MEM_Q = MEM_HEADS * MEM_HD
N_BRANCH = 3
IN_SPLITS = (Q_NSA, 6 * KV_NSA, 3 * NSA_HEADS, CONV_DIM, GDN_HEADS, GDN_HEADS, GDN_V, MEM_Q, N_BRANCH * D_MODEL)
IN_DIM = sum(IN_SPLITS)

kernel_name = 'hybrid_nsa_gdn_memory_decoder_step'

def split_offsets(sizes):
    offs, acc = [], 0
    for s in sizes[:-1]:
        acc += s
        offs.append(acc)
    return offs

def rmsnorm(x, g):
    xf = x.astype(jnp.float32)
    y = xf * lax.rsqrt(jnp.mean(xf * xf, axis=-1, keepdims=True) + EPS)
    return (y * g.astype(jnp.float32)).astype(x.dtype)

def l2norm(x):
    return x * lax.rsqrt(jnp.sum(x * x, axis=-1, keepdims=True) + EPS)

def rope(x, pos):
    half = x.shape[-1] // 2
    inv = ROPE_THETA ** (-jnp.arange(half, dtype=jnp.float32) / half)
    ang = pos.astype(jnp.float32)[:, None] * inv[None, :]
    bshape = (1, pos.shape[0]) + (1,) * (x.ndim - 3) + (half,)
    cos = jnp.cos(ang).reshape(bshape)
    sin = jnp.sin(ang).reshape(bshape)
    xf = x.astype(jnp.float32)
    x1, x2 = xf[..., :half], xf[..., half:]
    return jnp.concatenate([x1 * cos - x2 * sin, x2 * cos + x1 * sin], axis=-1).astype(x.dtype)

def masked_softmax(s, mask):
    s = jnp.where(mask, s.astype(jnp.float32), -1e30)
    p = jax.nn.softmax(s, axis=-1)
    return jnp.where(mask, p, 0.0)

def compress_blocks(x, pe, w1, w2):
    B, N = x.shape[0], x.shape[1]
    R = CMP_BLOCK // CMP_STRIDE
    n_chunks = N // CMP_STRIDE
    n_cmp = n_chunks - R + 1
    chunks = x[:, :n_chunks * CMP_STRIDE].reshape(B, n_chunks, CMP_STRIDE, NSA_KV_HEADS, NSA_HD)
    w1r = w1.reshape(R, CMP_STRIDE, NSA_HD, CMP_HID)
    h = jnp.einsum('ld,ldf->f', pe, w1.reshape(CMP_BLOCK, NSA_HD, CMP_HID))
    for r in range(R):
        h = h + jnp.einsum('bnsgd,sdf->bngf', chunks[:, r:r + n_cmp], w1r[r])
    return jnp.einsum('bngf,fd->bngd', jax.nn.gelu(h), w2)

def cmp_to_sel(n_cmp, n_sel):
    i = jnp.arange(n_cmp)[:, None]
    j = jnp.arange(n_sel)[None, :]
    hit = (i * CMP_STRIDE < (j + 1) * SEL_BLOCK) & (i * CMP_STRIDE + CMP_BLOCK > j * SEL_BLOCK)
    return hit.astype(jnp.float32)

def sel_attend(qg, ksb, vsb, idx, q_pos):
    B, Tq = qg.shape[0], qg.shape[1]
    n_top = idx.shape[-1]
    qb = SEL_Q_BLOCK if Tq % SEL_Q_BLOCK == 0 else Tq
    nqb = Tq // qb
    bi = jnp.arange(B)[:, None, None, None]
    gi = jnp.arange(NSA_KV_HEADS)[None, :, None, None]
    offs = jnp.arange(SEL_BLOCK, dtype=jnp.int32)

    def one_block(args):
        q_blk, idx_blk, pos_blk = args
        kb = ksb[bi, gi, idx_blk]
        vb = vsb[bi, gi, idx_blk]
        s = jnp.einsum('bqgjd,bgqnld->bgjqnl', q_blk, kb) * NSA_SCALE
        kpos = idx_blk[..., None] * SEL_BLOCK + offs
        mask = kpos <= pos_blk[None, None, :, None, None]
        sh = s.shape
        p = masked_softmax(s.reshape(sh[0], sh[1], sh[2], sh[3], -1), mask.reshape(B, NSA_KV_HEADS, 1, qb, -1))
        p = p.reshape(sh).astype(q_blk.dtype)
        return jnp.einsum('bgjqnl,bgqnld->bqgjd', p, vb)

    q_blocks = qg.reshape(B, nqb, qb, NSA_KV_HEADS, NSA_GROUP, NSA_HD).transpose(1, 0, 2, 3, 4, 5)
    idx_blocks = idx.reshape(B, NSA_KV_HEADS, nqb, qb, n_top).transpose(2, 0, 1, 3, 4)
    pos_blocks = q_pos.reshape(nqb, qb)
    out = lax.map(one_block, (q_blocks, idx_blocks, pos_blocks))
    return out.transpose(1, 0, 2, 3, 4, 5).reshape(B, Tq, NSA_KV_HEADS, NSA_GROUP, NSA_HD)

def window_attend(qg, kw, vw, kw_pos, q_pos):
    B, Tq = qg.shape[0], qg.shape[1]
    Nk = kw.shape[1]
    qb = WIN_Q_BLOCK if Tq % WIN_Q_BLOCK == 0 else Tq
    nqb = Tq // qb
    span = WINDOW + qb
    padw = ((0, 0), (WINDOW, 0), (0, 0), (0, 0))
    kp = jnp.pad(kw, padw)
    vp = jnp.pad(vw, padw)
    pos_p = jnp.concatenate([jnp.zeros((WINDOW,), jnp.int32), kw_pos])
    val_p = jnp.concatenate([jnp.zeros((WINDOW,), bool), jnp.ones((Nk,), bool)])
    start = jnp.arange(nqb, dtype=jnp.int32) * qb + (Nk - Tq)
    idx = start[:, None] + jnp.arange(span, dtype=jnp.int32)[None, :]
    kb = kp[:, idx]
    vb = vp[:, idx]
    kpos = pos_p[idx][:, None, :]
    qpos = q_pos.reshape(nqb, qb)[:, :, None]
    mask = val_p[idx][:, None, :] & (kpos <= qpos) & (kpos > qpos - WINDOW)
    qblk = qg.reshape(B, nqb, qb, NSA_KV_HEADS, NSA_GROUP, NSA_HD)
    s = jnp.einsum('bnqgjd,bnkgd->bgjnqk', qblk, kb) * NSA_SCALE
    p = masked_softmax(s, mask).astype(qg.dtype)
    o = jnp.einsum('bgjnqk,bnkgd->bnqgjd', p, vb)
    return o.reshape(B, Tq, NSA_KV_HEADS, NSA_GROUP, NSA_HD)

def nsa_core(q, q_pos, cmp_kv, sel_kv, win_kv, kw_pos, gates, cmp_pe, cmp_w1, cmp_w2):
    B, Tq = q.shape[0], q.shape[1]
    N = cmp_kv.shape[1]
    qg = q.reshape(B, Tq, NSA_KV_HEADS, NSA_GROUP, NSA_HD)
    kcmp = compress_blocks(cmp_kv[:, :, 0], cmp_pe[0], cmp_w1[0], cmp_w2[0])
    vcmp = compress_blocks(cmp_kv[:, :, 1], cmp_pe[1], cmp_w1[1], cmp_w2[1])
    n_cmp = kcmp.shape[1]
    blk_end = jnp.arange(n_cmp, dtype=jnp.int32) * CMP_STRIDE + CMP_BLOCK - 1
    cmask = blk_end[None, :] <= q_pos[:, None]
    s = jnp.einsum('btgjd,bigd->bgjti', qg, kcmp) * NSA_SCALE
    p_cmp = masked_softmax(s, cmask)
    o_cmp = jnp.einsum('bgjti,bigd->btgjd', p_cmp.astype(q.dtype), vcmp)
    n_sel = -(-N // SEL_BLOCK)
    imp = jnp.einsum('bgjti,is->bgts', p_cmp, cmp_to_sel(n_cmp, n_sel))
    jj = jnp.arange(n_sel, dtype=jnp.int32)[None, :]
    imp = jnp.where(jj * SEL_BLOCK <= q_pos[:, None], imp, -jnp.inf)
    imp = jnp.where((jj == 0) | (jj == q_pos[:, None] // SEL_BLOCK), FORCE_SCORE, imp)
    _, idx = lax.top_k(imp, min(SEL_TOP, n_sel))
    pad = ((0, 0), (0, n_sel * SEL_BLOCK - N), (0, 0), (0, 0))
    ksb = jnp.pad(sel_kv[:, :, 0], pad).reshape(B, n_sel, SEL_BLOCK, NSA_KV_HEADS, NSA_HD).transpose(0, 3, 1, 2, 4)
    vsb = jnp.pad(sel_kv[:, :, 1], pad).reshape(B, n_sel, SEL_BLOCK, NSA_KV_HEADS, NSA_HD).transpose(0, 3, 1, 2, 4)
    o_sel = sel_attend(qg, ksb, vsb, idx.astype(jnp.int32), q_pos)
    o_win = window_attend(qg, win_kv[:, :, 0], win_kv[:, :, 1], kw_pos, q_pos)
    g = jax.nn.sigmoid(gates.astype(jnp.float32)).astype(q.dtype).reshape(B, Tq, NSA_KV_HEADS, NSA_GROUP, 3)
    o = g[..., 0:1] * o_cmp + g[..., 1:2] * o_sel + g[..., 2:3] * o_win
    return o.reshape(B, Tq, NSA_HEADS * NSA_HD)

def short_conv(x, buf, w):
    T = x.shape[1]
    xx = jnp.concatenate([buf.astype(x.dtype), x], axis=1)
    y = xx[:, 0:T] * w[0]
    for j in range(1, CONV_W):
        y = y + xx[:, j:j + T] * w[j]
    return jax.nn.silu(y), xx[:, -(CONV_W - 1):]

def gated_delta_chunked(q, k, v, g, beta, s0):
    B, T, H, DK = q.shape
    C = GDN_CHUNK if T % GDN_CHUNK == 0 else T
    nc = T // C

    def to_chunks(a):
        a = a.reshape((B, nc, C, H) + a.shape[3:])
        return jnp.moveaxis(a, (1, 3), (0, 2))

    qc = to_chunks(q * (DK ** -0.5))
    kc = to_chunks(k)
    vc = to_chunks(v)
    bc = to_chunks(beta)
    dec = jnp.cumsum(to_chunks(g), axis=-1)
    tril = jnp.tril(jnp.ones((C, C), bool))
    strict = jnp.tril(jnp.ones((C, C), bool), -1)
    diff = dec[..., :, None] - dec[..., None, :]
    lmask = jnp.where(tril, jnp.exp(jnp.where(tril, diff, 0.0)), 0.0)
    kb = kc * bc[..., None]
    a_mat = jnp.where(strict, jnp.einsum('nbhid,nbhjd->nbhij', kb, kc) * lmask, 0.0)
    t_mat = a_mat + jnp.eye(C, dtype=jnp.float32)
    u = jax.lax.linalg.triangular_solve(t_mat, vc * bc[..., None], left_side=True, lower=True, unit_diagonal=True)
    w = jax.lax.linalg.triangular_solve(t_mat, kb * jnp.exp(dec)[..., None], left_side=True, lower=True, unit_diagonal=True)
    attn_in = jnp.einsum('nbhid,nbhjd->nbhij', qc, kc) * lmask

    def step(S, xs):
        q_i, k_i, u_i, w_i, a_i, d_i = xs
        v_new = u_i - jnp.einsum('bhcd,bhde->bhce', w_i, S)
        o = jnp.einsum('bhcd,bhde->bhce', q_i * jnp.exp(d_i)[..., None], S) + jnp.einsum('bhij,bhje->bhie', a_i, v_new)
        S = S * jnp.exp(d_i[..., -1])[..., None, None] + jnp.einsum('bhcd,bhce->bhde', k_i * jnp.exp(d_i[..., -1:] - d_i)[..., None], v_new)
        return S, o

    s_fin, o = lax.scan(step, s0, (qc, kc, u, w, attn_in, dec))
    o = jnp.moveaxis(o, (0, 2), (1, 3)).reshape(B, T, H, v.shape[-1])
    return o, s_fin

def gdn_mixer(qkv, b_raw, a_raw, z, conv_buf, s0, conv_w, A_log, dt_bias, o_norm):
    B, T, _ = qkv.shape
    c, conv_new = short_conv(qkv, conv_buf, conv_w)
    c = c.astype(jnp.float32)
    q, k, v = jnp.split(c, [GDN_QK, 2 * GDN_QK], axis=-1)
    q = l2norm(q.reshape(B, T, GDN_HEADS, GDN_DK))
    k = l2norm(k.reshape(B, T, GDN_HEADS, GDN_DK))
    v = v.reshape(B, T, GDN_HEADS, GDN_DV)
    beta = jax.nn.sigmoid(b_raw.astype(jnp.float32))
    g = -jnp.exp(A_log.astype(jnp.float32)) * jax.nn.softplus(a_raw.astype(jnp.float32) + dt_bias.astype(jnp.float32))
    o, s_new = gated_delta_chunked(q, k, v, g, beta, s0.astype(jnp.float32))
    o = rmsnorm(o, o_norm) * jax.nn.silu(z.astype(jnp.float32).reshape(B, T, GDN_HEADS, GDN_DV))
    return o.reshape(B, T, GDN_V).astype(qkv.dtype), s_new.astype(s0.dtype), conv_new

def memory_kv(mem, g_mem, w_mem_kv, mem_k_norm):
    B, M, _ = mem.shape
    kv = jnp.einsum('bmd,df->bmf', rmsnorm(mem, g_mem), w_mem_kv).reshape(B, M, 2, MEM_HEADS, MEM_HD)
    return jnp.stack([rmsnorm(kv[:, :, 0], mem_k_norm), kv[:, :, 1]], axis=2)

def mem_attend(q, kv):
    B, T = q.shape[0], q.shape[1]
    kv = kv.astype(q.dtype)
    s = jnp.einsum('bthd,bmhd->bhtm', q, kv[:, :, 0]) * MEM_SCALE
    p = jax.nn.softmax(s.astype(jnp.float32), axis=-1).astype(q.dtype)
    return jnp.einsum('bhtm,bmhd->bthd', p, kv[:, :, 1]).reshape(B, T, MEM_Q)

def gather_pages(pool, page_table):
    g = pool[page_table]
    return g.reshape((page_table.shape[0], -1) + pool.shape[2:])

def hybrid_layer(x, q_off, past_cmp, past_sel, win_buf, win_keep, gdn_s0, conv_buf, mem_kv, params):
    (g_mix, w_in, nsa_q_norm, nsa_k_norm, cmp_pe, cmp_w1, cmp_w2, gdn_conv_w, gdn_A_log,
     gdn_dt_bias, gdn_o_norm, mem_q_norm, w_br_nsa, w_br_gdn, w_br_mem, w_out, g_ffn, w_ff1, w_ff2) = params
    B, T, _ = x.shape
    pos = q_off + jnp.arange(T, dtype=jnp.int32)
    u = rmsnorm(x, g_mix)
    proj = jnp.einsum('btd,df->btf', u, w_in)
    (q_nsa, kv_nsa, g_nsa, qkv_gdn, b_gdn, a_gdn, z_gdn, q_mem, g_br) = jnp.split(proj, split_offsets(IN_SPLITS), axis=-1)
    q = rope(rmsnorm(q_nsa.reshape(B, T, NSA_HEADS, NSA_HD), nsa_q_norm), pos)
    kv = kv_nsa.reshape(B, T, 3, 2, NSA_KV_HEADS, NSA_HD)
    k = rope(rmsnorm(kv[:, :, :, 0], nsa_k_norm[:, None, :]), pos)
    rows = jnp.stack([k, kv[:, :, :, 1]], axis=3)
    new_cmp, new_sel, new_win = rows[:, :, 0], rows[:, :, 1], rows[:, :, 2]
    cmp_kv = jnp.concatenate([past_cmp.astype(x.dtype), new_cmp], axis=1)
    sel_kv = jnp.concatenate([past_sel.astype(x.dtype), new_sel], axis=1)
    win_kv = jnp.concatenate([win_buf.astype(x.dtype), new_win], axis=1)
    win_len = win_buf.shape[1]
    kw_pos = q_off - win_len + jnp.arange(win_len + T, dtype=jnp.int32)
    o_nsa = nsa_core(q, pos, cmp_kv, sel_kv, win_kv, kw_pos, g_nsa.reshape(B, T, NSA_HEADS, 3), cmp_pe, cmp_w1, cmp_w2)
    o_gdn, s_new, conv_new = gdn_mixer(qkv_gdn, b_gdn, a_gdn, z_gdn, conv_buf, gdn_s0, gdn_conv_w, gdn_A_log, gdn_dt_bias, gdn_o_norm)
    qm = rmsnorm(q_mem.reshape(B, T, MEM_HEADS, MEM_HD), mem_q_norm)
    o_mem = mem_attend(qm, mem_kv)
    gates = jax.nn.sigmoid(g_br.astype(jnp.float32)).astype(x.dtype).reshape(B, T, N_BRANCH, D_MODEL)
    merged = (gates[:, :, 0] * jnp.einsum('btc,cd->btd', o_nsa, w_br_nsa)
              + gates[:, :, 1] * jnp.einsum('btc,cd->btd', o_gdn, w_br_gdn)
              + gates[:, :, 2] * jnp.einsum('btc,cd->btd', o_mem, w_br_mem))
    h = x + jnp.einsum('btd,de->bte', merged, w_out)
    f = jnp.square(jax.nn.relu(jnp.einsum('btd,df->btf', rmsnorm(h, g_ffn), w_ff1)))
    y = h + jnp.einsum('btf,fd->btd', f, w_ff2)
    return y, new_cmp, new_sel, win_kv[:, -win_keep:], s_new, conv_new

def setup_inputs(seed: int = 0) -> dict:
    key = jax.random.key(seed)
    ks = jax.random.split(key, 40)
    f32 = jnp.float32

    def nrm(k, shape, scale):
        return jax.random.normal(k, shape, f32) * scale

    n_pages = PAST_LEN // PAGE_SIZE
    n_pool = (DEC_BATCH * n_pages * 5) // 4
    win_len = min(WINDOW, PAST_LEN)
    perm = jax.random.permutation(ks[0], n_pool)
    page_table = perm[:DEC_BATCH * n_pages].reshape(DEC_BATCH, n_pages).astype(jnp.int32)
    dt = jnp.exp(jax.random.uniform(ks[1], (GDN_HEADS,), f32, np.log(1e-3), np.log(1e-1)))
    return {
        'x_prompt': nrm(ks[2], (BATCH, SEQ, D_MODEL), 1.0),
        'x_sample': nrm(ks[3], (DEC_BATCH, DEC_SEQ, D_MODEL), 1.0),
        'cache_cmp_kv': nrm(ks[4], (n_pool, PAGE_SIZE, 2, NSA_KV_HEADS, NSA_HD), 1.0),
        'cache_sel_kv': nrm(ks[5], (n_pool, PAGE_SIZE, 2, NSA_KV_HEADS, NSA_HD), 1.0),
        'cache_win_kv': nrm(ks[6], (DEC_BATCH, win_len, 2, NSA_KV_HEADS, NSA_HD), 1.0),
        'state_gdn': nrm(ks[7], (DEC_BATCH, GDN_HEADS, GDN_DK, GDN_DV), 0.3),
        'state_gdn_conv': nrm(ks[8], (DEC_BATCH, CONV_W - 1, CONV_DIM), 1.0),
        'cache_mem_kv': nrm(ks[9], (DEC_BATCH, MEM_TOKENS, 2, MEM_HEADS, MEM_HD), 1.0),
        'page_table': page_table,
        'mem_prompt': nrm(ks[10], (BATCH, MEM_TOKENS, D_MODEL), 1.0),
        'g_mix': 1.0 + nrm(ks[11], (D_MODEL,), 0.1),
        'w_in': nrm(ks[12], (D_MODEL, IN_DIM), D_MODEL ** -0.5),
        'nsa_q_norm': 1.0 + nrm(ks[13], (NSA_HD,), 0.1),
        'nsa_k_norm': 1.0 + nrm(ks[14], (3, NSA_HD), 0.1),
        'cmp_pe': nrm(ks[15], (2, CMP_BLOCK, NSA_HD), 0.5),
        'cmp_w1': nrm(ks[16], (2, CMP_BLOCK * NSA_HD, CMP_HID), (CMP_BLOCK * NSA_HD) ** -0.5),
        'cmp_w2': nrm(ks[17], (2, CMP_HID, NSA_HD), CMP_HID ** -0.5),
        'gdn_conv_w': nrm(ks[18], (CONV_W, CONV_DIM), CONV_W ** -0.5),
        'gdn_A_log': jnp.log(jax.random.uniform(ks[19], (GDN_HEADS,), f32, 1.0, 16.0)),
        'gdn_dt_bias': jnp.log(jnp.expm1(dt)),
        'gdn_o_norm': 1.0 + nrm(ks[20], (GDN_DV,), 0.1),
        'g_mem': 1.0 + nrm(ks[21], (D_MODEL,), 0.1),
        'w_mem_kv': nrm(ks[22], (D_MODEL, 2 * MEM_Q), D_MODEL ** -0.5),
        'mem_q_norm': 1.0 + nrm(ks[23], (MEM_HD,), 0.1),
        'mem_k_norm': 1.0 + nrm(ks[24], (MEM_HD,), 0.1),
        'w_br_nsa': nrm(ks[25], (Q_NSA, D_MODEL), Q_NSA ** -0.5),
        'w_br_gdn': nrm(ks[26], (GDN_V, D_MODEL), GDN_V ** -0.5),
        'w_br_mem': nrm(ks[27], (MEM_Q, D_MODEL), MEM_Q ** -0.5),
        'w_out': nrm(ks[28], (D_MODEL, D_MODEL), D_MODEL ** -0.5),
        'g_ffn': 1.0 + nrm(ks[29], (D_MODEL,), 0.1),
        'w_ff1': nrm(ks[30], (D_MODEL, D_FF), D_MODEL ** -0.5),
        'w_ff2': nrm(ks[31], (D_FF, D_MODEL), D_FF ** -0.5),
    }

def reference(x_prompt, x_sample, cache_cmp_kv, cache_sel_kv, cache_win_kv, state_gdn, state_gdn_conv,
              cache_mem_kv, page_table, mem_prompt, g_mix, w_in, nsa_q_norm, nsa_k_norm, cmp_pe, cmp_w1,
              cmp_w2, gdn_conv_w, gdn_A_log, gdn_dt_bias, gdn_o_norm, g_mem, w_mem_kv, mem_q_norm,
              mem_k_norm, w_br_nsa, w_br_gdn, w_br_mem, w_out, g_ffn, w_ff1, w_ff2):
    params = (g_mix, w_in, nsa_q_norm, nsa_k_norm, cmp_pe, cmp_w1, cmp_w2, gdn_conv_w, gdn_A_log,
              gdn_dt_bias, gdn_o_norm, mem_q_norm, w_br_nsa, w_br_gdn, w_br_mem, w_out, g_ffn, w_ff1, w_ff2)
    bp, sp = x_prompt.shape[0], x_prompt.shape[1]
    dtp = x_prompt.dtype
    empty = jnp.zeros((bp, 0, 2, NSA_KV_HEADS, NSA_HD), dtp)
    p_mem_kv = memory_kv(mem_prompt, g_mem, w_mem_kv, mem_k_norm)
    y_prompt, p_cmp, p_sel, p_win, p_state, p_conv = hybrid_layer(
        x_prompt, 0, empty, empty, empty, min(WINDOW, sp),
        jnp.zeros((bp, GDN_HEADS, GDN_DK, GDN_DV), dtp), jnp.zeros((bp, CONV_W - 1, CONV_DIM), dtp),
        p_mem_kv, params)
    past_cmp = gather_pages(cache_cmp_kv, page_table)
    past_sel = gather_pages(cache_sel_kv, page_table)
    y_sample, s_cmp, s_sel, s_win, s_state, s_conv = hybrid_layer(
        x_sample, past_cmp.shape[1], past_cmp, past_sel, cache_win_kv, cache_win_kv.shape[1],
        state_gdn, state_gdn_conv, cache_mem_kv, params)
    return (y_prompt, y_sample, p_cmp, p_sel, p_win, p_state, p_conv, p_mem_kv, s_cmp, s_sel, s_win, s_state, s_conv)


_drawn_inputs = setup_inputs


def setup_inputs(seed=0):
    import zlib

    import numpy as np

    out = dict(_drawn_inputs(seed))
    spreads = {}
    factors = {'cache_sel_kv': 4.047, 'nsa_q_norm': 8.0, 'mem_q_norm': 8.0}
    for name, (base, spread) in spreads.items():
        noise = np.random.default_rng([zlib.crc32(name.encode()), seed]).standard_normal(out[name].shape)
        drawn = base * np.exp(spread * noise) if base else spread * noise
        out[name] = jnp.asarray(drawn.astype(out[name].dtype))
    for name, factor in factors.items():
        out[name] = (out[name] * factor).astype(out[name].dtype)
    return out
```

```python
from contextlib import ExitStack

import numpy as np

import concourse.bass as bass
from concourse import mybir

F32 = mybir.dt.float32
I32 = mybir.dt.int32
ALU = mybir.AluOpType
ACT = mybir.ActivationFunctionType
AX = mybir.AxisListType.X

P = 128
DM = 1024
SEQ = 512
NB = 8
NT = SEQ + NB
TT = SEQ // P
HALF = NT // 2
KC = DM // P
PAST = 2048
PAGE = 128
PAGES = PAST // PAGE
NH, NG, HD = 8, 2, 64
HPG = NH // NG
CB, CS = 32, 16
NCMP = PAST // CS - 1
PCMP = SEQ // CS - 1
NSEL = PAST // 64 + 1
WIN = 512
GH, GD = 4, 128
MT, MH, MD = 256, 4, 128
CONV = 3 * GH * GD
CC = CONV // P
DFF = 4 * DM
EPS = 1e-6
NEG = -1e30
FORCE = 1e9

C_Q, C_KV, C_GN, C_GDN, C_B, C_A, C_Z, C_QM, C_GB, C_END = (
    0, 512, 1280, 1304, 2840, 2844, 2848, 3360, 3872, 6944)
TOKCOLS = C_GDN + (C_GB - C_B)


VECS = [("nsa_q_norm", HD), ("nsa_k_norm", 3 * HD), ("mem_q_norm", MD), ("mem_k_norm", MD), ("gdn_o_norm", GD),
        ("gdn_A_log", GH), ("gdn_dt_bias", GH)]


def tok_col(c):
    return c if c < C_GDN else c - (C_B - C_GDN)


def rows(t):
    return P if t < TT else NB


def shape_constants():
    parts = {}
    r = np.arange(P)
    parts["ident"] = np.eye(P)
    parts["ones"] = np.ones((P, P))
    parts["upper"] = (r[:, None] <= r[None, :]) * 1.0
    lv = []
    for l in range(7):
        s = 1 << l
        lv.append((r[:, None] // (2 * s) == r[None, :] // (2 * s)) & (r[None, :] // s % 2 == 1) & (r[:, None] // s % 2 == 0))
    parts["levels"] = np.concatenate(lv, 1) * 1.0
    parts["causal"] = np.where(r[None, :] <= r[:, None], 0.0, NEG)
    pos = (np.arange(TT)[None, :] * P + r[:, None])
    blk_end = np.arange(32) * CS + CB - 1
    cm = (blk_end[None, None, :] <= pos[:, :, None]) & (np.arange(32) < PCMP)[None, None, :]
    parts["cmpok"] = cm.reshape(P, -1) * 1.0
    parts["cmpbias"] = np.where(cm, 0.0, NEG).reshape(P, -1)
    half = HD // 2
    inv = np.float32(10000.0) ** (-np.arange(half, dtype=np.float32) / np.float32(half))
    posr = np.concatenate([pos, np.full((P, 1), PAST)], 1).astype(np.float32)
    ang = (posr[:, :, None] * inv[None, None, :]).astype(np.float32)
    cos, sin = np.cos(ang), np.sin(ang)
    parts["cos"] = np.concatenate([cos, cos], 2).reshape(P, -1)
    parts["sin"] = np.concatenate([-sin, sin], 2).reshape(P, -1)
    h = r % 32
    same = (r[:, None] // 32 == r[None, :] // 32) & (h[:, None] // HPG == h[None, :] // HPG) & (h[:, None] < NH) & (h[None, :] < NH)
    parts["group"] = same * 1.0
    i, j = np.arange(P)[:, None], np.arange(NSEL)[None, :]
    parts["cmp2sel"] = ((i * CS < (j + 1) * 64) & (i * CS + CB > j * 64)) * 1.0
    at, off = {}, 0
    for k, v in parts.items():
        at[k] = (off, v.shape[1])
        off += v.shape[1]
    return np.concatenate([np.asarray(v, np.float32) for v in parts.values()], 1), at


class Count:

    def __init__(self, sem):
        self.sem, self.n = sem, 0

    def inc(self, ins, k=1):
        ins.then_inc(self.sem, k)
        self.n += k
        return self.n


class Chain(Count):

    def __init__(self, sem, eng):
        super().__init__(sem)
        self.eng = eng

    def step(self, ins):
        self.inc(ins)
        self.eng.wait_ge(self.sem, self.n)


class Steps:

    def __init__(self, sem, names):
        self.sem, self.names, self.n = sem, names, 0

    def done(self, ins, name, t):
        assert self.names[self.n % len(self.names)] == name and self.n // len(self.names) == t, (name, t, self.n)
        ins.then_inc(self.sem, 1)
        self.n += 1

    def wait(self, eng, name, t):
        if t >= 0:
            eng.wait_ge(self.sem, t * len(self.names) + self.names.index(name) + 1)


class Kernel:
    def __init__(self, nc, I, O, CONST):
        self.nc, self.I, self.O = nc, I, O
        self.stack = ExitStack()
        self.const_dram, self.const_at = CONST

    WORDS = 52_800

    def sb(self, name, shape):
        n, at = int(np.prod(shape[1:])), 0
        for a, b in sorted(self.taken.values()):
            if at + n <= a:
                break
            at = max(at, b)
        assert at + n <= self.WORDS and name not in self.taken, (name, at, n, self.taken)
        self.taken[name] = (at, at + n)
        ap = self.arena[0:shape[0], at:at + n]
        if len(shape) > 2:
            dims = " ".join(f"d{i}" for i in range(len(shape) - 1))
            ap = ap.rearrange(f"p ({dims}) -> p {dims}", **{f"d{i}": s for i, s in enumerate(shape[1:])})
        return ap

    def free(self, *names):
        for n in names:
            del self.taken[n]

    def sem(self, name):
        return self.stack.enter_context(self.nc.semaphore(name))

    def V(self, name):
        c = 0
        for k, n in VECS:
            if k == name:
                return self.vecs[:, c:c + n]
            c += n

    def C(self, name, a=None, b=None):
        off, n = self.const_at[name]
        a, b = a or 0, n if b is None else b
        return self.consts[:, off + a:off + b]

    def build(self):
        nc = self.nc
        with self.stack:
            self.arena = self.stack.enter_context(nc.sbuf_tensor("arena", [P, self.WORDS], F32))
            self.taken = {}
            self.ps = self.stack.enter_context(nc.psum_tensor("ps", [P, 8, 512], F32))
            self.consts = self.sb("consts", [P, sum(n for _, n in self.const_at.values())])
            self.gcol = self.sb("gcol", [P, 104])
            self.wt = [self.sb(f"wt{i}", [P, KC, 512]) for i in range(2)]
            self.w_loaded = [self.sem(f"w_loaded{i}") for i in range(2)]
            self.acc = self.sem("acc")
            self.units = 0
            self.tile_end = []
            self.tiles = 0
            self.vecs = self.sb("vecs", [P, sum(n for _, n in VECS)])
            self.vecs_loaded = self.sem("vecs_loaded")
            stages = self.stages()
            for s in stages:
                s()

    def load_tile(self, sp, src, width, chunks=KC):
        n = self.issued
        if n >= 2:
            sp.wait_ge(self.acc, self.tile_end[n - 2])
        sp.dma_start(self.wt[n % 2][:, 0:chunks, 0:width], src.rearrange("(c p) n -> p c n", p=P)).then_inc(self.w_loaded[n % 2], 16)
        self.issued += 1

    def tile_ready(self, pe):
        n = self.tiles
        pe.wait_ge(self.w_loaded[n % 2], 16 * (n // 2 + 1))
        self.tiles += 1
        return self.wt[n % 2]

    def compress_products(self, pe, XT, out, n, waits):
        for v in range(2):
            waits(v)
            for m in range(CB // 2):
                ins = pe.matmul(out(v), self.w1[:, v, m, :], XT[:, 2 * v:2 * v + 2, m:m + 8 * (n - 1) + 1:8],
                                start=(m == 0), stop=(m == CB // 2 - 1))
            ins.then_inc(self.hid_ready, 1)

    def compress_setup(self):
        self.w1 = self.sb("w1", [P, 2, CB // 2, P])
        self.w2 = self.sb("w2", [P, 2, HD])
        self.hbias = self.sb("hbias", [P, 2])

    def stage_compress(self):
        nc, I, ps = self.nc, self.I, self.ps
        self.compress_setup()
        self.issued = 0
        self.kcT = self.sb("kcT", [P, NB, NCMP + 1])
        self.vc = self.sb("vc", [P, NB, P])
        vrow = self.sb("vrow", [104, P])
        pt = self.sb("pt", [1, NB * PAGES]).bitcast(I32)
        raw = [self.sb(f"raw{i}", [P, PAGES, 2, P]) for i in range(2)]
        XT = [self.sb(f"XT{i}", [P, 4, PAST // 2]) for i in range(2)]
        HT = [self.sb(f"HT{i}", [P, 2, 2, NCMP]) for i in range(2)]
        S = self.sem
        vec_loaded, const_loaded, w1_loaded, pt_loaded = S("vec_loaded"), S("const_loaded"), S("w1_loaded"), S("pt_loaded")
        pages_in = [S("pages_in0"), S("pages_in1")]
        turned, kept = S("k_turned"), [S("k_kept0"), S("k_kept1")]
        gains_turned, gains, bias_sum, bias = S("gains_turned"), S("gains_kept"), S("bias_sum"), S("bias")
        self.hid_ready = S("hid_ready")
        gelu, cmp_ready, cmp_kept = S("gelu"), S("cmp_ready"), S("cmp_kept")
        pool = I["cache_cmp_kv"]
        NPOOL = pool.shape[0]
        TILES = PAGES // 2
        src = pool.rearrange("n r v g d -> n r v (g d)")
        with nc.Block() as block:
            @block.sync
            def _(sp):
                sp.dma_start(pt[:, :], I["page_table"].rearrange("(a b) p -> a (b p)", a=1)).then_inc(pt_loaded, 16)
                sp.dma_start(self.consts[:, :], self.const_dram).then_inc(const_loaded, 16)
                sp.wait_ge(pt_loaded, 16)
                for b in range(NB):
                    if b >= 2:
                        sp.wait_ge(turned, TILES * (b - 1))
                    with sp.Fori(0, PAGES) as p:
                        page = sp.value_load(pt[0:1, bass.ds(p + b * PAGES, 1)], min_val=0, max_val=NPOOL - 1)
                        sp.dma_start(raw[b % 2][:, bass.ds(p, 1)], src[bass.ds(page, 1)]).then_inc(pages_in[b % 2], 16)
                self.load_tile(sp, I["w_mem_kv"][:, 0:512], 512)
                self.load_tile(sp, I["w_mem_kv"][:, 512:1024], 512)


            @block.tensor
            def _(pe):
                pe.wait_ge(const_loaded, 16)
                pe.wait_ge(vec_loaded, 80)
                pe.transpose(ps[:, 7, 0:104], vrow[:, :], self.C("ident")[0:104, 0:104]).then_inc(gains_turned, 1)
                pe.wait_ge(w1_loaded, 80)
                pe.wait_ge(gains, 1)
                for v in range(2):
                    for m in range(CB // 2):
                        ins = pe.matmul(ps[:, 6, v:v + 1], self.w1[:, v, m, :], self.gcol[:, 72 + 16 * v + m:73 + 16 * v + m],
                                        start=(m == 0), stop=(m == CB // 2 - 1))
                ins.then_inc(bias_sum, 1)

                def turn(b):
                    pe.wait_ge(pages_in[b % 2], 16 * PAGES * (b // 2 + 1))
                    for q in range(TILES):
                        u = b * TILES + q
                        if u >= 4:
                            pe.wait_ge(kept[0], u - 3)
                            pe.wait_ge(kept[1], u - 3)
                        for c in range(4):
                            ins = pe.transpose(ps[:, u % 4, c * P:(c + 1) * P], raw[b % 2][:, 2 * q + c // 2, c % 2, :], self.C("ident"))
                        ins.then_inc(turned, 1)

                def hidden(b):
                    def waits(v):
                        if v == 0:
                            for k in range(2):
                                pe.wait_ge(kept[k], TILES * (b + 1))
                        if b:
                            pe.wait_ge(gelu, 2 * (b - 1) + v + 1)
                    self.compress_products(pe, XT[b % 2], lambda v: ps[:, 4 + v, 0:2 * NCMP], NCMP, waits)

                def small(b):
                    pe.wait_ge(gelu, 2 * b + 2)
                    if b:
                        pe.wait_ge(cmp_kept, 2 * b)
                    for g in range(NG):
                        pe.matmul(ps[g * HD:(g + 1) * HD, 6, 0:NCMP], self.w2[:, 0, :], HT[b % 2][:, 0, g, :], start=True, stop=True)
                    for g in range(NG):
                        ins = pe.matmul(ps[0:NCMP, 7, g * HD:(g + 1) * HD], HT[b % 2][:, 1, g, :], self.w2[:, 1, :], start=True, stop=True)
                    ins.then_inc(cmp_ready, 1)

                turn(0)
                pe.wait_ge(bias, 1)
                for b in range(NB):
                    if b + 1 < NB:
                        turn(b + 1)
                    hidden(b)
                    if b:
                        small(b - 1)
                small(NB - 1)

            def copy_unit(eng, copy, b, q, g):
                eng.wait_ge(turned, b * TILES + q + 1)
                if b >= 2:
                    eng.wait_ge(self.hid_ready, 2 * (b - 1))
                bank = ps[g * HD:(g + 1) * HD, (b * TILES + q) % 4, :].rearrange("p (c v t e) -> p c v t e", c=2, v=2, e=2)
                for e in range(2):
                    dst = XT[b % 2].rearrange("p (v g) t -> p v g t", v=2)[e * HD:(e + 1) * HD, :, g, q * P:(q + 1) * P]
                    ins = copy(dst.rearrange("p v (c t) -> p c v t", c=2), bank[:, :, :, :, e])
                ins.then_inc(kept[g], 1)

            @block.scalar
            def _(act):
                r = 0
                for name, pat, n in (("g_mix", "(c p) -> c p", 8), ("g_mem", "(c p) -> c p", 8), ("g_ffn", "(c p) -> c p", 8),
                                     ("gdn_conv_w", "j (c p) -> (j c) p", 48), ("cmp_pe", "v (m e) d -> (v m) (e d)", 32)):
                    kw = {"e": 2} if name == "cmp_pe" else {"p": P}
                    act.dma_start(vrow[r:r + n, :], I[name].rearrange(pat, **kw)).then_inc(vec_loaded, 16)
                    r += n
                for v in range(2):
                    for h in range(2):
                        act.dma_start(self.w1[:, v, 8 * h:8 * h + 8, :], I["cmp_w1"].rearrange("v (m p) f -> v p m f", p=P)[v, :, 8 * h:8 * h + 8]).then_inc(w1_loaded, 16)
                act.dma_start(self.w2[:, :, :], I["cmp_w2"].rearrange("v f d -> f v d")).then_inc(w1_loaded, 16)
                c = 0
                for name, n in VECS:
                    v = I[name]
                    v = v.rearrange("a b -> (a b)") if len(v.shape) > 1 else v
                    act.dma_start(self.vecs[:, c:c + n], v.partition_broadcast(P)).then_inc(self.vecs_loaded, 16)
                    c += n
                for b in range(NB + 1):
                    if b < NB:
                        for q in range(TILES):
                            copy_unit(act, act.copy, b, q, 1)
                    if b == 0:
                        act.wait_ge(bias, 1)
                    if b:
                        for v in range(2):
                            act.wait_ge(self.hid_ready, 2 * (b - 1) + v + 1)
                            if b > 2 and v == 0:
                                act.wait_ge(cmp_ready, b - 2)
                            act.activation(HT[(b - 1) % 2][:, v, :, :], ps[:, 4 + v, 0:2 * NCMP].rearrange("p (g n) -> p g n", g=2),
                                           ACT.Gelu_apprx_tanh, bias=self.hbias[:, v:v + 1]).then_inc(gelu, 1)

            @block.vector
            def _(dve):
                dve.wait_ge(gains_turned, 1)
                dve.tensor_copy(self.gcol[:, :], ps[:, 7, 0:104]).then_inc(gains, 1)
                dve.wait_ge(bias_sum, 1)
                dve.tensor_copy(self.hbias[:, :], ps[:, 6, 0:2]).then_inc(bias, 1)
                for b in range(NB + 2):
                    if b < NB:
                        for q in range(TILES):
                            copy_unit(dve, dve.tensor_copy, b, q, 0)
                    if b >= 2:
                        dve.wait_ge(cmp_ready, b - 1)
                        dve.tensor_copy(self.kcT[:, b - 2, 0:NCMP], ps[:, 6, 0:NCMP]).then_inc(cmp_kept, 1)
                        dve.tensor_copy(self.vc[0:NCMP, b - 2, :], ps[0:NCMP, 7, 0:P]).then_inc(cmp_kept, 1)
        self.free("vrow", "pt", "raw0", "raw1", "XT0", "XT1", "HT0", "HT1", "w1", "w2", "hbias")

    def stage_norms(self):
        nc, I, ps = self.nc, self.I, self.ps
        self.uT = self.sb("uT", [P, KC, NT])
        self.memT = self.sb("memT", [P, KC, MT])
        mem_tok = self.sb("mem_tok", [P, 2, DM])
        x_tok = self.sb("x_tok", [P, TT + 1, DM])
        x_loaded = [self.sem(f"x_loaded{i}") for i in range(3)]
        self.norm_stage_setup("a")
        srcs = [(x_tok[0:rows(t), t, :], rows(t), self.uT[:, :, t * P:t * P + rows(t)], 0) for t in range(TT + 1)]
        srcs += [(mem_tok[:, t, :], P, self.memT[:, :, t * P:(t + 1) * P], 8) for t in range(2)]
        with nc.Block() as block:
            @block.sync
            def _(sp):
                sp.dma_start(x_tok[:, 0:TT, :], I["x_prompt"][0].rearrange("(t p) d -> p t d", p=P)).then_inc(x_loaded[0], 16)
                sp.dma_start(x_tok[0:NB, TT, :], I["x_sample"][:, 0, :]).then_inc(x_loaded[1], 16)
                sp.dma_start(mem_tok[:, :, :], I["mem_prompt"][0].rearrange("(t p) d -> p t d", p=P)).then_inc(x_loaded[2], 16)

            @block.scalar
            def _(act):
                self.norm_act(act, srcs, {0: (x_loaded[0], 16), 4: (x_loaded[1], 16), 5: (x_loaded[2], 16)})

            @block.tensor
            def _(pe):
                self.norm_pe(pe, srcs)

            @block.vector
            def _(dve):
                self.norm_dve(dve, srcs)
        self.free("ss", "xn0", "xn1", "nj", "x_tok", "mem_tok")

    def norm_stage_setup(self, tag):
        n = dict(ss=self.sb("ss", [P, 8]), xn=[self.sb(f"xn{i}", [P, DM]) for i in range(2)],
                 junk=self.sb("nj", [P, DM]),
                 squares=self.sem("squares" + tag), mean=self.sem("mean" + tag), root=self.sem("root" + tag),
                 rstd=self.sem("rstd" + tag), scaled=self.sem("scaled" + tag), turned=self.sem("turned" + tag), kept=self.sem("kept" + tag))
        self.n = n
        return n

    def norm_act(self, act, srcs, waits):
        n = self.n
        for i, (src, R, _, _) in enumerate(srcs):
            if i in waits:
                act.wait_ge(*waits[i])
            if i:
                act.wait_ge(n["squares"], i)
            else:
                act.wait_ge(n["mean"], 1)
            act.activation(n["junk"][0:R, :], src, ACT.Square, accum_out=n["ss"][0:R, i:i + 1]).then_inc(n["squares"], 1)
        act.wait_ge(n["mean"], 2)
        act.activation(n["ss"][:, :], n["ss"][:, :], ACT.Sqrt).then_inc(n["root"], 1)

    def norm_dve(self, dve, srcs):
        n, ps = self.n, self.ps
        dve.memset(n["ss"][:, :], 1.0).then_inc(n["mean"], 1)
        dve.wait_ge(n["squares"], len(srcs))
        dve.tensor_scalar(n["ss"][:, :], n["ss"][:, :], 1.0 / DM, EPS, ALU.mult, ALU.add).then_inc(n["mean"], 1)
        dve.wait_ge(n["root"], 1)
        dve.reciprocal(n["ss"][:, :], n["ss"][:, :]).then_inc(n["rstd"], 1)
        dve.wait_ge(n["rstd"], 1)
        for i in range(len(srcs) + 1):
            if i < len(srcs):
                src, R, _, _ = srcs[i]
                if i >= 2:
                    dve.wait_ge(n["turned"], 2 * (i - 1))
                dve.tensor_scalar(n["xn"][i % 2][0:R, :], src, n["ss"][0:R, i:i + 1], None, ALU.mult).then_inc(n["scaled"], 1)
            if i:
                _, R, dst, g = srcs[i - 1]
                for h in range(2):
                    dve.wait_ge(n["turned"], 2 * (i - 1) + h + 1)
                    b = (2 * (i - 1) + h) % 4
                    dve.tensor_tensor(dst[:, 4 * h:4 * h + 4, :], ps[:, b, :].rearrange("p (c t) -> p c t", c=4)[:, :, 0:R],
                                      self.gcol[:, g + 4 * h:g + 4 * h + 4].unsqueeze(2).broadcast_to([P, 4, R]), ALU.mult).then_inc(n["kept"], 1)

    def norm_pe(self, pe, srcs):
        n, ps = self.n, self.ps
        for i, (_, R, _, _) in enumerate(srcs):
            pe.wait_ge(n["scaled"], i + 1)
            for h in range(2):
                u = 2 * i + h
                if u >= 4:
                    pe.wait_ge(n["kept"], u - 3)
                for c in range(4):
                    ins = pe.transpose(ps[:, u % 4, c * P:c * P + R], n["xn"][i % 2][0:R, (4 * h + c) * P:(4 * h + c + 1) * P],
                                       self.C("ident")[0:R, 0:R])
                ins.then_inc(n["turned"], 1)

    def dense(self, tag, tiles, units, loads):
        nc, ps = self.nc, self.ps
        acc, u0, kept = self.acc, self.units, [self.sem(tag + "_kept0"), self.sem(tag + "_kept1")]
        for n in range(len(tiles)):
            self.tile_end.append(u0 + 1 + max(u for u, x in enumerate(units) if x[0] == n))
        self.units += len(units)
        with nc.Block() as block:
            @block.sync
            def _(sp):
                for src, w, *chunks in loads:
                    self.load_tile(sp, src, w, *chunks)

            @block.tensor
            def _(pe):
                last = -1
                for u, (n, ops, R, N, _) in enumerate(units):
                    if n != last:
                        w = self.tile_ready(pe)
                        last = n
                    if u >= 4:
                        pe.wait_ge(kept[u % 2], (u - 4) // 2 + 1)
                    for c in range(KC):
                        a, b = ops(w, c)
                        ins = pe.matmul(ps[0:R, u % 4, 0:N], a, b, start=(c == 0), stop=(c == KC - 1))
                    ins.then_inc(acc, 1)

            def keep(eng, copy, k):
                for u, (_, _, R, N, dst) in enumerate(units):
                    if u % 2 == k:
                        eng.wait_ge(acc, u0 + u + 1)
                        copy(dst, ps[0:R, u % 4, 0:N]).then_inc(kept[k], 1)

            @block.scalar
            def _(act):
                keep(act, act.copy, 0)

            @block.vector
            def _(dve):
                keep(dve, dve.tensor_copy, 1)

    def stage_project(self):
        nc, I, ps = self.nc, self.I, self.ps
        self.mem_kv = self.sb("mem_kv", [P, 2, 2 * MH * MD])
        self.proj = self.sb("proj", [P, TT + 1, TOKCOLS])
        units = []
        tiles = []
        for n in range(2):
            tiles.append((I["w_mem_kv"][:, 512 * n:512 * n + 512], 512))
            for t in range(2):
                units.append((len(tiles) - 1, lambda w, c, t=t: (self.memT[:, c, t * P:(t + 1) * P], w[:, c, 0:512]), P, 512,
                              self.mem_kv[:, t, 512 * n:512 * n + 512]))
        for a, b in ((0, 512), (512, 896), (896, C_GDN), (C_B, 3100), (3100, C_QM), (C_QM, C_GB)):
            tiles.append((I["w_in"][:, a:b], b - a))
            for t in range(TT + 1):
                R = rows(t)
                units.append((len(tiles) - 1, lambda w, c, t=t, R=R, n=b - a: (self.uT[:, c, t * P:t * P + R], w[:, c, 0:n]), R, b - a,
                              self.proj[0:R, t, tok_col(a):tok_col(a) + b - a]))
        self.dense("proj", tiles, units, tiles[2:])
        self.free("memT")

    def stage_qk(self):
        nc, I, O, ps, proj = self.nc, self.I, self.O, self.ps, self.proj
        NK = 3 * NG
        self.qT = self.sb("qT", [P, 4, NT])
        self.kT = self.sb("kT", [P, 2 * NG, NT])
        self.qmT = self.sb("qmT", [P, MH, NT])
        self.kmT = self.sb("kmT", [P, MH, MT])
        self.qblk = self.sb("qblk", [P, NB, 32])
        self.qmpad = self.sb("qmpad", [P, NB, MH, 32])
        self.knT = self.sb("knT", [P, 2, NB])
        self.vnew = self.sb("vnew", [1, 2, NB, NG * HD])
        sq = self.sb("sq", [P, 2, (NH + NK) * HD + MH * MD])
        tmp = self.sb("ropetmp", [P, (NH + NK) * HD])
        qbd = self.sb("qbd", [NB, NH, P])
        NS = NH + NK + MH
        ss = self.sb("ssq", [P, TT + 3, NS])
        squared, summed, roots, chain = self.sem("c_squared"), self.sem("c_summed"), self.sem("c_roots"), self.sem("c_chain")
        turned, kept, stored, moved, zeroed = (self.sem("c_" + x) for x in ("turned", "kept", "stored", "moved", "zeroed"))
        kv3 = proj[:, :, C_KV:C_KV + 768].rearrange("p t (b v n) -> p t b v n", b=3, v=2)
        zm = tok_col(C_QM)
        ready = {}


        def k_in(t, R):
            return kv3[0:R, t, :, 0, :]

        with nc.Block() as block:
            @block.gpsimd
            def _(pool):
                pool.memset(self.qblk[:, :, :], 0.0).then_inc(zeroed, 1)
                pool.memset(self.qmpad[:, :, :, :], 0.0).then_inc(zeroed, 1)
                pool.memset(qbd[:, :, :], 0.0).then_inc(zeroed, 1)

            @block.vector
            def _(dve):
                ch = Chain(chain, dve)
                ch.step(dve.memset(ss[:, :, :], 1.0))
                for i in range(TT + 3):
                    dve.wait_ge(squared, 3 * (i + 1) if i <= TT else 3 * (TT + 1) + i - TT)
                    R = rows(i) if i <= TT else P
                    if i <= TT:
                        dve.tensor_reduce(ss[0:R, i, 0:NH + NK], sq[0:R, i % 2, 0:(NH + NK) * HD].rearrange("p (h d) -> p h d", d=HD), AX, ALU.add)
                    dve.tensor_reduce(ss[0:R, i, NH + NK:NS], sq[0:R, i % 2, (NH + NK) * HD:].rearrange("p (h d) -> p h d", d=MD), AX, ALU.add).then_inc(summed, 1)
                dve.wait_ge(summed, TT + 3)
                ch.step(dve.tensor_scalar(ss[:, :, 0:NH + NK], ss[:, :, 0:NH + NK], 1.0 / HD, EPS, ALU.mult, ALU.add))
                ch.step(dve.tensor_scalar(ss[:, :, NH + NK:NS], ss[:, :, NH + NK:NS], 1.0 / MD, EPS, ALU.mult, ALU.add))
                dve.wait_ge(roots, 1)
                ch.step(dve.reciprocal(ss[:, :, :], ss[:, :, :]))
                dve.wait_ge(self.vecs_loaded, 16 * len(VECS))
                ch.step(dve.tensor_scalar(self.V("nsa_q_norm"), self.V("nsa_q_norm"), float(HD) ** -0.5, None, ALU.mult))
                ch.step(dve.tensor_scalar(self.V("mem_q_norm"), self.V("mem_q_norm"), float(MD) ** -0.5, None, ALU.mult))

                def together(*ins):
                    for x in ins:
                        ch.inc(x)
                    dve.wait_ge(chain, ch.n)

                for t in range(2):
                    r = ss[:, TT + 1 + t, NH + NK:NS].unsqueeze(2).broadcast_to([P, MH, MD])
                    o = self.mem_kv[:, t, 0:MH * MD].rearrange("p (h d) -> p h d", d=MD)
                    ch.step(dve.tensor_tensor(o, o, r, ALU.mult))
                    ch.step(dve.tensor_tensor(o, o, self.V("mem_k_norm").unsqueeze(1).broadcast_to([P, MH, MD]), ALU.mult))
                    ready["mem", t] = ch.n
                for t in range(TT + 1):
                    R, H = rows(t), HD // 2
                    r = ss[0:R, t, :]
                    q = proj[0:R, t, 0:NH * HD].rearrange("p (h d) -> p h d", d=HD)
                    k = k_in(t, R).rearrange("p b (g d) -> p b g d", d=HD)
                    m = proj[0:R, t, zm:zm + MH * MD].rearrange("p (h d) -> p h d", d=MD)
                    together(dve.tensor_tensor(q, q, r[:, 0:NH].unsqueeze(2).broadcast_to([R, NH, HD]), ALU.mult),
                             dve.tensor_tensor(k, k, r[:, NH:NH + NK].rearrange("p (b g) -> p b g", b=3).unsqueeze(3).broadcast_to([R, 3, NG, HD]), ALU.mult),
                             dve.tensor_tensor(m, m, r[:, NH + NK:NS].unsqueeze(2).broadcast_to([R, MH, MD]), ALU.mult))
                    together(dve.tensor_tensor(q, q, self.V("nsa_q_norm")[0:R].unsqueeze(1).broadcast_to([R, NH, HD]), ALU.mult),
                             dve.tensor_tensor(k, k, self.V("nsa_k_norm")[0:R].rearrange("p (b d) -> p b d", b=3).unsqueeze(2).broadcast_to([R, 3, NG, HD]), ALU.mult),
                             dve.tensor_tensor(m, m, self.V("mem_q_norm")[0:R].unsqueeze(1).broadcast_to([R, MH, MD]), ALU.mult))
                    cos, sin = self.C("cos")[0:R, t * HD:(t + 1) * HD], self.C("sin")[0:R, t * HD:(t + 1) * HD]
                    yq = tmp[0:R, 0:NH * HD].rearrange("p (h d) -> p h d", d=HD)
                    yk = tmp[0:R, NH * HD:].rearrange("p (b g d) -> p b g d", b=3, g=NG)
                    bq = lambda a: a.unsqueeze(1).broadcast_to([R, NH, a.shape[1]])
                    bk = lambda a: a.unsqueeze(1).unsqueeze(1).broadcast_to([R, 3, NG, a.shape[1]])
                    together(dve.tensor_tensor(yq[:, :, 0:H], q[:, :, H:HD], bq(sin[:, 0:H]), ALU.mult),
                             dve.tensor_tensor(yq[:, :, H:HD], q[:, :, 0:H], bq(sin[:, H:HD]), ALU.mult),
                             dve.tensor_tensor(yk[:, :, :, 0:H], k[:, :, :, H:HD], bk(sin[:, 0:H]), ALU.mult),
                             dve.tensor_tensor(yk[:, :, :, H:HD], k[:, :, :, 0:H], bk(sin[:, H:HD]), ALU.mult))
                    together(dve.tensor_tensor(q, q, bq(cos), ALU.mult), dve.tensor_tensor(k, k, bk(cos), ALU.mult))
                    together(dve.tensor_tensor(q, q, yq, ALU.add), dve.tensor_tensor(k, k, yk, ALU.add))
                    ready[t] = ch.n
                dve.wait_ge(zeroed, 3)
                for g in range(NG):
                    ch.step(dve.tensor_copy(qbd[:, HPG * g:HPG * g + HPG, g * HD:(g + 1) * HD],
                                            proj[0:NB, TT, g * HPG * HD:(g + 1) * HPG * HD].rearrange("p (h d) -> p h d", d=HD)))
                ready["blk"] = ch.n

            ident, banks = self.C("ident"), []
            for t in range(2):
                banks.append(([self.mem_kv[:, t, h * P:(h + 1) * P] for h in range(4)], P, self.kmT[:, :, t * P:(t + 1) * P], ready["mem", t]))
            for t in range(TT + 1):
                R = rows(t)
                s = slice(t * P, t * P + R)
                banks.append(([proj[0:R, t, c * P:(c + 1) * P] for c in range(4)], R, self.qT[:, :, s], ready[t]))
                banks.append(([k_in(t, R)[:, 1 + i, :] for i in range(2)], R, (s, "both halves"), ready[t]))
                banks.append(([proj[0:R, t, zm + c * P:zm + (c + 1) * P] for c in range(4)], R, self.qmT[:, :, s], ready[t]))
            NBK = len(banks)

            @block.tensor
            def _(pe):
                for u, (blocks, R, _, n) in enumerate(banks):
                    pe.wait_ge(chain, n)
                    if u >= 4:
                        pe.wait_ge(kept, u - 3)
                    for c, b in enumerate(blocks):
                        ins = pe.transpose(ps[:, u % 4, c * P:c * P + R], b, ident[0:R, 0:R])
                    ins.then_inc(turned, 1)
                pe.wait_ge(chain, ready["blk"])
                for h in range(NH):
                    pe.transpose(ps[:, 4, h * NB:(h + 1) * NB], qbd[:, h, :], ident[0:NB, 0:NB])
                for i in range(2):
                    ins = pe.transpose(ps[:, 4, (NH + i) * NB:(NH + i + 1) * NB], k_in(TT, NB)[:, i + 1, :], ident[0:NB, 0:NB])
                ins.then_inc(turned, 1)

            @block.scalar
            def _(act):
                for i in range(TT + 3):
                    if i >= 2:
                        act.wait_ge(summed, i - 1)
                    elif i == 0:
                        act.wait_ge(chain, 1)
                    w = (NH + NK) * HD
                    if i <= TT:
                        R = rows(i)
                        act.activation(sq[0:R, i % 2, 0:NH * HD], proj[0:R, i, 0:NH * HD], ACT.Square).then_inc(squared, 1)
                        act.activation(sq[0:R, i % 2, NH * HD:w].rearrange("p (b n) -> p b n", b=3), k_in(i, R), ACT.Square).then_inc(squared, 1)
                        act.activation(sq[0:R, i % 2, w:], proj[0:R, i, zm:zm + MH * MD], ACT.Square).then_inc(squared, 1)
                    else:
                        act.activation(sq[:, i % 2, w:], self.mem_kv[:, i - TT - 1, 0:MH * MD], ACT.Square).then_inc(squared, 1)
                act.wait_ge(chain, 3)
                act.activation(ss[:, :, :], ss[:, :, :], ACT.Sqrt).then_inc(roots, 1)
                for u, (_, R, dst, _) in enumerate(banks):
                    act.wait_ge(turned, u + 1)
                    if type(dst) is tuple:
                        for g in range(NG):
                            for half in range(2):
                                ins = act.copy(self.kT.rearrange("p (b g) t -> p b g t", g=NG)[half * HD:half * HD + HD, :, g, dst[0]],
                                               ps[g * HD:g * HD + HD, u % 4, 0:2 * P].rearrange("p (c t) -> p c t", c=2)[:, :, 0:R])
                        ins.then_inc(kept, 1)
                        continue
                    act.copy(dst, ps[:, u % 4, :].rearrange("p (c t) -> p c t", c=4)[:, :, 0:R]).then_inc(kept, 1)
                act.wait_ge(turned, NBK + 1)
                act.wait_ge(zeroed, 3)
                act.copy(self.qblk[:, :, 0:NH].rearrange("p b h -> p h b"), ps[:, 4, 0:NH * NB].rearrange("p (h b) -> p h b", h=NH)).then_inc(kept, 1)
                act.copy(self.knT[:, :, :], ps[:, 4, NH * NB:(NH + 2) * NB].rearrange("p (h b) -> p h b", h=2)).then_inc(kept, 1)
                act.wait_ge(kept, NBK)
                act.copy(self.qmpad.rearrange("p b h c -> p b (h c)")[:, :, 0:P:33], self.qmT[:, :, SEQ:NT].rearrange("p h b -> p b h")).then_inc(kept, 1)

            @block.sync
            def _(sp):
                for i in range(2):
                    sp.dma_start(self.vnew[:, i], proj[0:NB, TT, C_KV + 256 * (i + 1) + P:C_KV + 256 * (i + 2)]).then_inc(moved, 16)
                sp.dma_start(O["s_win"][:, 0:WIN - 1], I["cache_win_kv"][:, 1:WIN]).then_inc(stored, 16)
                sp.wait_ge(chain, ready["mem", 1])
                sp.dma_start(O["p_mem"][0].rearrange("(t p) v h d -> p t (v h d)", p=P), self.mem_kv[:, :, :]).then_inc(stored, 16)
                sp.wait_ge(chain, ready[TT])
                for i, name in enumerate(("cmp", "sel", "win")):
                    c = C_KV + 256 * i
                    sp.dma_start(O["p_" + name][0].rearrange("(t p) v g d -> p t (v g d)", p=P), proj[:, 0:TT, c:c + 256]).then_inc(stored, 16)
                    sp.dma_start(O["s_" + name][:, WIN - 1 if name == "win" else 0].rearrange("b v g d -> b (v g d)"), proj[0:NB, TT, c:c + 256]).then_inc(stored, 16)
                sp.wait_ge(stored, 16 * 8)
                sp.wait_ge(moved, 32)
        self.free("sq", "ropetmp", "qbd", "ssq")

    def stage_prompt_attention(self):
        assert SEQ // 64 <= 16 and SEQ <= WIN
        nc, I, ps, proj = self.nc, self.I, self.ps, self.proj
        self.compress_setup()
        XT, HT = self.sb("XT", [P, 4, SEQ // 2]), self.sb("HT", [P, 2, 2, PCMP])
        kc = self.sb("kcp", [P, NG, 32])
        vc = self.sb("vcp", [32, P])
        self.gate = self.sb("gate", [P, TT + 1, 3 * NH])
        sc, cs = self.sb("sc", [P, NH, 32]), self.sb("cs", [P, 2, NH])
        PTc = self.sb("PTc", [32, NH, P])
        Pb, PTb = [self.sb(f"Pb{i}", [P, SEQ]) for i in range(2)], [self.sb(f"PTb{i}", [P, SEQ]) for i in range(2)]
        nm, rs, rg = self.sb("nm", [P, 2]), self.sb("rs", [P, 4]), self.sb("rg", [P, 2])
        S = self.sem
        w_loaded, turned, kept, gelu, small_ready, small_kept = (S("d_" + x) for x in ("w", "turned", "kept", "gelu", "small", "smallkept"))
        kept2, gates, zeroed = S("d_kept2"), S("d_gates"), S("d_zeroed")
        c_s, c_max, c_exp, c_p, c_t, c_tk, c_o, c_chain = (S("dc_" + x) for x in ("s", "max", "exp", "p", "t", "tk", "o", "chain"))
        s_ready, nmax, p_ready, pt_ready, pt_kept, o_ready, o_done, v_chain = (S("u_" + x) for x in (
            "scores", "max", "exp", "turned", "kept", "out", "done", "chain"))
        hid0 = 2 * NB
        ident = self.C("ident")

        units = []
        for qt in range(TT):
            q = slice(qt * P, (qt + 1) * P)
            for h in range(NH):
                g, lo = h // HPG, h % 2 * HD
                for br in range(2):
                    vcol = C_KV + 256 * (br + 1) + P + g * HD
                    units.append(dict(
                        q=self.qT[lo:lo + HD, h // 2, q], k=self.kT[lo:lo + HD, br * NG + g, 0:(qt + 1) * P], n=qt + 1, causal=True,
                        v=[proj[:, t, vcol:vcol + HD] for t in range(qt + 1)], N=HD, gate=self.gate[:, qt, 3 * h + 1 + br:3 * h + 2 + br],
                        dst=proj[:, qt, h * HD:(h + 1) * HD]))
            for h in range(MH):
                c = tok_col(C_QM) + h * MD
                units.append(dict(q=self.qmT[:, h, q], k=self.kmT[:, h, :], n=MT // P, causal=False,
                                  v=[self.mem_kv[:, t, MH * MD + h * MD:MH * MD + (h + 1) * MD] for t in range(MT // P)], N=MD, gate=None,
                                  dst=proj[:, qt, c:c + MD]))
        NU = len(units)

        with nc.Block() as block:
            @block.sync
            def _(sp):
                for v in range(2):
                    for h in range(2):
                        sp.dma_start(self.w1[:, v, 8 * h:8 * h + 8, :], I["cmp_w1"].rearrange("v (m p) f -> v p m f", p=P)[v, :, 8 * h:8 * h + 8]).then_inc(w_loaded, 16)
                sp.dma_start(self.w2[:, :, :], I["cmp_w2"].rearrange("v f d -> f v d")).then_inc(w_loaded, 16)

            @block.gpsimd
            def _(pool):
                pool.memset(kc[:, :, :], 0.0).then_inc(zeroed, 1)
                pool.memset(vc[:, :], 0.0).then_inc(zeroed, 1)

            @block.tensor
            def _(pe):
                for q in range(2):
                    for c in range(4):
                        a = C_KV + c % 2 * P
                        ins = pe.transpose(ps[:, q, c * P:(c + 1) * P], proj[:, 2 * q + c // 2, a:a + P], ident)
                    ins.then_inc(turned, 1)
                pe.wait_ge(w_loaded, 80)
                for v in range(2):
                    for m in range(CB // 2):
                        ins = pe.matmul(ps[:, 2, v:v + 1], self.w1[:, v, m, :], self.gcol[:, 72 + 16 * v + m:73 + 16 * v + m],
                                        start=(m == 0), stop=(m == CB // 2 - 1))
                ins.then_inc(turned, 1)
                pe.wait_ge(kept, 4)
                self.compress_products(pe, XT, lambda v: ps[:, 4 + v, 0:2 * PCMP], PCMP, lambda v: None)
                pe.wait_ge(gelu, 2)
                for g in range(NG):
                    for half in range(2):
                        pe.matmul(ps[half * HD:half * HD + HD, 3, g * 32:g * 32 + PCMP], self.w2[:, 0, :], HT[:, 0, g, :], start=True, stop=True)
                for g in range(NG):
                    ins = pe.matmul(ps[0:PCMP, 2, g * HD:(g + 1) * HD], HT[:, 1, g, :], self.w2[:, 1, :], start=True, stop=True)
                ins.then_inc(small_ready, 1)
                pe.wait_ge(small_kept, 2)
                for qt in range(TT):
                    if qt:
                        pe.wait_ge(c_p, qt)
                    for h in range(NH):
                        lo = h % 2 * HD
                        ins = pe.matmul(ps[:, 5 + h % 2, h // 2 * 32:(h // 2 + 1) * 32], self.qT[lo:lo + HD, h // 2, qt * P:(qt + 1) * P],
                                        kc[lo:lo + HD, h // HPG, :], start=True, stop=True)
                    ins.then_inc(c_s, 1)
                    pe.wait_ge(c_p, qt + 1)
                    for h in range(NH):
                        if h == 0 and qt:
                            pe.wait_ge(c_tk, 2 * qt)
                        ins = pe.transpose(ps[0:32, h // HPG, h % HPG * P:(h % HPG + 1) * P], sc[:, h % 2 * HPG + h // 2, :], ident)
                        if h % HPG == HPG - 1:
                            ins.then_inc(c_t, 1)
                    pe.wait_ge(c_tk, 2 * qt + 2)
                    if qt:
                        pe.wait_ge(o_done, qt)
                    for h in range(NH):
                        g = h // HPG
                        ins = pe.matmul(ps[:, 7, h * HD:(h + 1) * HD], PTc[:, h, :], vc[:, g * HD:(g + 1) * HD], start=True, stop=True)
                    ins.then_inc(c_o, 1)
                pe.wait_ge(o_done, TT)

                def scores(u):
                    x = units[u]
                    if u >= 2:
                        pe.wait_ge(p_ready, u - 1)
                    pe.matmul(ps[:, u % 2, 0:x["n"] * P], x["q"], x["k"], start=True, stop=True).then_inc(s_ready, 1)

                def turn(u):
                    x = units[u]
                    pe.wait_ge(p_ready, u + 1)
                    if u >= 2:
                        pe.wait_ge(pt_kept, u - 1)
                    for c in range(x["n"]):
                        ins = pe.transpose(ps[:, 2 + u % 2, c * P:(c + 1) * P], Pb[u % 2][:, c * P:(c + 1) * P], ident)
                    ins.then_inc(pt_ready, 1)

                def values(u):
                    x = units[u]
                    pe.wait_ge(pt_kept, u + 1)
                    if u >= 2:
                        pe.wait_ge(o_done, TT + u - 1)
                    for c in range(x["n"]):
                        ins = pe.matmul(ps[:, 4 + u % 2, 0:x["N"]], PTb[u % 2][:, c * P:(c + 1) * P], x["v"][c], start=(c == 0), stop=(c == x["n"] - 1))
                    ins.then_inc(o_ready, 1)

                scores(0)
                for u in range(NU + 1):
                    if u + 1 < NU:
                        scores(u + 1)
                    if u < NU:
                        turn(u)
                    if u:
                        values(u - 1)

            @block.scalar
            def _(act):
                for t in range(TT + 1):
                    act.activation(self.gate[0:rows(t), t, :], proj[0:rows(t), t, C_GN:C_GN + 24], ACT.Sigmoid).then_inc(gates, 1)
                act.wait_ge(kept2, 1)
                for v in range(2):
                    act.wait_ge(self.hid_ready, hid0 + v + 1)
                    act.activation(HT[:, v, :, :], ps[:, 4 + v, 0:2 * PCMP].rearrange("p (g n) -> p g n", g=2),
                                   ACT.Gelu_apprx_tanh, bias=self.hbias[:, v:v + 1]).then_inc(gelu, 1)
                for qt in range(TT):
                    act.wait_ge(c_max, qt + 1)
                    act.activation(sc[:, :, :], sc[:, :, :], ACT.Exp).then_inc(c_exp, 1)
                    for i in range(2):
                        act.wait_ge(c_t, 2 * qt + i + 1)
                        if qt:
                            act.wait_ge(c_o, qt)
                        act.copy(PTc[:, HPG * i:HPG * i + HPG, :], ps[0:32, i, :].rearrange("p (h t) -> p h t", h=HPG)).then_inc(c_tk, 1)

                def exp(u):
                    x = units[u]
                    L = x["n"] * P
                    act.wait_ge(nmax, u + 1)
                    if u >= 2:
                        act.wait_ge(pt_ready, u - 1)
                    if u >= 4:
                        act.wait_ge(o_done, TT + u - 3)
                    act.activation(Pb[u % 2][:, 0:L], ps[:, u % 2, 0:L], ACT.Exp, bias=nm[:, u % 2:u % 2 + 1],
                                   accum_out=rs[:, u % 4:u % 4 + 1]).then_inc(p_ready, 1)

                def keep(u):
                    L = units[u]["n"] * P
                    act.wait_ge(pt_ready, u + 1)
                    if u >= 2:
                        act.wait_ge(o_ready, u - 1)
                    act.copy(PTb[u % 2][:, 0:L], ps[:, 2 + u % 2, 0:L]).then_inc(pt_kept, 1)

                for u in range(NU + 1):
                    if u < NU:
                        exp(u)
                    if u:
                        keep(u - 1)

            @block.vector
            def _(dve):
                for q in range(2):
                    dve.wait_ge(turned, q + 1)
                    for g in range(NG):
                        bank = ps[g * HD:(g + 1) * HD, q, :].rearrange("p (c v t e) -> p c v t e", c=2, v=2, e=2)
                        for e in range(2):
                            dst = XT.rearrange("p (v g) t -> p v g t", v=2)[e * HD:(e + 1) * HD, :, g, q * P:(q + 1) * P]
                            ins = dve.tensor_copy(dst.rearrange("p v (c t) -> p c v t", c=2), bank[:, :, :, :, e])
                        ins.then_inc(kept, 1)
                dve.wait_ge(turned, 3)
                dve.tensor_copy(self.hbias[:, :], ps[:, 2, 0:2]).then_inc(kept2, 1)
                dve.wait_ge(small_ready, 1)
                dve.wait_ge(zeroed, 2)
                dve.tensor_copy(kc[:, :, 0:PCMP], ps[:, 3, 0:64].rearrange("p (g n) -> p g n", g=2)[:, :, 0:PCMP]).then_inc(small_kept, 1)
                dve.tensor_copy(vc[0:PCMP, :], ps[0:PCMP, 2, 0:P]).then_inc(small_kept, 1)
                dve.wait_ge(gates, TT + 1)
                ch = Chain(c_chain, dve)
                over = lambda a: a.unsqueeze(1).broadcast_to([P, NH, 32])
                each = lambda a: a.unsqueeze(2).broadcast_to([P, NH, 32])
                for qt in range(TT):
                    dve.wait_ge(c_s, qt + 1)
                    ch.step(dve.tensor_tensor(sc.rearrange("p (e h) n -> p e h n", e=2), ps[:, 5:7, 0:HPG * 32].rearrange("p e (h n) -> p e h n", h=HPG),
                                              self.C("cmpbias", 32 * qt, 32 * qt + 32).unsqueeze(1).unsqueeze(1).broadcast_to([P, 2, HPG, 32]), ALU.add))
                    ch.step(dve.tensor_reduce(cs[:, 0, :], sc[:, :, :], AX, ALU.max))
                    dve.tensor_tensor(sc[:, :, :], sc[:, :, :], each(cs[:, 0, :]), ALU.subtract).then_inc(c_max, 1)
                    dve.wait_ge(c_exp, qt + 1)
                    ch.step(dve.tensor_reduce(cs[:, 1, :], sc[:, :, :], AX, ALU.add))
                    ch.step(dve.reciprocal(cs[:, 1, :], cs[:, 1, :]))
                    ch.step(dve.tensor_tensor(sc[:, :, :], sc[:, :, :], each(cs[:, 1, :]), ALU.mult))
                    dve.tensor_tensor(sc[:, :, :], sc[:, :, :], over(self.C("cmpok", 32 * qt, 32 * qt + 32)), ALU.mult).then_inc(c_p, 1)
                    dve.wait_ge(c_o, qt + 1)
                    g0 = self.gate[:, qt, 0:3 * NH:3].unsqueeze(2).broadcast_to([P, NH, HD])
                    dve.tensor_tensor(proj[:, qt, 0:NH * HD].rearrange("p (h d) -> p h d", d=HD), ps[:, 7, :].rearrange("p (h d) -> p h d", d=HD), g0, ALU.mult).then_inc(o_done, 1)
                dve.wait_ge(o_done, TT)
                vch = Chain(v_chain, dve)

                def biggest(u):
                    x = units[u]
                    L = x["n"] * P
                    dve.wait_ge(s_ready, u + 1)
                    if x["causal"]:
                        vch.step(dve.tensor_tensor(ps[:, u % 2, L - P:L], ps[:, u % 2, L - P:L], self.C("causal"), ALU.add))
                    dve.tensor_reduce(nm[:, u % 2:u % 2 + 1], ps[:, u % 2, 0:L], AX, ALU.max, negate=True).then_inc(nmax, 1)

                def finish(u):
                    x = units[u]
                    out, r = ps[:, 4 + u % 2, 0:x["N"]], rg[:, u % 2:u % 2 + 1]
                    dve.wait_ge(o_ready, u + 1)
                    vch.step(dve.reciprocal(r, rs[:, u % 4:u % 4 + 1]))
                    if x["gate"] is None:
                        dve.tensor_scalar(x["dst"], out, r, None, ALU.mult).then_inc(o_done, 1)
                    else:
                        vch.step(dve.tensor_tensor(r, r, x["gate"], ALU.mult))
                        dve.wait_ge(o_done, TT + u)
                        dve.scalar_tensor_tensor(x["dst"], out, r, x["dst"], ALU.mult, ALU.add).then_inc(o_done, 1)

                for u in range(NU + 2):
                    if u < NU:
                        biggest(u)
                    if u >= 2:
                        finish(u - 2)
        self.free("w1", "w2", "hbias", "XT", "HT", "kcp", "vcp", "sc", "cs", "PTc", "Pb0", "Pb1", "PTb0", "PTb1", "nm", "rs", "rg",
                  "qT", "kT", "qmT", "kmT", "mem_kv")

    def stage_sample_attention(self):
        nc, I, O, ps, proj = self.nc, self.I, self.O, self.ps, self.proj
        ident = self.C("ident")
        R4 = NB // 4
        pt = self.sb("pt", [1, NB * PAGES]).bitcast(I32)
        slots = [w.rearrange("p a b -> p (a b)") for w in self.wt] + [self.sb(f"slot{i}", [P, PAGES * 256]) for i in range(2)]
        KT = [self.sb(f"KT{i}", [P, PAST]) for i in range(2)]
        PT = self.sb("PT", [P, PAGES, P])
        PTn = self.sb("PTn", [1, P])
        Ss = self.sb("Ss", [P, PAST + 1])
        pc, PTc = self.sb("pc", [P, NCMP]), self.sb("PTc", [P, P])
        imp = self.sb("imp", [P, 4, NSEL])
        bias = self.sb("bias", [P, R4, NSEL])
        top = self.sb("top", [P, 2, 8])
        st = self.sb("st", [P, 4])
        osb = [self.sb(f"osb{i}", [P, 512]) for i in range(2)]
        obr = KT[0][0:NB, 0:3 * NH * HD].rearrange("b (i c) -> b i c", i=3)
        scr = {n: nc.dram_tensor("scratch_" + n, (NB, 32, w), F32, kind="Internal").ap()
               for n, w in (("cmp", P), ("sel", P), ("win", P), ("mem", 512))}

        jobs = [(br, r) for r in range(R4) for br in ("sel", "win", "mem")]
        NTL = {"sel": PAGES, "win": WIN // P, "mem": MT // P}
        KU = {"sel": 4, "win": 1, "mem": 2}
        PU = {"sel": 5, "win": 2, "mem": 1}
        base = [0]
        for br, _ in jobs:
            base.append(base[-1] + 4 * KU[br] + PU[br])
        loads = []
        at = [0] * 4
        for br, _ in jobs:
            at = [a + 16 * (PAGES if br == "sel" else 1) for a in at]
            loads.append(list(at))

        S = self.sem
        pt_loaded, filled, slot_free = S("e_pt"), [S(f"e_slot{j}") for j in range(4)], S("e_slot_free")
        e_s, e_max, e_exp, e_pt, e_ptk, e_imp, e_o, chain = (S("e1_" + x) for x in ("s", "max", "exp", "pt", "ptk", "imp", "o", "chain"))
        turned, kept, s_done, s_read, nmax, p_ready, o_ready, o_read = (S("e_turned"), [S("e_kept0"), S("e_kept1")], S("e_scores"), S("e_sread"),
                                                                        S("e_max"), S("e_exp"), S("e_out"), S("e_oread"))
        imp_kept, o_scr, back, merged, j_chain = S("e_impk"), [S("e_scr0"), S("e_scr1")], S("e_back"), S("e_merged"), S("e_jchain")
        pool_kv = I["cache_sel_kv"].rearrange("n r v g d -> n r (v g d)")
        NPOOL = pool_kv.shape[0]

        def kv(br, j):
            n = NTL[br]
            w = 2 * MH * MD if br == "mem" else 2 * P
            return slots[j][:, 0:n * w].rearrange("p (t c) -> p t c", t=n)

        def load(eng, n, j):
            br, r = jobs[n]
            b = 4 * r + j
            if n:
                eng.wait_ge(slot_free, 4 * (n - 1) + j + 1)
            if br == "sel":
                with eng.Fori(0, PAGES) as p:
                    page = eng.value_load(pt[0:1, bass.ds(p + b * PAGES, 1)], min_val=0, max_val=NPOOL - 1)
                    eng.dma_start(kv(br, j)[:, bass.ds(p, 1)], pool_kv[bass.ds(page, 1)].rearrange("a r c -> r a c")).then_inc(filled[j], 16)
            else:
                src = I["cache_win_kv" if br == "win" else "cache_mem_kv"][b].rearrange("(t p) v g d -> p t (v g d)", p=P)
                eng.dma_start(kv(br, j)[:, :, :], src).then_inc(filled[j], 16)

        with nc.Block() as block:
            @block.sync
            def _(sp):
                sp.dma_start(pt[:, :], I["page_table"].rearrange("(a b) p -> a (b p)", a=1)).then_inc(pt_loaded, 16)
                sp.wait_ge(pt_loaded, 16)
                for n in range(len(jobs)):
                    for j in (0, 2):
                        load(sp, n, j)
                for k in range(2):
                    sp.wait_ge(o_scr[k], 16 * (R4 + len(jobs)) // 2)
                for i, br in enumerate(("cmp", "sel", "win")):
                    for g in range(NG):
                        sp.dma_start(obr[:, i, g * HPG * HD:(g + 1) * HPG * HD].rearrange("b (h d) -> b h d", d=HD),
                                     scr[br][:, g * HPG:(g + 1) * HPG, g * HD:(g + 1) * HD]).then_inc(back, 16)
                for h in range(MH):
                    c = tok_col(C_QM) + h * MD
                    sp.dma_start(proj[0:NB, TT, c:c + MD], scr["mem"][:, h, h * MD:(h + 1) * MD]).then_inc(back, 16)
                for n in range(2):
                    self.load_tile(sp, I["w_in"][:, C_GDN + 512 * n:C_GDN + 512 * n + 512], 512)

            @block.gpsimd
            def _(pool):
                pool.wait_ge(pt_loaded, 16)
                for n in range(len(jobs)):
                    for j in (1, 3):
                        load(pool, n, j)

            @block.tensor
            def _(pe):
                for r in range(R4):
                    if r:
                        pe.wait_ge(e_exp, r)
                    for j in range(4):
                        ins = pe.matmul(ps[32 * j:32 * j + 32, 0, 0:NCMP], self.qblk[:, 4 * r + j, :], self.kcT[:, 4 * r + j, 0:NCMP], start=True, stop=True)
                    ins.then_inc(e_s, 1)
                    pe.wait_ge(chain, 3 * r + 2)
                    pe.transpose(ps[0:NCMP, 1, 0:P], pc[:, :], ident).then_inc(e_pt, 1)
                    pe.wait_ge(e_ptk, r + 1)
                    pe.matmul(ps[:, 2, 0:NSEL], PTc[0:NCMP, :], self.C("cmp2sel")[0:NCMP, :], start=True, stop=True).then_inc(e_imp, 1)
                    for j in range(4):
                        ins = pe.matmul(ps[32 * j:32 * j + 32, 3, 0:P], PTc[0:NCMP, 32 * j:32 * j + 32], self.vc[0:NCMP, 4 * r + j, :], start=True, stop=True)
                    ins.then_inc(e_o, 1)
                    pe.wait_ge(imp_kept, r + 1)
                    pe.matmul(ps[:, 4, 0:NSEL], self.C("group"), imp[:, 0, :], start=True, stop=True).then_inc(e_imp, 1)
                    pe.wait_ge(chain, 3 * r + 3)

                def bank(u):
                    if u >= 2:
                        pe.wait_ge(kept[u % 2], u // 2)
                    return ps[:, 5 + u % 2]

                for n, (br, r) in enumerate(jobs):
                    T = NTL[br]
                    u = base[n]
                    for j in range(4):
                        b = 4 * r + j
                        pe.wait_ge(filled[j], loads[n][j])
                        K = kv(br, j)
                        for i in range(KU[br]):
                            o = bank(u)
                            for c in range(4):
                                blk = K[:, i, c * MD:(c + 1) * MD] if br == "mem" else K[:, 4 * i + c, 0:P]
                                ins = pe.transpose(o[:, c * P:(c + 1) * P], blk, ident)
                            ins.then_inc(turned, 1)
                            u += 1
                        pe.wait_ge(kept[0], (u + 1) // 2)
                        pe.wait_ge(kept[1], u // 2)
                        if j == 0 and n:
                            pe.wait_ge(s_read, n)
                        row = slice(32 * j, 32 * j + 32)
                        if br == "mem":
                            for h in range(MH):
                                ins = pe.matmul(ps[row, 0, 0:MT], self.qmpad[:, b, h, :], KT[j % 2][:, h * MT:(h + 1) * MT], start=(h == 0), stop=(h == MH - 1))
                        else:
                            for i in range(T // 4):
                                pe.matmul(ps[row, i, :], self.qblk[:, b, :], KT[j % 2][:, i * 512:(i + 1) * 512], start=True, stop=True)
                            ins = pe.matmul(ps[row, 4, 0:1], self.qblk[:, b, :], self.knT[:, 0 if br == "sel" else 1, b:b + 1], start=True, stop=True)
                        ins.then_inc(s_done, 1)
                    pe.wait_ge(p_ready, n + 1)
                    for i in range(-(-T // 4)):
                        o = bank(u)
                        for c in range(min(4, T)):
                            ins = pe.transpose(o[:, c * P:(c + 1) * P], Ss[:, (4 * i + c) * P:(4 * i + c + 1) * P], ident)
                        ins.then_inc(turned, 1)
                        u += 1
                    if br != "mem":
                        pe.transpose(bank(u)[0:1, 0:P], Ss[:, T * P:T * P + 1], ident).then_inc(turned, 1)
                        u += 1
                    pe.wait_ge(kept[0], (u + 1) // 2)
                    pe.wait_ge(kept[1], u // 2)
                    if n:
                        pe.wait_ge(o_read, n)
                    for j in range(4):
                        row, V = slice(32 * j, 32 * j + 32), kv(br, j)
                        for t in range(T):
                            v = V[:, t, MH * MD:] if br == "mem" else V[:, t, P:2 * P]
                            ins = pe.matmul(ps[row, 7, 0:v.shape[1]], PT[:, t, row], v, start=(t == 0), stop=(br == "mem" and t == T - 1))
                        if br != "mem":
                            ins = pe.matmul(ps[row, 7, 0:P], PTn[:, row], self.vnew[:, 0 if br == "sel" else 1, 4 * r + j, :], start=False, stop=True)
                        ins.then_inc(slot_free, 1)

            def keep_keys(eng, copy, k, n):
                br, r = jobs[n]
                u = base[n]
                for j in range(4):
                    for i in range(KU[br]):
                        if u % 2 == k:
                            eng.wait_ge(turned, u + 1)
                            if 4 * n + j >= 2:
                                eng.wait_ge(s_done, 4 * n + j - 1)
                            src = ps[:, 5 + u % 2, :]
                            if br == "mem":
                                dst = KT[j % 2][:, 0:MH * MT].rearrange("p (h t) -> p h t", h=MH)[:, :, i * P:(i + 1) * P]
                                src = src.rearrange("p (h t) -> p h t", h=MH)
                            else:
                                dst = KT[j % 2][:, i * 512:(i + 1) * 512]
                            copy(dst, src).then_inc(kept[k], 1)
                        u += 1

            def keep_probs(eng, copy, k, n):
                br, r = jobs[n]
                T = NTL[br]
                u = base[n] + 4 * KU[br]
                if n:
                    eng.wait_ge(slot_free, 4 * n)
                for i in range(PU[br]):
                    if u % 2 == k:
                        eng.wait_ge(turned, u + 1)
                        if i < -(-T // 4):
                            w = min(4, T)
                            copy(PT[:, 4 * i:4 * i + w, :], ps[:, 5 + u % 2, 0:w * P].rearrange("p (t q) -> p t q", t=w)).then_inc(kept[k], 1)
                        else:
                            copy(PTn[:, :], ps[0:1, 5 + u % 2, 0:P]).then_inc(kept[k], 1)
                    u += 1

            def width(n):
                br, _ = jobs[n]
                return NTL[br] * P + (br != "mem")

            @block.scalar
            def _(act):
                for r in range(R4):
                    act.wait_ge(e_max, r + 1)
                    act.activation(pc[:, :], ps[:, 0, 0:NCMP], ACT.Exp, bias=st[:, 0:1], accum_out=st[:, 1:2]).then_inc(e_exp, 1)
                    act.wait_ge(e_pt, r + 1)
                    act.copy(PTc[0:NCMP, :], ps[0:NCMP, 1, 0:P]).then_inc(e_ptk, 1)
                    act.wait_ge(chain, 3 * r + 3)
                    act.dma_start(scr["cmp"].rearrange("b h c -> (b h) c")[P * r:P * r + P], osb[r % 2][:, 0:P]).then_inc(o_scr[r % 2], 16)
                for n, (br, r) in enumerate(jobs):
                    keep_keys(act, act.copy, 1, n)
                    act.wait_ge(nmax, n + 1)
                    act.activation(Ss[:, 0:width(n)], Ss[:, 0:width(n)], ACT.Exp, bias=st[:, 0:1], accum_out=st[:, 1:2]).then_inc(p_ready, 1)
                    keep_probs(act, act.copy, 1, n)
                    w = 512 if br == "mem" else P
                    act.wait_ge(o_read, n + 1)
                    act.dma_start(scr[br].rearrange("b h c -> (b h) c")[P * r:P * r + P], osb[n % 2][:, 0:w]).then_inc(o_scr[n % 2], 16)

            @block.vector
            def _(dve):
                ch = Chain(j_chain, dve)
                dve.wait_ge(self.vecs_loaded, 16 * len(VECS))
                for r in range(R4):
                    dve.wait_ge(e_s, r + 1)
                    dve.tensor_reduce(st[:, 0:1], ps[:, 0, 0:NCMP], AX, ALU.max, negate=True).then_inc(e_max, 1)
                    dve.wait_ge(e_exp, r + 1)
                    dve.reciprocal(st[:, 2:3], st[:, 1:2]).then_inc(chain, 1)
                    dve.wait_ge(chain, 3 * r + 1)
                    dve.tensor_scalar(pc[:, :], pc[:, :], st[:, 2:3], None, ALU.mult).then_inc(chain, 1)
                    dve.wait_ge(e_imp, 2 * r + 1)
                    dve.tensor_copy(imp[:, 0, :], ps[:, 2, 0:NSEL]).then_inc(imp_kept, 1)
                    dve.wait_ge(e_imp, 2 * r + 2)
                    ch.step(dve.tensor_copy(imp[:, 1, :], ps[:, 4, 0:NSEL]))
                    ch.step(dve.memset(imp[:, 1, 0:NSEL:NSEL - 1], FORCE))
                    ch.step(dve.max(top[:, 0, :], imp[:, 1, :]))
                    ch.step(dve.match_replace(imp[:, 2, :], top[:, 0, :], imp[:, 1, :], NEG))
                    ch.step(dve.max(top[:, 1, :], imp[:, 2, :]))
                    ch.step(dve.match_replace(imp[:, 3, :], top[:, 1, :], imp[:, 2, :], NEG))
                    ch.step(dve.tensor_tensor(bias[:, r, :], imp[:, 3, :], imp[:, 1, :], ALU.not_equal))
                    ch.step(dve.tensor_scalar(bias[:, r, :], bias[:, r, :], -1.0, -NEG, ALU.add, ALU.mult))
                    dve.wait_ge(e_o, r + 1)
                    dve.tensor_copy(osb[r % 2][:, 0:P], ps[:, 3, 0:P]).then_inc(chain, 1)
                dve.wait_ge(e_exp, R4)
                for n, (br, r) in enumerate(jobs):
                    T = NTL[br]
                    L = T * P
                    keep_keys(dve, dve.tensor_copy, 0, n)
                    dve.wait_ge(s_done, 4 * n + 4)
                    if n:
                        dve.wait_ge(turned, base[n])
                    if br == "sel":
                        dve.tensor_tensor(Ss[:, 0:L].rearrange("p (s k) -> p s k", k=64), ps[:, 0:4, :].rearrange("p b (s k) -> p (b s) k", k=64),
                                          bias[:, r, 0:NSEL - 1].unsqueeze(2).broadcast_to([P, NSEL - 1, 64]), ALU.add).then_inc(j_chain, 1)
                    else:
                        dve.tensor_copy(Ss[:, 0:L], ps[:, 0, 0:L]).then_inc(j_chain, 1)
                    ch.n += 1
                    if br != "mem":
                        dve.tensor_copy(Ss[:, L:L + 1], ps[:, 4, 0:1]).then_inc(j_chain, 1)
                        ch.n += 1
                    dve.wait_ge(j_chain, ch.n)
                    dve.sem_inc(s_read, 1)
                    if br == "win":
                        ch.step(dve.memset(Ss[:, 0:1], NEG))
                    dve.tensor_reduce(st[:, 0:1], Ss[:, 0:width(n)], AX, ALU.max, negate=True).then_inc(nmax, 1)
                    dve.wait_ge(p_ready, n + 1)
                    ch.step(dve.reciprocal(st[:, 2:3], st[:, 1:2]))
                    keep_probs(dve, dve.tensor_copy, 0, n)
                    dve.wait_ge(slot_free, 4 * n + 4)
                    w = 512 if br == "mem" else P
                    dve.wait_ge(o_scr[n % 2], 16 * (1 + n // 2))
                    dve.tensor_scalar(osb[n % 2][:, 0:w], ps[:, 7, 0:w], st[:, 2:3], None, ALU.mult).then_inc(o_read, 1)
                dve.wait_ge(back, 160)
                g = lambda i: self.gate[0:NB, TT, i:3 * NH:3].unsqueeze(2).broadcast_to([NB, NH, HD])
                hd = lambda a: a.rearrange("b (h d) -> b h d", d=HD)
                for i in range(3):
                    ch.step(dve.tensor_tensor(hd(obr[:, i, :]), hd(obr[:, i, :]), g(i), ALU.mult))
                ch.step(dve.tensor_tensor(obr[:, 0, :], obr[:, 0, :], obr[:, 1, :], ALU.add))
                ch.step(dve.tensor_tensor(proj[0:NB, TT, 0:NH * HD], obr[:, 0, :], obr[:, 2, :], ALU.add))
        self.free("pt", "slot0", "slot1", "KT0", "KT1", "PT", "PTn", "Ss", "pc", "PTc", "imp", "bias", "top", "st", "osb0", "osb1",
                  "kcT", "vc", "qblk", "qmpad", "knT", "vnew", "gate")

    def stage_gdn_project(self):
        I = self.I
        self.graw = self.sb("graw", [P, CC, 3 + NT])
        tiles, units = [], []
        for n in range(3):
            tiles.append((I["w_in"][:, C_GDN + 512 * n:C_GDN + 512 * n + 512], 512))
            for m in range(4):
                for h in range(2):
                    units.append((n, lambda w, c, m=m, h=h: (w[:, c, m * P:(m + 1) * P], self.uT[:, c, 260 * h:260 * h + 260]),
                                  P, 260, self.graw[:, 4 * n + m, 3 + 260 * h:3 + 260 * h + 260]))
        self.dense("gdn", tiles, units, tiles[2:] + self.merge_tiles()[0:2])

    def stage_gdn_conv(self):
        nc, I, O, ps, proj, graw = self.nc, self.I, self.O, self.ps, self.proj, self.graw
        ident = self.C("ident")
        cT = self.cT = self.sb("cT", [P, CC, NT])
        self.beta, self.g = self.sb("beta", [P, TT + 1, GH]), self.sb("g", [P, TT + 1, GH])
        buf, bufT = self.sb("buf", [3 * NB, CONV]), self.sb("bufT", [P, CC, 3 * NB])
        newc = self.sb("newc", [3 + NB, CONV])
        tmp, tmp2 = self.sb("ctmp", [P, 2, CC, NB]), self.sb("gtmp", [P, 3, (TT + 1) * GH])
        nega = self.sb("nega", [P, GH])
        S = self.sem
        buf_in, turned, kept, convd, silu, gates, gact, stored, zeroed = (S("f_" + x) for x in ("buf", "turned", "kept", "conv", "silu", "g", "gact", "stored", "zero"))
        chain = S("f_chain")
        w = lambda j, c: self.gcol[:, 24 + 12 * j + c:25 + 12 * j + c]
        x0 = (TT + 1) * GH
        with nc.Block() as block:
            @block.sync
            def _(sp):
                sp.dma_start(buf[:, :], I["state_gdn_conv"].rearrange("b j c -> (b j) c")).then_inc(buf_in, 16)
                sp.dma_start(O["s_conv"][:, 0:2], I["state_gdn_conv"][:, 1:3]).then_inc(stored, 16)
                sp.wait_ge(kept, 6)
                sp.dma_start(O["p_conv"][0], newc[0:3, :]).then_inc(stored, 16)
                sp.dma_start(O["s_conv"][:, 2], newc[3:3 + NB, :]).then_inc(stored, 16)
                sp.wait_ge(stored, 48)

            @block.tensor
            def _(pe):
                for i in range(3):
                    for c in range(4):
                        ins = pe.transpose(ps[0:3 + NB, i, c * P:(c + 1) * P], graw[:, 4 * i + c, SEQ:SEQ + 3 + NB], ident)
                    ins.then_inc(turned, 1)
                pe.wait_ge(buf_in, 16)
                for i in range(3):
                    for c in range(4):
                        ins = pe.transpose(ps[:, 3 + i, c * P:c * P + 3 * NB], buf[:, (4 * i + c) * P:(4 * i + c + 1) * P], ident[0:3 * NB, 0:3 * NB])
                    ins.then_inc(turned, 1)

            @block.scalar
            def _(act):
                for i in range(3):
                    act.wait_ge(turned, i + 1)
                    act.copy(newc[:, 512 * i:512 * i + 512], ps[0:3 + NB, i, :]).then_inc(kept, 1)
                for i in range(3):
                    act.wait_ge(turned, 4 + i)
                    act.copy(bufT[:, 4 * i:4 * i + 4, :], ps[:, 3 + i, :].rearrange("p (c t) -> p c t", c=4)[:, :, 0:3 * NB]).then_inc(kept, 1)
                act.wait_ge(gates, 1)
                act.activation(self.beta[:, :, :], self.beta[:, :, :], ACT.Sigmoid).then_inc(gact, 1)
                act.wait_ge(gates, 2)
                act.activation(tmp2[:, 1, :], tmp2[:, 1, :], ACT.Exp, scale=-1.0).then_inc(gact, 1)
                act.activation(nega[:, :], self.V("gdn_A_log"), ACT.Exp).then_inc(gact, 1)
                act.wait_ge(gates, 3)
                act.activation(tmp2[:, 1, :], tmp2[:, 1, :], ACT.Ln).then_inc(gact, 1)
                act.activation(proj[:, 0:TT, tok_col(C_Z):tok_col(C_Z) + 512], proj[:, 0:TT, tok_col(C_Z):tok_col(C_Z) + 512], ACT.Silu).then_inc(silu, 1)
                act.activation(proj[0:NB, TT, tok_col(C_Z):tok_col(C_Z) + 512], proj[0:NB, TT, tok_col(C_Z):tok_col(C_Z) + 512], ACT.Silu).then_inc(silu, 1)
                act.wait_ge(convd, 1)
                act.activation(cT[:, :, SEQ:NT], cT[:, :, SEQ:NT], ACT.Silu).then_inc(silu, 1)
                for i in range(3):
                    act.wait_ge(convd, 2 + i)
                    act.activation(cT[:, 4 * i:4 * i + 4, 0:SEQ], cT[:, 4 * i:4 * i + 4, 0:SEQ], ACT.Silu).then_inc(silu, 1)

            @block.vector
            def _(dve):
                ch = Chain(chain, dve)
                ch.step(dve.memset(self.beta[:, :, :], 0.0))
                ch.step(dve.memset(self.g[:, :, :], 0.0))
                ba = lambda c, t, R: proj[0:R, t, tok_col(c):tok_col(c) + GH]
                ch.inc(dve.tensor_copy(self.g[:, 0:TT, :], proj[:, 0:TT, tok_col(C_A):tok_col(C_A) + GH]))
                ch.inc(dve.tensor_copy(self.g[0:NB, TT, :], ba(C_A, TT, NB)))
                ch.step(dve.tensor_copy(self.beta[:, 0:TT, :], proj[:, 0:TT, tok_col(C_B):tok_col(C_B) + GH]))
                dve.tensor_copy(self.beta[0:NB, TT, :], ba(C_B, TT, NB)).then_inc(gates, 1)
                ch.step(dve.tensor_tensor(self.g[:, :, :], self.g[:, :, :], self.V("gdn_dt_bias").unsqueeze(1).broadcast_to([P, TT + 1, GH]), ALU.add))
                gf = self.g.rearrange("p t h -> p (t h)")
                ch.step(dve.tensor_scalar(tmp2[:, 0, :], gf, 0.0, None, ALU.max))
                dve.scalar_tensor_tensor(tmp2[:, 1, :], gf, -1.0, gf, ALU.mult, ALU.max).then_inc(gates, 1)
                dve.wait_ge(gact, 2)
                dve.tensor_scalar(tmp2[:, 1, :], tmp2[:, 1, :], 1.0, None, ALU.add).then_inc(gates, 1)
                dve.wait_ge(gact, 4)
                ch.step(dve.tensor_tensor(gf, tmp2[:, 0, :], tmp2[:, 1, :], ALU.add))
                ch.step(dve.tensor_scalar(nega[:, :], nega[:, :], -1.0, None, ALU.mult))
                ch.step(dve.tensor_tensor(self.g[:, :, :], self.g[:, :, :], nega.unsqueeze(1).broadcast_to([P, TT + 1, GH]), ALU.mult))
                dve.wait_ge(kept, 6)
                cs = cT[:, :, SEQ:NT]
                wj = lambda j: self.gcol[:, 24 + 12 * j:36 + 12 * j].unsqueeze(2).broadcast_to([P, CC, NB])
                ch.step(dve.tensor_tensor(cs, graw[:, :, 3 + SEQ:3 + NT], wj(3), ALU.mult))
                bT = bufT.rearrange("p c (b j) -> p c j b", j=3)
                for j in range(3):
                    ch.step(dve.tensor_tensor(tmp[:, j % 2], bT[:, :, j, :], wj(j), ALU.mult))
                    if j < 2:
                        ch.step(dve.tensor_tensor(cs, cs, tmp[:, j % 2], ALU.add))
                    else:
                        dve.tensor_tensor(cs, cs, tmp[:, j % 2], ALU.add).then_inc(convd, 1)
                for half in range(3):
                    dve.memset(graw[:, 4 * half:4 * half + 4, 0:3], 0.0).then_inc(zeroed, 1)
                dve.wait_ge(zeroed, 3)
                for i in range(3):
                    for j in range(4):
                        for c in range(4 * i, 4 * i + 4):
                            if j == 0:
                                ins = dve.tensor_scalar(cT[:, c, 0:SEQ], graw[:, c, 0:SEQ], w(0, c), None, ALU.mult)
                            else:
                                dve.wait_ge(chain, ch.n - 3)
                                ins = dve.scalar_tensor_tensor(cT[:, c, 0:SEQ], graw[:, c, j:j + SEQ], w(j, c), cT[:, c, 0:SEQ], ALU.mult, ALU.add)
                            if j == 3 and c == 4 * i + 3:
                                ins.then_inc(convd, 1)
                            else:
                                ch.inc(ins)
        self.free("graw", "buf", "bufT", "newc", "ctmp", "gtmp", "nega")

    def stage_gdn_prompt(self):
        nc, I, O, ps, proj = self.nc, self.I, self.O, self.ps, self.proj
        ident, cT = self.C("ident"), self.cT
        names = ("qn", "kn", "kb", "kbe", "kd", "qe", "vb", "qnT", "knT", "kbT", "qeT", "E", "AT", "attT", "X0", "X1", "XT0", "XT1",
                 "Am", "Y", "nWT", "vn", "state")
        B = {n: self.sb("g_" + n, [P, GH, P]) for n in names}
        B["sq"] = self.sb("g_sq", [P, 2 * GH, P])
        X, XT = [B["X0"], B["X1"]], [B["XT0"], B["XT1"]]
        sc = self.sb("g_sc", [P, 12, GH])
        DEC, DL, LAST, ED, EDL, EL, RQ, RK, RQE, RKB, RKBE, RKD = range(12)
        so = self.sb("g_so", [P, GH])
        S = self.sem
        L = 7
        p = Steps(S("gp_pe"), ["dec", "tq", "tk", "tv", "tqn", "tkn", "tkb", "tqe", "at", "att", "Y0"]
                  + [n + str(l) for l in range(1, L) for n in ("Y", "XY", "XYT") if n + str(l) != f"XY{L - 1}"] + ["wt", "vn", "o", "ds"])
        v = Steps(S("gp_dve"), ["sc", "e1", "ss", "rt", "qn", "qe", "kn", "kb", "kbe", "kd", "vb", "e2", "AT", "attT", "Am0", "XT0", "X0"]
                  + [n + str(l) for l in range(1, L) for n in ("Am", "X", "XT") if n + str(l) != f"X{L - 1}"] + ["so", "state", "out"])
        a = Steps(S("gp_act"), ["ed", "E", "sqq", "sqk", "rt", "qnT", "knT", "kbT", "qeT"] + [f"Y{l}" for l in range(1, L)] + ["nWT", "vn", "sqo", "ro"])
        stored = S("gp_stored")
        bank = lambda b: ps[:, b, :].rearrange("p (h d) -> p h d", h=GH)
        bc = lambda x: x.unsqueeze(2).broadcast_to([P, GH, P])
        heads = lambda x: x.unsqueeze(1).broadcast_to([P, GH, P])
        with nc.Block() as block:
            @block.sync
            def _(sp):
                v.wait(sp, "state", TT - 1)
                sp.dma_start(O["p_state"][0].rearrange("h k v -> k h v"), B["state"][:, :, :]).then_inc(stored, 16)
                sp.wait_ge(stored, 16)

            @block.tensor
            def _(pe):
                def product(b, lhsT, rhs, name, t, start=True, stop=True):
                    for h in range(GH):
                        ins = pe.matmul(ps[:, b, h * P:(h + 1) * P], lhsT[:, h, :], rhs[:, h, :], start=start, stop=stop)
                    p.done(ins, name, t)

                for t in range(TT):
                    s = slice(t * P, (t + 1) * P)
                    if t:
                        v.wait(pe, "out", t - 1)
                    g = self.g[:, t, :]
                    for h in range(GH):
                        pe.matmul(ps[:, 0, h * P:(h + 1) * P], g[:, h:h + 1].broadcast_to([P, P]), self.C("upper"), start=True, stop=True)
                    pe.matmul(ps[:, 1, 0:GH], self.C("upper"), g, start=True, stop=True)
                    p.done(pe.matmul(ps[:, 1, GH:2 * GH], self.C("ones"), g, start=True, stop=True), "dec", t)
                    for i, name in enumerate(("tq", "tk", "tv")):
                        for h in range(GH):
                            ins = pe.transpose(ps[:, 2 + i, h * P:(h + 1) * P], cT[:, GH * i + h, s], ident)
                        p.done(ins, name, t)
                    for name, b in (("qn", 5), ("kn", 6), ("kb", 7), ("qe", 0)):
                        v.wait(pe, name, t)
                        for h in range(GH):
                            ins = pe.transpose(ps[:, b, h * P:(h + 1) * P], B[name][:, h, :], ident)
                        p.done(ins, "t" + name, t)
                    a.wait(pe, "kbT", t)
                    product(1, B["knT"], B["kbT"], "at", t)
                    product(2, B["knT"], B["qnT"], "att", t)
                    v.wait(pe, "Am0", t)
                    for h in range(GH):
                        ins = pe.matmul(ps[:, 3, h * P:(h + 1) * P], B["Am"][:, h, :], ident, start=True, stop=True)
                    p.done(ins, "Y0", t)
                    for l in range(1, L):
                        x, xt = X[(l + 1) % 2], XT[(l + 1) % 2]
                        v.wait(pe, f"Am{l}", t)
                        v.wait(pe, f"X{l - 1}", t)
                        product(3, B["Am"], x, f"Y{l}", t)
                        v.wait(pe, f"XT{l - 1}", t)
                        a.wait(pe, f"Y{l}", t)
                        if l < L - 1:
                            product(4, xt, B["Y"], f"XY{l}", t)
                        product(5, B["Y"], xt, f"XYT{l}", t)
                    v.wait(pe, f"XT{L - 1}", t)
                    xt = XT[(L - 1) % 2]
                    product(6, B["kbe"], xt, "wt", t)
                    a.wait(pe, "nWT", t)
                    for h in range(GH):
                        ins = pe.matmul(ps[:, 7, h * P:(h + 1) * P], xt[:, h, :], B["vb"][:, h, :], start=True, stop=(t == 0))
                        if t:
                            ins = pe.matmul(ps[:, 7, h * P:(h + 1) * P], B["nWT"][:, h, :], B["state"][:, h, :], start=False, stop=True)
                    p.done(ins, "vn", t)
                    a.wait(pe, "vn", t)
                    a.wait(pe, "qeT", t)
                    v.wait(pe, "attT", t)
                    for h in range(GH):
                        if t:
                            pe.matmul(ps[:, 0, h * P:(h + 1) * P], B["qeT"][:, h, :], B["state"][:, h, :], start=True, stop=False)
                        ins = pe.matmul(ps[:, 0, h * P:(h + 1) * P], B["attT"][:, h, :], B["vn"][:, h, :], start=(t == 0), stop=True)
                    p.done(ins, "o", t)
                    product(1, B["kd"], B["vn"], "ds", t)

            @block.scalar
            def _(act):
                def keep(b, dst, name, t, src="t", scale=1.0):
                    p.wait(act, src + name if src == "t" else src, t)
                    a.done(act.activation(B[dst][:, :, :], bank(b), ACT.Copy, scale=scale), dst, t)

                for t in range(TT):
                    v.wait(act, "sc", t)
                    a.done(act.activation(sc[:, ED:EL + 1, :], sc[:, DEC:LAST + 1, :], ACT.Exp), "ed", t)
                    v.wait(act, "e1", t)
                    a.done(act.activation(B["E"][:, :, :], B["E"][:, :, :], ACT.Exp), "E", t)
                    p.wait(act, "tk", t)
                    a.done(act.activation(B["sq"][:, 0:GH, :], bank(2), ACT.Square), "sqq", t)
                    a.done(act.activation(B["sq"][:, GH:, :], bank(3), ACT.Square), "sqk", t)
                    v.wait(act, "ss", t)
                    a.done(act.activation(sc[:, RQ:RK + 1, :], sc[:, RQ:RK + 1, :], ACT.Sqrt), "rt", t)
                    for name, b in (("qn", 5), ("kn", 6), ("kb", 7), ("qe", 0)):
                        p.wait(act, "t" + name, t)
                        a.done(act.copy(B[name + "T"][:, :, :], bank(b)), name + "T", t)
                    for l in range(1, L):
                        p.wait(act, f"Y{l}", t)
                        if l > 1:
                            p.wait(act, f"XYT{l - 1}", t)
                        a.done(act.copy(B["Y"][:, :, :], bank(3)), f"Y{l}", t)
                    p.wait(act, "wt", t)
                    a.done(act.activation(B["nWT"][:, :, :], bank(6), ACT.Copy, scale=-1.0), "nWT", t)
                    p.wait(act, "vn", t)
                    a.done(act.copy(B["vn"][:, :, :], bank(7)), "vn", t)
                    p.wait(act, "o", t)
                    a.done(act.activation(B["sq"][:, 0:GH, :], bank(0), ACT.Square), "sqo", t)
                    v.wait(act, "so", t)
                    a.done(act.activation(so[:, :], so[:, :], ACT.Sqrt), "ro", t)

            @block.vector
            def _(dve):
                ch = Chain(S("gp_chain"), dve)
                for t in range(TT):
                    beta = self.beta[:, t, :]
                    p.wait(dve, "dec", t)
                    ch.step(dve.tensor_copy(sc[:, DEC, :], ps[:, 1, 0:GH]))
                    ch.step(dve.tensor_copy(sc[:, LAST, :], ps[:, 1, GH:2 * GH]))
                    v.done(dve.tensor_tensor(sc[:, DL, :], sc[:, LAST, :], sc[:, DEC, :], ALU.subtract), "sc", t)
                    for h in range(GH):
                        ins = dve.tensor_scalar(B["E"][:, h, :], ps[:, 0, h * P:(h + 1) * P], sc[:, DEC, h:h + 1], 0.0, ALU.subtract, ALU.min)
                        if h < GH - 1:
                            ch.inc(ins)
                    dve.wait_ge(ch.sem, ch.n)
                    v.done(ins, "e1", t)
                    a.wait(dve, "sqk", t)
                    ch.step(dve.tensor_reduce(sc[:, RQ:RK + 1, :].rearrange("p a h -> p (a h)"), B["sq"][:, :, :], AX, ALU.add))
                    v.done(dve.tensor_scalar(sc[:, RQ:RK + 1, :], sc[:, RQ:RK + 1, :], EPS, None, ALU.add), "ss", t)
                    a.wait(dve, "rt", t)
                    ch.step(dve.reciprocal(sc[:, RQ:RK + 1, :], sc[:, RQ:RK + 1, :]))
                    ch.step(dve.tensor_scalar(sc[:, RQ, :], sc[:, RQ, :], float(GD) ** -0.5, None, ALU.mult))
                    ch.step(dve.tensor_tensor(sc[:, RKB, :], sc[:, RK, :], beta, ALU.mult))
                    ch.step(dve.tensor_tensor(sc[:, RQE, :], sc[:, RQ, :], sc[:, ED, :], ALU.mult))
                    ch.step(dve.tensor_tensor(sc[:, RKBE, :], sc[:, RKB, :], sc[:, ED, :], ALU.mult))
                    v.done(dve.tensor_tensor(sc[:, RKD, :], sc[:, RK, :], sc[:, EDL, :], ALU.mult), "rt", t)
                    v.wait(dve, "rt", t)
                    for name, b, r in (("qn", 2, RQ), ("qe", 2, RQE), ("kn", 3, RK), ("kb", 3, RKB), ("kbe", 3, RKBE), ("kd", 3, RKD)):
                        v.done(dve.tensor_tensor(B[name][:, :, :], bank(b), bc(sc[:, r, :]), ALU.mult), name, t)
                    p.wait(dve, "tv", t)
                    v.done(dve.tensor_tensor(B["vb"][:, :, :], bank(4), bc(beta), ALU.mult), "vb", t)
                    a.wait(dve, "E", t)
                    v.done(dve.tensor_tensor(B["E"][:, :, :], B["E"][:, :, :], heads(self.C("upper")), ALU.mult), "e2", t)
                    v.wait(dve, "e2", t)
                    p.wait(dve, "at", t)
                    v.done(dve.tensor_tensor(B["AT"][:, :, :], bank(1), B["E"][:, :, :], ALU.mult), "AT", t)
                    p.wait(dve, "att", t)
                    v.done(dve.tensor_tensor(B["attT"][:, :, :], bank(2), B["E"][:, :, :], ALU.mult), "attT", t)
                    v.wait(dve, "AT", t)
                    level = lambda l: heads(self.C("levels", l * P, (l + 1) * P))
                    v.done(dve.tensor_tensor(B["Am"][:, :, :], B["AT"][:, :, :], level(0), ALU.mult), "Am0", t)
                    v.wait(dve, "Am0", t)
                    v.done(dve.tensor_tensor(XT[0][:, :, :], heads(ident), B["Am"][:, :, :], ALU.subtract), "XT0", t)
                    p.wait(dve, "Y0", t)
                    v.done(dve.scalar_tensor_tensor(X[0][:, :, :], bank(3), -1.0, heads(ident), ALU.mult, ALU.add), "X0", t)
                    for l in range(1, L):
                        x, xt, y, yt = X[(l + 1) % 2], XT[(l + 1) % 2], X[l % 2], XT[l % 2]
                        p.wait(dve, f"Y{l - 1}", t)
                        v.wait(dve, f"XT{l - 1}", t)
                        v.done(dve.tensor_tensor(B["Am"][:, :, :], B["AT"][:, :, :], level(l), ALU.mult), f"Am{l}", t)
                        if l < L - 1:
                            p.wait(dve, f"XY{l}", t)
                            v.done(dve.scalar_tensor_tensor(y[:, :, :], bank(4), -1.0, x[:, :, :], ALU.mult, ALU.add), f"X{l}", t)
                        p.wait(dve, f"XYT{l}", t)
                        v.done(dve.scalar_tensor_tensor(yt[:, :, :], bank(5), -1.0, xt[:, :, :], ALU.mult, ALU.add), f"XT{l}", t)
                    a.wait(dve, "sqo", t)
                    ch.step(dve.tensor_reduce(so[:, :], B["sq"][:, 0:GH, :], AX, ALU.add))
                    v.done(dve.tensor_scalar(so[:, :], so[:, :], 1.0 / GD, EPS, ALU.mult, ALU.add), "so", t)
                    p.wait(dve, "ds", t)
                    if t == 0:
                        v.done(dve.tensor_copy(B["state"][:, :, :], bank(1)), "state", t)
                    else:
                        ch.step(dve.tensor_tensor(B["state"][:, :, :], B["state"][:, :, :], bc(sc[:, EL, :]), ALU.mult))
                        v.done(dve.tensor_tensor(B["state"][:, :, :], B["state"][:, :, :], bank(1), ALU.add), "state", t)
                    z = proj[:, t, tok_col(C_Z):tok_col(C_Z) + GH * GD].rearrange("p (h d) -> p h d", d=GD)
                    dst = proj[:, t, 512:1024].rearrange("p (h d) -> p h d", d=GD)
                    a.wait(dve, "ro", t)
                    ch.step(dve.reciprocal(so[:, :], so[:, :]))
                    ch.step(dve.tensor_tensor(dst, bank(0), bc(so), ALU.mult))
                    ch.step(dve.tensor_tensor(dst, dst, heads(self.V("gdn_o_norm")), ALU.mult))
                    v.done(dve.tensor_tensor(dst, dst, z, ALU.mult), "out", t)
                    v.wait(dve, "out", t)
        self.free(*("g_" + n for n in names), "g_sq", "g_sc", "g_so")

    def stage_gdn_sample(self):
        nc, I, O, ps, proj = self.nc, self.I, self.O, self.ps, self.proj
        ident, cT = self.C("ident"), self.cT
        HB = GH * NB
        S0 = self.sb("s_S0", [P, GH, NB, P])
        sq, qkn = self.sb("s_sq", [P, 2 * HB]), self.sb("s_qkn", [P, 2 * HB])
        rn = self.sb("s_rn", [P, 2 * HB])
        pairs = self.sb("s_pairs", [P, HB, 2])
        prod = self.sb("s_prod", [P, HB])
        gb = self.sb("s_gb", [NB, 2, HB])
        bcs = self.sb("s_bcs", [P, 3, HB])
        vn, oT = self.sb("s_vn", [P, HB]), self.sb("s_oT", [P, HB])
        rows_kv = self.sb("s_rows", [HB, 2, P])
        Vm = self.sb("s_Vm", [HB, HB, P])
        eg = self.sb("s_eg", [NB, GH])
        tmp = self.sb("s_tmp", [P, HB])
        so, sqo = self.sb("s_so", [NB, GH]), self.sb("s_sqo", [NB, GH, GD])
        S = self.sem
        s_in, stored = S("s_in"), S("s_stored")
        p = Steps(S("s_pe"), ["sums", "bc", "qk", "read", "rows", "orow"] + [f"add{i}" for i in range(8)])
        a = Steps(S("s_act"), ["eg", "rt", "rows", "sqo", "ro"])
        v = Steps(S("s_dve"), ["sq", "mean", "gb", "prod", "pairs", "vn", "oT", "Vm", "so", "out"] + [f"add{i}" for i in range(8)])
        two = lambda x: x.rearrange("p c b -> p (c b)")
        with nc.Block() as block:
            @block.sync
            def _(sp):
                for h in range(GH):
                    sp.dma_start(S0[:, h], I["state_gdn"][:, h].rearrange("b k v -> k b v")).then_inc(s_in, 16)
                for h in range(GH):
                    v.wait(sp, f"add{2 * h + 1}", 0)
                    sp.dma_start(O["s_state"][:, h].rearrange("b k v -> k b v"), S0[:, h]).then_inc(stored, 16)
                sp.wait_ge(stored, 64)

            @block.tensor
            def _(pe):
                v.wait(pe, "sq", 0)
                p.done(pe.matmul(ps[:, 0, 0:2 * HB], self.C("ones"), sq[:, :], start=True, stop=True), "sums", 0)
                v.wait(pe, "gb", 0)
                p.done(pe.matmul(ps[:, 1, 0:2 * HB], self.C("ones")[0:NB, :], gb.rearrange("b i c -> b (i c)"), start=True, stop=True), "bc", 0)
                v.wait(pe, "prod", 0)
                p.done(pe.matmul(ps[:, 2, 0:HB], self.C("ones"), prod[:, :], start=True, stop=True), "qk", 0)
                v.wait(pe, "pairs", 0)
                pe.wait_ge(s_in, 64)
                for i in range(HB):
                    ins = pe.matmul(ps[:, 3, 2 * i:2 * i + 2], S0[:, i // NB, i % NB, :], pairs[:, i, :], start=True, stop=True)
                p.done(ins, "read", 0)
                v.wait(pe, "vn", 0)
                pe.transpose(ps[0:HB, 4, 0:P], qkn[:, HB:], ident)
                p.done(pe.transpose(ps[0:HB, 4, P:2 * P], vn[:, :], ident), "rows", 0)
                v.wait(pe, "oT", 0)
                for h in range(GH):
                    ins = pe.transpose(ps[0:NB, 5, h * P:(h + 1) * P], oT[:, h * NB:(h + 1) * NB], ident)
                p.done(ins, "orow", 0)
                v.wait(pe, "Vm", 0)
                for i in range(8):
                    if i >= 2:
                        v.wait(pe, f"add{i - 2}", 0)
                    p.done(pe.matmul(ps[:, 6 + i % 2, :], rows_kv[:, 0, :], Vm[:, 4 * i:4 * i + 4, :], start=True, stop=True), f"add{i}", 0)

            @block.scalar
            def _(act):
                a.done(act.activation(eg[:, :], self.g[0:NB, TT, :], ACT.Exp), "eg", 0)
                v.wait(act, "mean", 0)
                a.done(act.activation(rn[:, :], rn[:, :], ACT.Sqrt), "rt", 0)
                p.wait(act, "rows", 0)
                a.done(act.copy(rows_kv[:, :, :], ps[0:HB, 4, 0:2 * P].rearrange("p (i d) -> p i d", i=2)), "rows", 0)
                p.wait(act, "orow", 0)
                a.done(act.activation(sqo[:, :, :], ps[0:NB, 5, :].rearrange("p (h d) -> p h d", h=GH), ACT.Square), "sqo", 0)
                v.wait(act, "so", 0)
                a.done(act.activation(so[:, :], so[:, :], ACT.Sqrt), "ro", 0)

            @block.vector
            def _(dve):
                ch = Chain(S("s_chain"), dve)
                qk = cT[:, 0:2 * GH, SEQ:NT]
                v3 = lambda x: x.rearrange("p (c b) -> p c b", b=NB)
                v.done(dve.tensor_tensor(v3(sq), qk, qk, ALU.mult), "sq", 0)
                p.wait(dve, "sums", 0)
                v.done(dve.tensor_scalar(rn[:, :], ps[:, 0, 0:2 * HB], EPS, None, ALU.add), "mean", 0)
                a.wait(dve, "eg", 0)
                own = ident[0:NB, 0:NB].unsqueeze(1).broadcast_to([NB, GH, NB])
                each = lambda x: x.unsqueeze(2).broadcast_to([NB, GH, NB])
                ch.step(dve.tensor_tensor(v3(gb[:, 0]), own, each(self.beta[0:NB, TT, :]), ALU.mult))
                v.done(dve.tensor_tensor(v3(gb[:, 1]), own, each(eg), ALU.mult), "gb", 0)
                a.wait(dve, "rt", 0)
                ch.step(dve.reciprocal(rn[:, :], rn[:, :]))
                ch.step(dve.tensor_tensor(v3(qkn), qk, v3(rn), ALU.mult))
                ch.step(dve.tensor_scalar(qkn[:, 0:HB], qkn[:, 0:HB], float(GD) ** -0.5, None, ALU.mult))
                v.done(dve.tensor_tensor(prod[:, :], qkn[:, 0:HB], qkn[:, HB:], ALU.mult), "prod", 0)
                ch.step(dve.tensor_copy(pairs[:, :, 0], qkn[:, HB:]))
                v.done(dve.tensor_copy(pairs[:, :, 1], qkn[:, 0:HB]), "pairs", 0)
                p.wait(dve, "qk", 0)
                ch.step(dve.tensor_copy(bcs[:, 0:2, :], ps[:, 1, 0:2 * HB].rearrange("p (i c) -> p i c", i=2)))
                ch.step(dve.tensor_copy(bcs[:, 2, :], ps[:, 2, 0:HB]))
                p.wait(dve, "read", 0)
                kS, qS = ps[:, 3, 0:2 * HB:2], ps[:, 3, 1:2 * HB:2]
                ch.step(dve.tensor_tensor(tmp[:, :], kS, bcs[:, 1, :], ALU.mult))
                ch.step(dve.tensor_tensor(v3(tmp), cT[:, 2 * GH:3 * GH, SEQ:NT], v3(tmp), ALU.subtract))
                v.done(dve.tensor_tensor(vn[:, :], tmp[:, :], bcs[:, 0, :], ALU.mult), "vn", 0)
                v.wait(dve, "vn", 0)
                ch.step(dve.tensor_tensor(tmp[:, :], vn[:, :], bcs[:, 2, :], ALU.mult))
                ch.step(dve.tensor_tensor(oT[:, :], qS, bcs[:, 1, :], ALU.mult))
                v.done(dve.tensor_tensor(oT[:, :], oT[:, :], tmp[:, :], ALU.add), "oT", 0)
                a.wait(dve, "rows", 0)
                v.done(dve.tensor_tensor(Vm[:, :, :], rows_kv[:, 1, :].unsqueeze(1).broadcast_to([HB, HB, P]),
                                         ident[0:HB, 0:HB].unsqueeze(2).broadcast_to([HB, HB, P]), ALU.mult), "Vm", 0)
                a.wait(dve, "sqo", 0)
                ch.step(dve.tensor_reduce(so[:, :], sqo[:, :, :], AX, ALU.add))
                v.done(dve.tensor_scalar(so[:, :], so[:, :], 1.0 / GD, EPS, ALU.mult, ALU.add), "so", 0)
                a.wait(dve, "ro", 0)
                ch.step(dve.reciprocal(so[:, :], so[:, :]))
                dst = proj[0:NB, TT, 512:1024].rearrange("p (h d) -> p h d", d=GD)
                z = proj[0:NB, TT, tok_col(C_Z):tok_col(C_Z) + GH * GD].rearrange("p (h d) -> p h d", d=GD)
                ch.step(dve.tensor_tensor(dst, ps[0:NB, 5, :].rearrange("p (h d) -> p h d", h=GH), so.unsqueeze(2).broadcast_to([NB, GH, GD]), ALU.mult))
                ch.step(dve.tensor_tensor(dst, dst, self.V("gdn_o_norm")[0:NB].unsqueeze(1).broadcast_to([NB, GH, GD]), ALU.mult))
                v.done(dve.tensor_tensor(dst, dst, z, ALU.mult), "out", 0)
                dve.wait_ge(s_in, 64)
                for i in range(8):
                    Si = S0[:, i // 2, 4 * (i % 2):4 * (i % 2) + 4, :]
                    ch.step(dve.tensor_tensor(Si, Si, bcs[:, 1, 4 * i:4 * i + 4].unsqueeze(2).broadcast_to([P, 4, P]), ALU.mult))
                    p.wait(dve, f"add{i}", 0)
                    v.done(dve.tensor_tensor(Si, Si, ps[:, 6 + i % 2, :].rearrange("p (s d) -> p s d", s=4), ALU.add), f"add{i}", 0)
        self.free("s_S0", "s_sq", "s_qkn", "s_rn", "s_pairs", "s_prod", "s_gb", "s_bcs", "s_vn", "s_oT", "s_rows", "s_Vm", "s_eg", "s_tmp",
                  "s_so", "s_sqo", "cT", "beta", "g")

    def merge_tiles(self):
        I, tiles = self.I, []
        for br, w in enumerate((I["w_br_nsa"], I["w_br_gdn"], I["w_br_mem"])):
            for half in range(2):
                a = C_GB + DM * br + 512 * half
                tiles.append((I["w_in"][:, a:a + 512], 512, KC))
                tiles.append((w[:, 512 * half:512 * half + 512], 512, 4))
        return tiles

    def half_units(self):
        return [(m, slice(HALF * h, HALF * h + HALF)) for m in range(4) for h in range(2)]

    def stage_merge(self):
        nc, I, ps, proj = self.nc, self.I, self.ps, self.proj
        ident = self.C("ident")
        oT = self.sb("oT", [P, 3, 4, NT])
        self.mergedT = self.sb("mergedT", [P, KC, NT])
        sig = self.sb("sig", [P, 4, NT])
        prod = [self.sb(f"m_prod{i}", [P, HALF]) for i in range(2)]
        S = self.sem
        gated, turned, oT_kept, taken, added, multiplied = (S("m_" + x) for x in ("gated", "turned", "oT_kept", "taken", "added", "multiplied"))
        acc, u0 = self.acc, self.units
        tiles, U = self.merge_tiles(), self.half_units()
        NU, PAIRS = len(U), len(tiles) // 2
        for n in range(len(tiles)):
            self.tile_end.append(u0 + NU * (n + 1))
        self.units += NU * len(tiles)
        cols = (0, 512, tok_col(C_QM))
        with nc.Block() as block:
            @block.sync
            def _(sp):
                for src, w, chunks in tiles[2:]:
                    self.load_tile(sp, src, w, chunks)
                for a in range(2):
                    self.load_tile(sp, I["w_out"][:, 512 * a:512 * a + 512], 512)

            @block.tensor
            def _(pe):
                for q in range(PAIRS):
                    w = self.tile_ready(pe)
                    for i, (m, tok) in enumerate(U):
                        u = q * NU + i
                        if u >= 4:
                            pe.wait_ge(gated, u - 3)
                        for c in range(KC):
                            ins = pe.matmul(ps[:, u % 4, 0:HALF], w[:, c, m * P:(m + 1) * P], self.uT[:, c, tok], start=(c == 0), stop=(c == KC - 1))
                        ins.then_inc(acc, 1)
                    if q == 0:
                        for i in range(3 * (TT + 1)):
                            br, t = i // (TT + 1), i % (TT + 1)
                            if i >= 4:
                                pe.wait_ge(oT_kept, i - 3)
                            for c in range(4):
                                ins = pe.transpose(ps[:, 4 + i % 4, c * P:c * P + rows(t)], proj[0:rows(t), t, cols[br] + c * P:cols[br] + (c + 1) * P],
                                                   ident[0:rows(t), 0:rows(t)])
                            ins.then_inc(turned, 1)
                        pe.wait_ge(oT_kept, 3 * (TT + 1))
                    w = self.tile_ready(pe)
                    for i, (m, tok) in enumerate(U):
                        u = q * NU + i
                        if u >= 4:
                            pe.wait_ge(taken, u - 3)
                        for c in range(4):
                            ins = pe.matmul(ps[:, 4 + u % 4, 0:HALF], w[:, c, m * P:(m + 1) * P], oT[:, q // 2, c, tok], start=(c == 0), stop=(c == 3))
                        ins.then_inc(acc, 1)

            @block.scalar
            def _(act):
                for q in range(PAIRS):
                    for i, (m, tok) in enumerate(U):
                        u = q * NU + i
                        act.wait_ge(acc, u0 + 2 * q * NU + i + 1)
                        if q:
                            act.wait_ge(taken, u - NU + 1)
                        act.activation(sig[:, m, tok], ps[:, u % 4, 0:HALF], ACT.Sigmoid).then_inc(gated, 1)

            @block.vector
            def _(dve):
                for i in range(3 * (TT + 1)):
                    br, t = i // (TT + 1), i % (TT + 1)
                    dve.wait_ge(turned, i + 1)
                    dve.tensor_copy(oT[:, br, :, t * P:t * P + rows(t)], ps[:, 4 + i % 4, :].rearrange("p (c t) -> p c t", c=4)[:, :, 0:rows(t)]).then_inc(oT_kept, 1)
                for q in range(PAIRS):
                    for i, (m, tok) in enumerate(U):
                        u = q * NU + i
                        dst = self.mergedT[:, 4 * (q % 2) + m, tok]
                        dve.wait_ge(gated, u + 1)
                        dve.wait_ge(acc, u0 + (2 * q + 1) * NU + i + 1)
                        if q < 2:
                            dve.tensor_tensor(dst, ps[:, 4 + u % 4, 0:HALF], sig[:, m, tok], ALU.mult).then_inc(taken, 1)
                            continue
                        v = u - 2 * NU
                        if v >= 2:
                            dve.wait_ge(added, v - 1)
                        dve.tensor_tensor(prod[v % 2], ps[:, 4 + u % 4, 0:HALF], sig[:, m, tok], ALU.mult).then_inc(taken, 1)
                        dve.wait_ge(taken, u + 1)
                        dve.tensor_tensor(dst, dst, prod[v % 2], ALU.add).then_inc(added, 1)
                dve.wait_ge(added, NU * (PAIRS - 2))
        self.free("oT", "sig", "m_prod0", "m_prod1", "proj", "uT")

    def ff1_tile(self, n):
        return self.I["w_ff1"][:, 512 * n:512 * n + 512]

    def stage_out(self):
        nc, I, ps = self.nc, self.I, self.ps
        h = self.h = self.sb("h", [P, TT + 1, DM])
        self.hT = self.sb("hT", [P, KC, NT])
        x_in, x_in_sample, h_ready = self.sem("o_x"), self.sem("o_xs"), self.sem("o_h")
        self.norm_stage_setup("o")
        srcs = [(h[0:rows(t), t, :], rows(t), self.hT[:, :, t * P:t * P + rows(t)], 16) for t in range(TT + 1)]
        acc, u0 = self.acc, self.units
        UN = TT + 1
        for n in range(2):
            self.tile_end.append(u0 + UN * (n + 1))
        self.units += 2 * UN
        with nc.Block() as block:
            @block.sync
            def _(sp):
                sp.dma_start(h[:, 0:TT, :], I["x_prompt"][0].rearrange("(t p) d -> p t d", p=P)).then_inc(x_in, 16)
                sp.dma_start(h[0:NB, TT, :], I["x_sample"][:, 0, :]).then_inc(x_in_sample, 16)
                for n in range(2):
                    self.load_tile(sp, self.ff1_tile(n), 512)

            @block.tensor
            def _(pe):
                for n in range(2):
                    w = self.tile_ready(pe)
                    for t in range(TT + 1):
                        u = n * UN + t
                        if u >= 4:
                            pe.wait_ge(h_ready, u - 3)
                        for c in range(KC):
                            ins = pe.matmul(ps[0:rows(t), 4 + u % 4, :], self.mergedT[:, c, t * P:t * P + rows(t)], w[:, c, :], start=(c == 0), stop=(c == KC - 1))
                        ins.then_inc(acc, 1)
                self.norm_pe(pe, srcs)

            @block.scalar
            def _(act):
                self.norm_act(act, srcs, {t: (h_ready, UN + t + 1) for t in range(TT + 1)})

            @block.vector
            def _(dve):
                dve.wait_ge(x_in, 16)
                dve.wait_ge(x_in_sample, 16)
                for n in range(2):
                    for t in range(TT + 1):
                        R, u = rows(t), n * UN + t
                        dve.wait_ge(acc, u0 + u + 1)
                        hh = h[0:R, t, 512 * n:512 * n + 512]
                        dve.tensor_tensor(hh, hh, ps[0:R, 4 + u % 4, :], ALU.add).then_inc(h_ready, 1)
                self.norm_dve(dve, srcs)
        self.free("ss", "xn0", "xn1", "nj", "mergedT")

    def stage_ff1(self):
        nc, ps = self.nc, self.ps
        fT = self.fT = self.sb("fT", [P, DFF // P, NT])
        positive = self.sb("positive", [P, 4, HALF])
        relu, kept = self.sem("ff1_relu"), self.sem("ff1_kept")
        acc, u0, first = self.acc, self.units, self.tiles
        U, PAIRS = self.half_units(), DFF // 1024
        NU = len(U)
        for n in range(2 * PAIRS):
            self.tile_end.append(u0 + NU * (n + 1))
        self.units += 2 * NU * PAIRS
        loaded = [16 * ((first + j) // 2 + 1) for j in range(2)]
        slot = [(first + j) % 2 for j in range(2)]
        self.tiles += 2 * PAIRS
        with nc.Block() as block:
            @block.sync
            def _(sp):
                with sp.Fori(1, PAIRS) as q:
                    for j in range(2):
                        sp.wait_ge(acc, q * (2 * NU) + (u0 + NU * (j - 1)))
                        src = self.I["w_ff1"][:, bass.ds(q * 1024 + 512 * j, 512)]
                        sp.dma_start(self.wt[slot[j]][:, :, :], src.rearrange("(c p) n -> p c n", p=P)).then_inc(self.w_loaded[slot[j]], 16)
                self.issued += 2 * (PAIRS - 1)
                for n in range(2):
                    self.load_tile(sp, self.ff2_tile(n), 512)

            @block.tensor
            def _(pe):
                def unit(q, j, i, wait):
                    m, tok = U[i]
                    if wait:
                        pe.wait_ge(kept, q * (2 * NU) + (j * NU + i - 3))
                    for c in range(KC):
                        ins = pe.matmul(ps[:, i % 4, 0:HALF], self.wt[slot[j]][:, c, m * P:(m + 1) * P], self.hT[:, c, tok], start=(c == 0), stop=(c == KC - 1))
                    ins.then_inc(acc, 1)

                for j in range(2):
                    pe.wait_ge(self.w_loaded[slot[j]], loaded[j])
                    for i in range(NU):
                        unit(0, j, i, j or i >= 4)
                with pe.Fori(1, PAIRS) as q:
                    for j in range(2):
                        pe.wait_ge(self.w_loaded[slot[j]], q * 16 + loaded[j])
                        for i in range(NU):
                            unit(q, j, i, True)

            @block.scalar
            def _(act):
                with act.Fori(0, PAIRS) as q:
                    for j in range(2):
                        for i in range(NU):
                            act.wait_ge(acc, q * (2 * NU) + (u0 + j * NU + i + 1))
                            act.activation(positive[:, i % 4, :], ps[:, i % 4, 0:HALF], ACT.Relu).then_inc(relu, 1)

            @block.vector
            def _(dve):
                with dve.Fori(0, PAIRS) as q:
                    for j in range(2):
                        for i, (m, tok) in enumerate(U):
                            dve.wait_ge(relu, q * (2 * NU) + (j * NU + i + 1))
                            dst = fT[:, bass.ds(q * 8 + (4 * j + m), 1), tok].rearrange("p a t -> p (a t)")
                            dve.tensor_tensor(dst, ps[:, i % 4, 0:HALF], positive[:, i % 4, :], ALU.mult).then_inc(kept, 1)
        self.free("hT", "positive")

    def ff2_tile(self, n):
        return self.I["w_ff2"][1024 * (n % 4):1024 * (n % 4) + 1024, 512 * (n // 4):512 * (n // 4) + 512]

    def stage_ff2(self):
        nc, O, ps, fT, h = self.nc, self.O, self.ps, self.fT, self.h
        yT = self.sb("yT", [P, KC, NT])
        kept, turned, summed, stored = (self.sem("ff2_" + x) for x in ("kept", "turned", "summed", "stored"))
        acc, u0, U = self.acc, self.units, self.half_units()
        NU, TILES = len(U), 2 * DFF // 1024
        QUARTERS = DFF // 1024
        for n in range(TILES):
            self.tile_end.append(u0 + NU * (n + 1))
        self.units += NU * TILES
        with nc.Block() as block:
            @block.sync
            def _(sp):
                for n in range(2, TILES):
                    self.load_tile(sp, self.ff2_tile(n), 512)
                for t in range(TT + 1):
                    sp.wait_ge(summed, 2 * (t + 1))
                    dst = O["y_prompt"][0, t * P:(t + 1) * P, :] if t < TT else O["y_sample"][:, 0, :]
                    sp.dma_start(dst, h[0:rows(t), t, :]).then_inc(stored, 16)
                sp.wait_ge(stored, 16 * (TT + 1))

            @block.tensor
            def _(pe):
                for n in range(TILES):
                    w, r = self.tile_ready(pe), n % QUARTERS
                    for i, (m, tok) in enumerate(U):
                        if n == QUARTERS:
                            pe.wait_ge(kept, i + 1)
                        for c in range(KC):
                            ins = pe.matmul(ps[:, i, 0:HALF], w[:, c, m * P:(m + 1) * P], fT[:, KC * r + c, tok],
                                            start=(r == 0 and c == 0), stop=(r == QUARTERS - 1 and c == KC - 1))
                        ins.then_inc(acc, 1)
                for u in range(2 * (TT + 1)):
                    t, half = u // 2, u % 2
                    if u == 0:
                        pe.wait_ge(kept, 2 * NU)
                    if u >= 8:
                        pe.wait_ge(summed, u - 7)
                    for c in range(4):
                        ins = pe.transpose(ps[0:rows(t), u % 8, c * P:(c + 1) * P], yT[:, 4 * half + c, t * P:t * P + rows(t)], self.C("ident"))
                    ins.then_inc(turned, 1)

            @block.scalar
            def _(act):
                for half in range(2):
                    for i, (m, tok) in enumerate(U):
                        act.wait_ge(acc, u0 + (QUARTERS * (half + 1) - 1) * NU + i + 1)
                        act.copy(yT[:, 4 * half + m, tok], ps[:, i, 0:HALF]).then_inc(kept, 1)

            @block.vector
            def _(dve):
                for u in range(2 * (TT + 1)):
                    t, half = u // 2, u % 2
                    hh = h[0:rows(t), t, 512 * half:512 * half + 512]
                    dve.wait_ge(turned, u + 1)
                    dve.tensor_tensor(hh, hh, ps[0:rows(t), u % 8, :], ALU.add).then_inc(summed, 1)
        self.free("yT", "fT", "h")

    def stages(self):
        return [self.stage_compress, self.stage_norms, self.stage_project, self.stage_qk, self.stage_prompt_attention,
                self.stage_sample_attention, self.stage_gdn_project, self.stage_gdn_conv, self.stage_gdn_prompt, self.stage_gdn_sample,
                self.stage_merge, self.stage_out, self.stage_ff1, self.stage_ff2]


_INS = ["x_prompt", "x_sample", "cache_cmp_kv", "cache_sel_kv", "cache_win_kv", "state_gdn", "state_gdn_conv", "cache_mem_kv",
        "page_table", "mem_prompt", "g_mix", "w_in", "nsa_q_norm", "nsa_k_norm", "cmp_pe", "cmp_w1", "cmp_w2", "gdn_conv_w",
        "gdn_A_log", "gdn_dt_bias", "gdn_o_norm", "g_mem", "w_mem_kv", "mem_q_norm", "mem_k_norm", "w_br_nsa", "w_br_gdn",
        "w_br_mem", "w_out", "g_ffn", "w_ff1", "w_ff2"]
_OUTS = [("y_prompt", (1, SEQ, DM)), ("y_sample", (NB, 1, DM)), ("p_cmp", (1, SEQ, 2, NG, HD)), ("p_sel", (1, SEQ, 2, NG, HD)),
         ("p_win", (1, WIN, 2, NG, HD)), ("p_state", (1, GH, GD, GD)), ("p_conv", (1, 3, CONV)), ("p_mem", (1, MT, 2, MH, MD)),
         ("s_cmp", (NB, 1, 2, NG, HD)), ("s_sel", (NB, 1, 2, NG, HD)), ("s_win", (NB, WIN, 2, NG, HD)),
         ("s_state", (NB, GH, GD, GD)), ("s_conv", (NB, 3, CONV))]


def kernel(**inputs):
    from concourse import bacc
    from concourse.bass_utils import run_bass_kernel_spmd

    nc = bacc.Bacc("TRN2", target_bir_lowering=False, num_devices=1)
    arrays, ins = {}, {}
    table, at = shape_constants()
    for name in _INS:
        a = np.ascontiguousarray(inputs[name])
        arrays["in_" + name] = a
        ins[name] = nc.dram_tensor("in_" + name, a.shape, mybir.dt.from_np(a.dtype), kind="ExternalInput").ap()
    arrays["in_table"] = table
    const = nc.dram_tensor("in_table", table.shape, F32, kind="ExternalInput").ap()
    outs = {n: nc.dram_tensor("out_" + n, s, F32, kind="ExternalOutput").ap() for n, s in _OUTS}
    Kernel(nc, ins, outs, (const, at)).build()
    r = run_bass_kernel_spmd(nc, [arrays], core_ids=[0])
    return tuple(r.results[0]["out_" + n] for n, _ in _OUTS)
```

```python
from contextlib import ExitStack

import numpy as np

import concourse.bass as bass
from concourse import mybir

F32 = mybir.dt.float32
I32 = mybir.dt.int32
F32R = mybir.dt.float32r
ALU = mybir.AluOpType
ACT = mybir.ActivationFunctionType
AX = mybir.AxisListType.X

P = 128
DM = 1024
SEQ = 512
NB = 8
NT = SEQ + NB
TT = SEQ // P
HALF = NT // 2
WCOLS = 256
WM = WCOLS // P
KC = DM // P
PAST = 2048
PAGE = 128
PAGES = PAST // PAGE
NH, NG, HD = 8, 2, 64
HPG = NH // NG
CB, CS = 32, 16
NCMP = PAST // CS - 1
PCMP = SEQ // CS - 1
NSEL = PAST // 64 + 1
WIN = 512
GH, GD = 4, 128
MT, MH, MD = 256, 4, 128
CONV = 3 * GH * GD
CC = CONV // P
DFF = 4 * DM
EPS = 1e-6
NEG = -1e30
FORCE = 1e9

C_Q, C_KV, C_GN, C_GDN, C_B, C_A, C_Z, C_QM, C_GB, C_END = (
    0, 512, 1280, 1304, 2840, 2844, 2848, 3360, 3872, 6944)
TOKCOLS = C_GDN + (C_GB - C_B)


VECS = [("nsa_q_norm", HD), ("nsa_k_norm", 3 * HD), ("mem_q_norm", MD), ("mem_k_norm", MD), ("gdn_o_norm", GD),
        ("gdn_A_log", GH), ("gdn_dt_bias", GH)]


def tok_col(c):
    return c if c < C_GDN else c - (C_B - C_GDN)


def rows(t):
    return P if t < TT else NB


def shape_constants():
    parts = {}
    r = np.arange(P)
    parts["ident"] = np.eye(P)
    parts["ones"] = np.ones((P, P))
    parts["upper"] = (r[:, None] <= r[None, :]) * 1.0
    lv = []
    for l in range(7):
        s = 1 << l
        lv.append((r[:, None] // (2 * s) == r[None, :] // (2 * s)) & (r[None, :] // s % 2 == 1) & (r[:, None] // s % 2 == 0))
    parts["levels"] = np.concatenate(lv, 1) * 1.0
    parts["causal"] = np.where(r[None, :] <= r[:, None], 0.0, NEG)
    pos = (np.arange(TT)[None, :] * P + r[:, None])
    blk_end = np.arange(32) * CS + CB - 1
    cm = (blk_end[None, None, :] <= pos[:, :, None]) & (np.arange(32) < PCMP)[None, None, :]
    parts["cmpok"] = cm.reshape(P, -1) * 1.0
    parts["cmpbias"] = np.where(cm, 0.0, NEG).reshape(P, -1)
    half = HD // 2
    inv = np.float32(10000.0) ** (-np.arange(half, dtype=np.float32) / np.float32(half))
    posr = np.concatenate([pos, np.full((P, 1), PAST)], 1).astype(np.float32)
    ang = (posr[:, :, None] * inv[None, None, :]).astype(np.float32)
    cos, sin = np.cos(ang), np.sin(ang)
    parts["cos"] = np.concatenate([cos, cos], 2).reshape(P, -1)
    parts["sin"] = np.concatenate([-sin, sin], 2).reshape(P, -1)
    h = r % 32
    same = (r[:, None] // 32 == r[None, :] // 32) & (h[:, None] // HPG == h[None, :] // HPG) & (h[:, None] < NH) & (h[None, :] < NH)
    parts["group"] = same * 1.0
    i, j = np.arange(P)[:, None], np.arange(NSEL)[None, :]
    parts["cmp2sel"] = ((i * CS < (j + 1) * 64) & (i * CS + CB > j * 64)) * 1.0
    at, off = {}, 0
    for k, v in parts.items():
        at[k] = (off, v.shape[1])
        off += v.shape[1]
    return np.concatenate([np.asarray(v, np.float32) for v in parts.values()], 1), at


class Count:

    def __init__(self, sem):
        self.sem, self.n = sem, 0

    def inc(self, ins, k=1):
        ins.then_inc(self.sem, k)
        self.n += k
        return self.n


class Chain(Count):

    def __init__(self, sem, eng):
        super().__init__(sem)
        self.eng = eng

    def step(self, ins):
        self.inc(ins)
        self.eng.wait_ge(self.sem, self.n)


class Steps:

    def __init__(self, sem, names):
        self.sem, self.names, self.n = sem, names, 0

    def done(self, ins, name, t):
        assert self.names[self.n % len(self.names)] == name and self.n // len(self.names) == t, (name, t, self.n)
        ins.then_inc(self.sem, 1)
        self.n += 1

    def wait(self, eng, name, t):
        if t >= 0:
            eng.wait_ge(self.sem, t * len(self.names) + self.names.index(name) + 1)


class Kernel:
    def __init__(self, nc, I, O, CONST):
        self.nc, self.I, self.O = nc, I, O
        self.stack = ExitStack()
        self.const_dram, self.const_at = CONST

    def sb(self, name, shape):
        n, at = -(-int(np.prod(shape[1:])) // 8) * 8, 0
        for a, b in sorted(self.taken.values()):
            if at + n <= a:
                break
            at = max(at, b)
        assert at + n <= self.words and name not in self.taken, (name, at, n, self.taken)
        self.taken[name] = (at, at + n)
        return self.view(name, shape, F32)

    def view(self, name, shape, dtype):
        self.tensors += 1
        t = self.nc.alloc_sbuf_tensor_at(f"{name}_{self.tensors}", shape, dtype, offset=self.base + 4 * self.taken[name][0])
        return t[tuple(slice(0, n) for n in shape)]

    def sbr(self, name, shape):
        if name not in self.taken:
            self.sb(name, shape)
        return self.view(name, shape, F32R)

    def free(self, *names):
        for n in names:
            del self.taken[n]

    def sem(self, name):
        return self.stack.enter_context(self.nc.semaphore(name))

    def V(self, name):
        c = 0
        for k, n in VECS:
            if k == name:
                return self.vecs[:, c:c + n]
            c += n

    def C(self, name, a=None, b=None):
        off, n = self.const_at[name]
        a, b = a or 0, n if b is None else b
        return self.consts[:, off + a:off + b]

    def build(self):
        nc = self.nc
        with self.stack:
            self.base = -(-nc.sbuf_base // 32) * 32
            self.words = (nc.sbuf_usable_end - self.base) // 4
            self.tensors = 0
            self.taken = {}
            self.ps = self.stack.enter_context(nc.psum_tensor("ps", [P, 8, 512], F32))
            self.consts = self.sb("consts", [P, sum(n for _, n in self.const_at.values())])
            self.gcol = self.sb("gcol", [P, 104])
            self.w_loaded = [self.sem(f"w_loaded{i}") for i in range(2)]
            self.w_high, self.w_split = self.sem("w_high"), self.sem("w_split")
            self.x_split = Count(self.sem("x_split"))
            self.issued, self.splits, self.loaded_at = 0, 0, []
            self.acc = self.sem("acc")
            self.units = 0
            self.tile_end = []
            self.tiles = 0
            self.vecs = self.sb("vecs", [P, sum(n for _, n in VECS)])
            self.vecs_loaded = self.sem("vecs_loaded")
            stages = self.stages()
            for s in stages:
                s()

    def weight_setup(self):
        if "wt0" not in self.taken:
            self.wt = [self.sb(f"wt{i}", [P, KC, WCOLS]) for i in range(2)]
        self.wh = [self.sbr(f"wh{i}", [P, KC, WCOLS]) for i in range(2)]
        self.wl = [self.sbr(f"wl{i}", [P, KC, WCOLS]) for i in range(2)]

    def weight_free(self):
        self.free(*(f"{n}{i}" for n in ("wt", "wh", "wl") for i in range(2)))

    def load_tile(self, sp, srcs, chunks=KC):
        n, at = self.issued, 0
        if n >= 2:
            sp.wait_ge(self.w_split, n - 1)
        for src in srcs:
            w = src.shape[1]
            sp.dma_start(self.wt[n % 2][:, 0:chunks, at:at + w], src.rearrange("(c p) n -> p c n", p=P)).then_inc(self.w_loaded[n % 2], 16)
            at += w
        self.loaded_at.append((self.loaded_at[n - 2] if n >= 2 else 0) + 16 * len(srcs))
        self.issued += 1

    def high_low(self, dve, x, high, low, high_sem, high_count):
        dve.tensor_copy(high, x).then_inc(high_sem, 1)
        dve.wait_ge(high_sem, high_count)
        return dve.tensor_tensor(low, x, high.bitcast(F32), ALU.subtract)

    def split_tile(self, dve, width=WCOLS, chunks=KC):
        n = self.splits
        dve.wait_ge(self.w_loaded[n % 2], self.loaded_at[n])
        if n >= 2:
            dve.wait_ge(self.acc, self.tile_end[n - 2])
        cut = lambda x: x[n % 2][:, 0:chunks, 0:width]
        self.high_low(dve, cut(self.wt), cut(self.wh), cut(self.wl), self.w_high, n + 1).then_inc(self.w_split, 1)
        self.splits += 1

    def tile_ready(self, pe):
        n = self.tiles
        pe.wait_ge(self.w_split, n + 1)
        self.tiles += 1
        return self.wh[n % 2], self.wl[n % 2]

    def split_acts(self, dve, x, high, low):
        self.x_split.n += 1
        ins = self.high_low(dve, x, high, low, self.x_split.sem, self.x_split.n)
        self.x_split.inc(ins)

    def product3(self, pe, out, lhsT, rhs, chunks=KC, first=True, last=True):
        for c in range(chunks):
            for k, (i, j) in enumerate(((0, 0), (0, 1), (1, 0))):
                ins = pe.matmul(out, lhsT(i, c), rhs(j, c),
                                start=(first and c == 0 and k == 0), stop=(last and c == chunks - 1 and k == 2))
        return ins

    def compress_products(self, pe, XT, out, n, waits):
        for v in range(2):
            waits(v)
            for m in range(CB // 2):
                ins = pe.matmul(out(v), self.w1[:, v, m, :], XT[:, 2 * v:2 * v + 2, m:m + 8 * (n - 1) + 1:8],
                                start=(m == 0), stop=(m == CB // 2 - 1))
            ins.then_inc(self.hid_ready, 1)

    def compress_setup(self):
        self.w1 = self.sb("w1", [P, 2, CB // 2, P])
        self.w2 = self.sb("w2", [P, 2, HD])
        self.hbias = self.sb("hbias", [P, 2])

    def stage_compress(self):
        nc, I, ps = self.nc, self.I, self.ps
        self.compress_setup()
        self.weight_setup()
        self.kcT = self.sb("kcT", [P, NB, NCMP + 1])
        self.vc = self.sb("vc", [P, NB, P])
        vrow = self.sb("vrow", [104, P])
        pt = self.sb("pt", [1, NB * PAGES]).bitcast(I32)
        raw = [self.sb(f"raw{i}", [P, PAGES, 2, P]) for i in range(2)]
        XT = [self.sb(f"XT{i}", [P, 4, PAST // 2]) for i in range(2)]
        HT = [self.sb(f"HT{i}", [P, 2, 2, NCMP]) for i in range(2)]
        S = self.sem
        vec_loaded, const_loaded, w1_loaded, pt_loaded = S("vec_loaded"), S("const_loaded"), S("w1_loaded"), S("pt_loaded")
        pages_in = [S("pages_in0"), S("pages_in1")]
        turned, kept = S("k_turned"), [S("k_kept0"), S("k_kept1")]
        gains_turned, gains, bias_sum, bias = S("gains_turned"), S("gains_kept"), S("bias_sum"), S("bias")
        self.hid_ready = S("hid_ready")
        gelu, cmp_ready, cmp_kept = S("gelu"), S("cmp_ready"), S("cmp_kept")
        pool = I["cache_cmp_kv"]
        NPOOL = pool.shape[0]
        TILES = PAGES // 2
        src = pool.rearrange("n r v g d -> n r v (g d)")
        with nc.Block() as block:
            @block.sync
            def _(sp):
                sp.dma_start(pt[:, :], I["page_table"].rearrange("(a b) p -> a (b p)", a=1)).then_inc(pt_loaded, 16)
                sp.dma_start(self.consts[:, :], self.const_dram).then_inc(const_loaded, 16)
                sp.wait_ge(pt_loaded, 16)
                for b in range(NB):
                    if b >= 2:
                        sp.wait_ge(turned, TILES * (b - 1))
                    with sp.Fori(0, PAGES) as p:
                        page = sp.value_load(pt[0:1, bass.ds(p + b * PAGES, 1)], min_val=0, max_val=NPOOL - 1)
                        sp.dma_start(raw[b % 2][:, bass.ds(p, 1)], src[bass.ds(page, 1)]).then_inc(pages_in[b % 2], 16)
                for n in range(2):
                    self.load_tile(sp, [I["w_mem_kv"][:, WCOLS * n:WCOLS * n + WCOLS]])


            @block.tensor
            def _(pe):
                pe.wait_ge(const_loaded, 16)
                pe.wait_ge(vec_loaded, 80)
                pe.transpose(ps[:, 7, 0:104], vrow[:, :], self.C("ident")[0:104, 0:104]).then_inc(gains_turned, 1)
                pe.wait_ge(w1_loaded, 80)
                pe.wait_ge(gains, 1)
                for v in range(2):
                    for m in range(CB // 2):
                        ins = pe.matmul(ps[:, 6, v:v + 1], self.w1[:, v, m, :], self.gcol[:, 72 + 16 * v + m:73 + 16 * v + m],
                                        start=(m == 0), stop=(m == CB // 2 - 1))
                ins.then_inc(bias_sum, 1)

                def turn(b):
                    pe.wait_ge(pages_in[b % 2], 16 * PAGES * (b // 2 + 1))
                    for q in range(TILES):
                        u = b * TILES + q
                        if u >= 4:
                            pe.wait_ge(kept[0], u - 3)
                            pe.wait_ge(kept[1], u - 3)
                        for c in range(4):
                            ins = pe.transpose(ps[:, u % 4, c * P:(c + 1) * P], raw[b % 2][:, 2 * q + c // 2, c % 2, :], self.C("ident"))
                        ins.then_inc(turned, 1)

                def hidden(b):
                    def waits(v):
                        if v == 0:
                            for k in range(2):
                                pe.wait_ge(kept[k], TILES * (b + 1))
                        if b:
                            pe.wait_ge(gelu, 2 * (b - 1) + v + 1)
                    self.compress_products(pe, XT[b % 2], lambda v: ps[:, 4 + v, 0:2 * NCMP], NCMP, waits)

                def small(b):
                    pe.wait_ge(gelu, 2 * b + 2)
                    if b:
                        pe.wait_ge(cmp_kept, 2 * b)
                    for g in range(NG):
                        pe.matmul(ps[g * HD:(g + 1) * HD, 6, 0:NCMP], self.w2[:, 0, :], HT[b % 2][:, 0, g, :], start=True, stop=True)
                    for g in range(NG):
                        ins = pe.matmul(ps[0:NCMP, 7, g * HD:(g + 1) * HD], HT[b % 2][:, 1, g, :], self.w2[:, 1, :], start=True, stop=True)
                    ins.then_inc(cmp_ready, 1)

                turn(0)
                pe.wait_ge(bias, 1)
                for b in range(NB):
                    if b + 1 < NB:
                        turn(b + 1)
                    hidden(b)
                    if b:
                        small(b - 1)
                small(NB - 1)

            def copy_unit(eng, copy, b, q, g):
                eng.wait_ge(turned, b * TILES + q + 1)
                if b >= 2:
                    eng.wait_ge(self.hid_ready, 2 * (b - 1))
                bank = ps[g * HD:(g + 1) * HD, (b * TILES + q) % 4, :].rearrange("p (c v t e) -> p c v t e", c=2, v=2, e=2)
                for e in range(2):
                    dst = XT[b % 2].rearrange("p (v g) t -> p v g t", v=2)[e * HD:(e + 1) * HD, :, g, q * P:(q + 1) * P]
                    ins = copy(dst.rearrange("p v (c t) -> p c v t", c=2), bank[:, :, :, :, e])
                ins.then_inc(kept[g], 1)

            @block.scalar
            def _(act):
                r = 0
                for name, pat, n in (("g_mix", "(c p) -> c p", 8), ("g_mem", "(c p) -> c p", 8), ("g_ffn", "(c p) -> c p", 8),
                                     ("gdn_conv_w", "j (c p) -> (j c) p", 48), ("cmp_pe", "v (m e) d -> (v m) (e d)", 32)):
                    kw = {"e": 2} if name == "cmp_pe" else {"p": P}
                    act.dma_start(vrow[r:r + n, :], I[name].rearrange(pat, **kw)).then_inc(vec_loaded, 16)
                    r += n
                for v in range(2):
                    for h in range(2):
                        act.dma_start(self.w1[:, v, 8 * h:8 * h + 8, :], I["cmp_w1"].rearrange("v (m p) f -> v p m f", p=P)[v, :, 8 * h:8 * h + 8]).then_inc(w1_loaded, 16)
                act.dma_start(self.w2[:, :, :], I["cmp_w2"].rearrange("v f d -> f v d")).then_inc(w1_loaded, 16)
                c = 0
                for name, n in VECS:
                    v = I[name]
                    v = v.rearrange("a b -> (a b)") if len(v.shape) > 1 else v
                    act.dma_start(self.vecs[:, c:c + n], v.partition_broadcast(P)).then_inc(self.vecs_loaded, 16)
                    c += n
                for b in range(NB + 1):
                    if b < NB:
                        for q in range(TILES):
                            copy_unit(act, act.copy, b, q, 1)
                    if b == 0:
                        act.wait_ge(bias, 1)
                    if b:
                        for v in range(2):
                            act.wait_ge(self.hid_ready, 2 * (b - 1) + v + 1)
                            if b > 2 and v == 0:
                                act.wait_ge(cmp_ready, b - 2)
                            act.activation(HT[(b - 1) % 2][:, v, :, :], ps[:, 4 + v, 0:2 * NCMP].rearrange("p (g n) -> p g n", g=2),
                                           ACT.Gelu_apprx_tanh, bias=self.hbias[:, v:v + 1]).then_inc(gelu, 1)

            @block.vector
            def _(dve):
                dve.wait_ge(gains_turned, 1)
                dve.tensor_copy(self.gcol[:, :], ps[:, 7, 0:104]).then_inc(gains, 1)
                dve.wait_ge(bias_sum, 1)
                dve.tensor_copy(self.hbias[:, :], ps[:, 6, 0:2]).then_inc(bias, 1)
                for b in range(NB + 2):
                    if b < NB:
                        for q in range(TILES):
                            copy_unit(dve, dve.tensor_copy, b, q, 0)
                    if b >= 2:
                        dve.wait_ge(cmp_ready, b - 1)
                        dve.tensor_copy(self.kcT[:, b - 2, 0:NCMP], ps[:, 6, 0:NCMP]).then_inc(cmp_kept, 1)
                        dve.tensor_copy(self.vc[0:NCMP, b - 2, :], ps[0:NCMP, 7, 0:P]).then_inc(cmp_kept, 1)
        self.free("vrow", "pt", "raw0", "raw1", "XT0", "XT1", "HT0", "HT1", "w1", "w2", "hbias")

    def stage_norms(self):
        nc, I, ps = self.nc, self.I, self.ps
        self.uT = self.sb("uT", [P, KC, NT])
        self.memT = self.sb("memT", [P, KC, MT])
        self.uH, self.memH = self.sbr("uH", [P, KC, NT]), self.sbr("memH", [P, KC, MT])
        self.uL, self.memL = self.sbr("uT", [P, KC, NT]), self.sbr("memT", [P, KC, MT])
        mem_tok = self.sb("mem_tok", [P, 2, DM])
        x_tok = self.sb("x_tok", [P, TT + 1, DM])
        x_loaded = [self.sem(f"x_loaded{i}") for i in range(3)]
        self.norm_stage_setup("a")
        srcs = [(x_tok[0:rows(t), t, :], rows(t), self.uT[:, :, t * P:t * P + rows(t)], 0) for t in range(TT + 1)]
        srcs += [(mem_tok[:, t, :], P, self.memT[:, :, t * P:(t + 1) * P], 8) for t in range(2)]
        with nc.Block() as block:
            @block.sync
            def _(sp):
                sp.dma_start(x_tok[:, 0:TT, :], I["x_prompt"][0].rearrange("(t p) d -> p t d", p=P)).then_inc(x_loaded[0], 16)
                sp.dma_start(x_tok[0:NB, TT, :], I["x_sample"][:, 0, :]).then_inc(x_loaded[1], 16)
                sp.dma_start(mem_tok[:, :, :], I["mem_prompt"][0].rearrange("(t p) d -> p t d", p=P)).then_inc(x_loaded[2], 16)

            @block.scalar
            def _(act):
                self.norm_act(act, srcs, {0: (x_loaded[0], 16), 4: (x_loaded[1], 16), 5: (x_loaded[2], 16)})

            @block.tensor
            def _(pe):
                self.norm_pe(pe, srcs)

            @block.vector
            def _(dve):
                self.norm_dve(dve, srcs, [[x[:, :, t * P:t * P + rows(t)] for x in (self.uH, self.uL)] for t in range(TT + 1)]
                              + [[x[:, :, t * P:(t + 1) * P] for x in (self.memH, self.memL)] for t in range(2)])
        self.free("ss", "xn0", "xn1", "nj", "x_tok", "mem_tok")

    def norm_stage_setup(self, tag):
        n = dict(ss=self.sb("ss", [P, 8]), xn=[self.sb(f"xn{i}", [P, DM]) for i in range(2)],
                 junk=self.sb("nj", [P, DM]),
                 squares=self.sem("squares" + tag), mean=self.sem("mean" + tag), root=self.sem("root" + tag),
                 rstd=self.sem("rstd" + tag), scaled=self.sem("scaled" + tag), turned=self.sem("turned" + tag), kept=self.sem("kept" + tag))
        self.n = n
        return n

    def norm_act(self, act, srcs, waits):
        n = self.n
        for i, (src, R, _, _) in enumerate(srcs):
            if i in waits:
                act.wait_ge(*waits[i])
            if i:
                act.wait_ge(n["squares"], i)
            else:
                act.wait_ge(n["mean"], 1)
            act.activation(n["junk"][0:R, :], src, ACT.Square, accum_out=n["ss"][0:R, i:i + 1]).then_inc(n["squares"], 1)
        act.wait_ge(n["mean"], 2)
        act.activation(n["ss"][:, :], n["ss"][:, :], ACT.Sqrt).then_inc(n["root"], 1)

    def norm_dve(self, dve, srcs, parts):
        n, ps = self.n, self.ps
        dve.memset(n["ss"][:, :], 1.0).then_inc(n["mean"], 1)
        dve.wait_ge(n["squares"], len(srcs))
        dve.tensor_scalar(n["ss"][:, :], n["ss"][:, :], 1.0 / DM, EPS, ALU.mult, ALU.add).then_inc(n["mean"], 1)
        dve.wait_ge(n["root"], 1)
        dve.reciprocal(n["ss"][:, :], n["ss"][:, :]).then_inc(n["rstd"], 1)
        dve.wait_ge(n["rstd"], 1)
        for i in range(len(srcs) + 1):
            if i < len(srcs):
                src, R, _, _ = srcs[i]
                if i >= 2:
                    dve.wait_ge(n["turned"], 2 * (i - 1))
                dve.tensor_scalar(n["xn"][i % 2][0:R, :], src, n["ss"][0:R, i:i + 1], None, ALU.mult).then_inc(n["scaled"], 1)
            if i:
                _, R, dst, g = srcs[i - 1]
                for h in range(2):
                    dve.wait_ge(n["turned"], 2 * (i - 1) + h + 1)
                    b = (2 * (i - 1) + h) % 4
                    dve.tensor_tensor(dst[:, 4 * h:4 * h + 4, :], ps[:, b, :].rearrange("p (c t) -> p c t", c=4)[:, :, 0:R],
                                      self.gcol[:, g + 4 * h:g + 4 * h + 4].unsqueeze(2).broadcast_to([P, 4, R]), ALU.mult).then_inc(n["kept"], 1)
                dve.wait_ge(n["kept"], 2 * i)
                self.split_acts(dve, dst, *parts[i - 1])

    def norm_pe(self, pe, srcs):
        n, ps = self.n, self.ps
        for i, (_, R, _, _) in enumerate(srcs):
            pe.wait_ge(n["scaled"], i + 1)
            for h in range(2):
                u = 2 * i + h
                if u >= 4:
                    pe.wait_ge(n["kept"], u - 3)
                for c in range(4):
                    ins = pe.transpose(ps[:, u % 4, c * P:c * P + R], n["xn"][i % 2][0:R, (4 * h + c) * P:(4 * h + c + 1) * P],
                                       self.C("ident")[0:R, 0:R])
                ins.then_inc(n["turned"], 1)

    def dense(self, tag, tiles, units, loads, before=None):
        nc, ps = self.nc, self.ps
        acc, u0, kept = self.acc, self.units, [self.sem(tag + "_kept0"), self.sem(tag + "_kept1")]
        for n in range(len(tiles)):
            self.tile_end.append(u0 + 1 + max(u for u, x in enumerate(units) if x[0] == n))
        self.units += len(units)
        with nc.Block() as block:
            @block.sync
            def _(sp):
                for srcs in loads:
                    self.load_tile(sp, srcs)

            @block.tensor
            def _(pe):
                if before:
                    pe.wait_ge(self.x_split.sem, self.x_split.n + 2 * before[1])
                last = -1
                for u, (n, lhsT, rhs, R, N, _) in enumerate(units):
                    if n != last:
                        w = self.tile_ready(pe)
                        last = n
                    if u >= 4:
                        pe.wait_ge(kept[u % 2], (u - 4) // 2 + 1)
                    self.product3(pe, ps[0:R, u % 4, 0:N], lambda i, c: lhsT(w, i, c), lambda i, c: rhs(w, i, c)).then_inc(acc, 1)

            @block.scalar
            def _(act):
                for u, (_, _, _, R, N, dst) in enumerate(units):
                    if u % 2 == 0:
                        act.wait_ge(acc, u0 + u + 1)
                        act.copy(dst, ps[0:R, u % 4, 0:N]).then_inc(kept[0], 1)

            @block.vector
            def _(dve):
                if before:
                    before[0](dve)
                width = lambda n: sum(x.shape[1] for x in tiles[n])
                self.split_tile(dve, width(0))
                last = -1
                for u, (n, _, _, R, N, dst) in enumerate(units):
                    if n != last and n + 1 < len(tiles):
                        self.split_tile(dve, width(n + 1))
                    last = n
                    if u % 2:
                        dve.wait_ge(acc, u0 + u + 1)
                        dve.tensor_copy(dst, ps[0:R, u % 4, 0:N]).then_inc(kept[1], 1)

    def stage_project(self):
        I = self.I
        self.mem_kv = self.sb("mem_kv", [P, 2, 2 * MH * MD])
        self.proj = self.sb("proj", [P, TT + 1, TOKCOLS])
        units = []
        tiles = []
        W = WCOLS
        U, M = (self.uH, self.uL), (self.memH, self.memL)
        for n in range(2 * MH * MD // W):
            tiles.append([I["w_mem_kv"][:, W * n:W * n + W]])
            for t in range(2):
                units.append((n, lambda w, i, c, t=t: M[i][:, c, t * P:(t + 1) * P], lambda w, i, c: w[i][:, c, :], P, W,
                              self.mem_kv[:, t, W * n:W * n + W]))
        w_in = I["w_in"]
        assert C_GN % W == 0 and (C_GB - C_Z) % W == 0
        parts = [[w_in[:, a:a + W]] for a in range(0, C_GN, W)]
        at = [a for a in range(0, C_GN, W)]
        parts.append([w_in[:, C_GN:C_GDN], w_in[:, C_B:C_Z]])
        at.append(C_GN)
        for a in range(C_Z, C_GB, W):
            parts.append([w_in[:, a:a + W]])
            at.append(tok_col(a))
        for srcs, a in zip(parts, at):
            n = sum(x.shape[1] for x in srcs)
            tiles.append(srcs)
            for t in range(TT + 1):
                R = rows(t)
                units.append((len(tiles) - 1, lambda w, i, c, t=t, R=R: U[i][:, c, t * P:t * P + R], lambda w, i, c, n=n: w[i][:, c, 0:n], R, n,
                              self.proj[0:R, t, a:a + n]))
        self.dense("proj", tiles, units, tiles[2:])
        self.free("memT", "memH")
        self.weight_free()

    def stage_qk(self):
        nc, I, O, ps, proj = self.nc, self.I, self.O, self.ps, self.proj
        NK = 3 * NG
        self.qT = self.sb("qT", [P, 4, NT])
        self.kT = self.sb("kT", [P, 2 * NG, NT])
        self.qmT = self.sb("qmT", [P, MH, NT])
        self.kmT = self.sb("kmT", [P, MH, MT])
        self.qblk = self.sb("qblk", [P, NB, 32])
        self.qmpad = self.sb("qmpad", [P, NB, MH, 32])
        self.knT = self.sb("knT", [P, 2, NB])
        self.vnew = self.sb("vnew", [1, 2, NB, NG * HD])
        sq = self.sb("sq", [P, 2, (NH + NK) * HD + MH * MD])
        tmp = self.sb("ropetmp", [P, (NH + NK) * HD])
        qbd = self.sb("qbd", [NB, NH, P])
        NS = NH + NK + MH
        ss = self.sb("ssq", [P, TT + 3, NS])
        squared, summed, roots, chain = self.sem("c_squared"), self.sem("c_summed"), self.sem("c_roots"), self.sem("c_chain")
        turned, kept, stored, moved, zeroed = (self.sem("c_" + x) for x in ("turned", "kept", "stored", "moved", "zeroed"))
        kv3 = proj[:, :, C_KV:C_KV + 768].rearrange("p t (b v n) -> p t b v n", b=3, v=2)
        zm = tok_col(C_QM)
        joined = self.sem("c_joined")
        self.compress_setup()
        w_loaded = self.w1_loaded = self.sem("d_w")
        ready = {}


        def k_in(t, R):
            return kv3[0:R, t, :, 0, :]

        with nc.Block() as block:
            @block.gpsimd
            def _(pool):
                pool.memset(self.qblk[:, :, :], 0.0).then_inc(zeroed, 1)
                pool.memset(self.qmpad[:, :, :, :], 0.0).then_inc(zeroed, 1)
                pool.memset(qbd[:, :, :], 0.0).then_inc(zeroed, 1)
                pool.tensor_tensor(self.uT[:, :, :], self.uL.bitcast(F32), self.uH.bitcast(F32), ALU.add).then_inc(joined, 1)
                pool.wait_ge(joined, 1)

            @block.vector
            def _(dve):
                ch = Chain(chain, dve)
                ch.step(dve.memset(ss[:, :, :], 1.0))
                for i in range(TT + 3):
                    dve.wait_ge(squared, 3 * (i + 1) if i <= TT else 3 * (TT + 1) + i - TT)
                    R = rows(i) if i <= TT else P
                    if i <= TT:
                        dve.tensor_reduce(ss[0:R, i, 0:NH + NK], sq[0:R, i % 2, 0:(NH + NK) * HD].rearrange("p (h d) -> p h d", d=HD), AX, ALU.add)
                    dve.tensor_reduce(ss[0:R, i, NH + NK:NS], sq[0:R, i % 2, (NH + NK) * HD:].rearrange("p (h d) -> p h d", d=MD), AX, ALU.add).then_inc(summed, 1)
                dve.wait_ge(summed, TT + 3)
                ch.step(dve.tensor_scalar(ss[:, :, 0:NH + NK], ss[:, :, 0:NH + NK], 1.0 / HD, EPS, ALU.mult, ALU.add))
                ch.step(dve.tensor_scalar(ss[:, :, NH + NK:NS], ss[:, :, NH + NK:NS], 1.0 / MD, EPS, ALU.mult, ALU.add))
                dve.wait_ge(roots, 1)
                ch.step(dve.reciprocal(ss[:, :, :], ss[:, :, :]))
                dve.wait_ge(self.vecs_loaded, 16 * len(VECS))
                ch.step(dve.tensor_scalar(self.V("nsa_q_norm"), self.V("nsa_q_norm"), float(HD) ** -0.5, None, ALU.mult))
                ch.step(dve.tensor_scalar(self.V("mem_q_norm"), self.V("mem_q_norm"), float(MD) ** -0.5, None, ALU.mult))

                def together(*ins):
                    for x in ins:
                        ch.inc(x)
                    dve.wait_ge(chain, ch.n)

                for t in range(2):
                    r = ss[:, TT + 1 + t, NH + NK:NS].unsqueeze(2).broadcast_to([P, MH, MD])
                    o = self.mem_kv[:, t, 0:MH * MD].rearrange("p (h d) -> p h d", d=MD)
                    ch.step(dve.tensor_tensor(o, o, r, ALU.mult))
                    ch.step(dve.tensor_tensor(o, o, self.V("mem_k_norm").unsqueeze(1).broadcast_to([P, MH, MD]), ALU.mult))
                    ready["mem", t] = ch.n
                for t in range(TT + 1):
                    R, H = rows(t), HD // 2
                    r = ss[0:R, t, :]
                    q = proj[0:R, t, 0:NH * HD].rearrange("p (h d) -> p h d", d=HD)
                    k = k_in(t, R).rearrange("p b (g d) -> p b g d", d=HD)
                    m = proj[0:R, t, zm:zm + MH * MD].rearrange("p (h d) -> p h d", d=MD)
                    together(dve.tensor_tensor(q, q, r[:, 0:NH].unsqueeze(2).broadcast_to([R, NH, HD]), ALU.mult),
                             dve.tensor_tensor(k, k, r[:, NH:NH + NK].rearrange("p (b g) -> p b g", b=3).unsqueeze(3).broadcast_to([R, 3, NG, HD]), ALU.mult),
                             dve.tensor_tensor(m, m, r[:, NH + NK:NS].unsqueeze(2).broadcast_to([R, MH, MD]), ALU.mult))
                    together(dve.tensor_tensor(q, q, self.V("nsa_q_norm")[0:R].unsqueeze(1).broadcast_to([R, NH, HD]), ALU.mult),
                             dve.tensor_tensor(k, k, self.V("nsa_k_norm")[0:R].rearrange("p (b d) -> p b d", b=3).unsqueeze(2).broadcast_to([R, 3, NG, HD]), ALU.mult),
                             dve.tensor_tensor(m, m, self.V("mem_q_norm")[0:R].unsqueeze(1).broadcast_to([R, MH, MD]), ALU.mult))
                    cos, sin = self.C("cos")[0:R, t * HD:(t + 1) * HD], self.C("sin")[0:R, t * HD:(t + 1) * HD]
                    yq = tmp[0:R, 0:NH * HD].rearrange("p (h d) -> p h d", d=HD)
                    yk = tmp[0:R, NH * HD:].rearrange("p (b g d) -> p b g d", b=3, g=NG)
                    bq = lambda a: a.unsqueeze(1).broadcast_to([R, NH, a.shape[1]])
                    bk = lambda a: a.unsqueeze(1).unsqueeze(1).broadcast_to([R, 3, NG, a.shape[1]])
                    together(dve.tensor_tensor(yq[:, :, 0:H], q[:, :, H:HD], bq(sin[:, 0:H]), ALU.mult),
                             dve.tensor_tensor(yq[:, :, H:HD], q[:, :, 0:H], bq(sin[:, H:HD]), ALU.mult),
                             dve.tensor_tensor(yk[:, :, :, 0:H], k[:, :, :, H:HD], bk(sin[:, 0:H]), ALU.mult),
                             dve.tensor_tensor(yk[:, :, :, H:HD], k[:, :, :, 0:H], bk(sin[:, H:HD]), ALU.mult))
                    together(dve.tensor_tensor(q, q, bq(cos), ALU.mult), dve.tensor_tensor(k, k, bk(cos), ALU.mult))
                    together(dve.tensor_tensor(q, q, yq, ALU.add), dve.tensor_tensor(k, k, yk, ALU.add))
                    ready[t] = ch.n
                dve.wait_ge(zeroed, 3)
                for g in range(NG):
                    ch.step(dve.tensor_copy(qbd[:, HPG * g:HPG * g + HPG, g * HD:(g + 1) * HD],
                                            proj[0:NB, TT, g * HPG * HD:(g + 1) * HPG * HD].rearrange("p (h d) -> p h d", d=HD)))
                ready["blk"] = ch.n

            ident, banks = self.C("ident"), []
            for t in range(2):
                banks.append(([self.mem_kv[:, t, h * P:(h + 1) * P] for h in range(4)], P, self.kmT[:, :, t * P:(t + 1) * P], ready["mem", t]))
            for t in range(TT + 1):
                R = rows(t)
                s = slice(t * P, t * P + R)
                banks.append(([proj[0:R, t, c * P:(c + 1) * P] for c in range(4)], R, self.qT[:, :, s], ready[t]))
                banks.append(([k_in(t, R)[:, 1 + i, :] for i in range(2)], R, (s, "both halves"), ready[t]))
                banks.append(([proj[0:R, t, zm + c * P:zm + (c + 1) * P] for c in range(4)], R, self.qmT[:, :, s], ready[t]))
            NBK = len(banks)

            @block.tensor
            def _(pe):
                for u, (blocks, R, _, n) in enumerate(banks):
                    pe.wait_ge(chain, n)
                    if u >= 4:
                        pe.wait_ge(kept, u - 3)
                    for c, b in enumerate(blocks):
                        ins = pe.transpose(ps[:, u % 4, c * P:c * P + R], b, ident[0:R, 0:R])
                    ins.then_inc(turned, 1)
                pe.wait_ge(chain, ready["blk"])
                for h in range(NH):
                    pe.transpose(ps[:, 4, h * NB:(h + 1) * NB], qbd[:, h, :], ident[0:NB, 0:NB])
                for i in range(2):
                    ins = pe.transpose(ps[:, 4, (NH + i) * NB:(NH + i + 1) * NB], k_in(TT, NB)[:, i + 1, :], ident[0:NB, 0:NB])
                ins.then_inc(turned, 1)

            @block.scalar
            def _(act):
                for i in range(TT + 3):
                    if i >= 2:
                        act.wait_ge(summed, i - 1)
                    elif i == 0:
                        act.wait_ge(chain, 1)
                    w = (NH + NK) * HD
                    if i <= TT:
                        R = rows(i)
                        act.activation(sq[0:R, i % 2, 0:NH * HD], proj[0:R, i, 0:NH * HD], ACT.Square).then_inc(squared, 1)
                        act.activation(sq[0:R, i % 2, NH * HD:w].rearrange("p (b n) -> p b n", b=3), k_in(i, R), ACT.Square).then_inc(squared, 1)
                        act.activation(sq[0:R, i % 2, w:], proj[0:R, i, zm:zm + MH * MD], ACT.Square).then_inc(squared, 1)
                    else:
                        act.activation(sq[:, i % 2, w:], self.mem_kv[:, i - TT - 1, 0:MH * MD], ACT.Square).then_inc(squared, 1)
                act.wait_ge(chain, 3)
                act.activation(ss[:, :, :], ss[:, :, :], ACT.Sqrt).then_inc(roots, 1)
                for u, (_, R, dst, _) in enumerate(banks):
                    act.wait_ge(turned, u + 1)
                    if type(dst) is tuple:
                        for g in range(NG):
                            for half in range(2):
                                ins = act.copy(self.kT.rearrange("p (b g) t -> p b g t", g=NG)[half * HD:half * HD + HD, :, g, dst[0]],
                                               ps[g * HD:g * HD + HD, u % 4, 0:2 * P].rearrange("p (c t) -> p c t", c=2)[:, :, 0:R])
                        ins.then_inc(kept, 1)
                        continue
                    act.copy(dst, ps[:, u % 4, :].rearrange("p (c t) -> p c t", c=4)[:, :, 0:R]).then_inc(kept, 1)
                act.wait_ge(turned, NBK + 1)
                act.wait_ge(zeroed, 3)
                act.copy(self.qblk[:, :, 0:NH].rearrange("p b h -> p h b"), ps[:, 4, 0:NH * NB].rearrange("p (h b) -> p h b", h=NH)).then_inc(kept, 1)
                act.copy(self.knT[:, :, :], ps[:, 4, NH * NB:(NH + 2) * NB].rearrange("p (h b) -> p h b", h=2)).then_inc(kept, 1)
                act.wait_ge(kept, NBK)
                act.copy(self.qmpad.rearrange("p b h c -> p b (h c)")[:, :, 0:P:33], self.qmT[:, :, SEQ:NT].rearrange("p h b -> p b h")).then_inc(kept, 1)

            @block.sync
            def _(sp):
                for v in range(2):
                    for h in range(2):
                        sp.dma_start(self.w1[:, v, 8 * h:8 * h + 8, :], I["cmp_w1"].rearrange("v (m p) f -> v p m f", p=P)[v, :, 8 * h:8 * h + 8]).then_inc(w_loaded, 16)
                sp.dma_start(self.w2[:, :, :], I["cmp_w2"].rearrange("v f d -> f v d")).then_inc(w_loaded, 16)
                for i in range(2):
                    sp.dma_start(self.vnew[:, i], proj[0:NB, TT, C_KV + 256 * (i + 1) + P:C_KV + 256 * (i + 2)]).then_inc(moved, 16)
                sp.dma_start(O["s_win"][:, 0:WIN - 1], I["cache_win_kv"][:, 1:WIN]).then_inc(stored, 16)
                sp.wait_ge(chain, ready["mem", 1])
                sp.dma_start(O["p_mem"][0].rearrange("(t p) v h d -> p t (v h d)", p=P), self.mem_kv[:, :, :]).then_inc(stored, 16)
                sp.wait_ge(chain, ready[TT])
                for i, name in enumerate(("cmp", "sel", "win")):
                    c = C_KV + 256 * i
                    sp.dma_start(O["p_" + name][0].rearrange("(t p) v g d -> p t (v g d)", p=P), proj[:, 0:TT, c:c + 256]).then_inc(stored, 16)
                    sp.dma_start(O["s_" + name][:, WIN - 1 if name == "win" else 0].rearrange("b v g d -> b (v g d)"), proj[0:NB, TT, c:c + 256]).then_inc(stored, 16)
                sp.wait_ge(stored, 16 * 8)
                sp.wait_ge(moved, 32)
        self.free("sq", "ropetmp", "qbd", "ssq", "uH")

    def stage_prompt_attention(self):
        assert SEQ // 64 <= 16 and SEQ <= WIN
        nc, I, ps, proj = self.nc, self.I, self.ps, self.proj
        self.pt = self.sb("pt", [1, NB * PAGES]).bitcast(I32)
        self.slots = {j: self.sb(f"slot{j}", [P, PAGES * 256]) for j in (0, 2)}
        self.pt_loaded, self.filled = self.sem("e_pt"), [self.sem(f"e_slot{j}") for j in range(4)]
        XT, HT = self.sb("XT", [P, 4, SEQ // 2]), self.sb("HT", [P, 2, 2, PCMP])
        kc = self.sb("kcp", [P, NG, 32])
        vc = self.sb("vcp", [32, P])
        self.gate = self.sb("gate", [P, TT + 1, 3 * NH])
        sc, cs = self.sb("sc", [P, NH, 32]), self.sb("cs", [P, 2, NH])
        PTc = self.sb("PTc", [32, NH, P])
        Pb, PTb = [self.sb(f"Pb{i}", [P, SEQ]) for i in range(2)], [self.sb(f"PTb{i}", [P, SEQ]) for i in range(2)]
        nm, rs, rg = self.sb("nm", [P, 2]), self.sb("rs", [P, 4]), self.sb("rg", [P, 2])
        S = self.sem
        w_loaded = self.w1_loaded
        turned, kept, gelu, small_ready, small_kept = (S("d_" + x) for x in ("turned", "kept", "gelu", "small", "smallkept"))
        kept2, gates, zeroed = S("d_kept2"), S("d_gates"), S("d_zeroed")
        c_s, c_max, c_exp, c_p, c_t, c_tk, c_o, c_chain = (S("dc_" + x) for x in ("s", "max", "exp", "p", "t", "tk", "o", "chain"))
        s_ready, nmax, p_ready, pt_ready, pt_kept, o_ready, o_done, v_chain = (S("u_" + x) for x in (
            "scores", "max", "exp", "turned", "kept", "out", "done", "chain"))
        hid0 = 2 * NB
        ident = self.C("ident")

        units = []
        for qt in range(TT):
            q = slice(qt * P, (qt + 1) * P)
            for h in range(NH):
                g, lo = h // HPG, h % 2 * HD
                for br in range(2):
                    vcol = C_KV + 256 * (br + 1) + P + g * HD
                    units.append(dict(
                        q=self.qT[lo:lo + HD, h // 2, q], k=self.kT[lo:lo + HD, br * NG + g, 0:(qt + 1) * P], n=qt + 1, causal=True,
                        v=[proj[:, t, vcol:vcol + HD] for t in range(qt + 1)], N=HD, gate=self.gate[:, qt, 3 * h + 1 + br:3 * h + 2 + br],
                        dst=proj[:, qt, h * HD:(h + 1) * HD]))
            for h in range(MH):
                c = tok_col(C_QM) + h * MD
                units.append(dict(q=self.qmT[:, h, q], k=self.kmT[:, h, :], n=MT // P, causal=False,
                                  v=[self.mem_kv[:, t, MH * MD + h * MD:MH * MD + (h + 1) * MD] for t in range(MT // P)], N=MD, gate=None,
                                  dst=proj[:, qt, c:c + MD]))
        NU = len(units)

        with nc.Block() as block:
            @block.sync
            def _(sp):
                sp.dma_start(self.pt[:, :], I["page_table"].rearrange("(a b) p -> a (b p)", a=1)).then_inc(self.pt_loaded, 16)
                sp.wait_ge(self.pt_loaded, 16)
                for j in (0, 2):
                    self.load_pages(sp, j, j)

            @block.gpsimd
            def _(pool):
                pool.memset(kc[:, :, :], 0.0).then_inc(zeroed, 1)
                pool.memset(vc[:, :], 0.0).then_inc(zeroed, 1)

            @block.tensor
            def _(pe):
                for q in range(2):
                    for c in range(4):
                        a = C_KV + c % 2 * P
                        ins = pe.transpose(ps[:, q, c * P:(c + 1) * P], proj[:, 2 * q + c // 2, a:a + P], ident)
                    ins.then_inc(turned, 1)
                pe.wait_ge(w_loaded, 80)
                for v in range(2):
                    for m in range(CB // 2):
                        ins = pe.matmul(ps[:, 2, v:v + 1], self.w1[:, v, m, :], self.gcol[:, 72 + 16 * v + m:73 + 16 * v + m],
                                        start=(m == 0), stop=(m == CB // 2 - 1))
                ins.then_inc(turned, 1)
                pe.wait_ge(kept, 4)
                self.compress_products(pe, XT, lambda v: ps[:, 4 + v, 0:2 * PCMP], PCMP, lambda v: None)
                pe.wait_ge(gelu, 2)
                for g in range(NG):
                    for half in range(2):
                        pe.matmul(ps[half * HD:half * HD + HD, 3, g * 32:g * 32 + PCMP], self.w2[:, 0, :], HT[:, 0, g, :], start=True, stop=True)
                for g in range(NG):
                    ins = pe.matmul(ps[0:PCMP, 2, g * HD:(g + 1) * HD], HT[:, 1, g, :], self.w2[:, 1, :], start=True, stop=True)
                ins.then_inc(small_ready, 1)
                pe.wait_ge(small_kept, 2)
                for qt in range(TT):
                    if qt:
                        pe.wait_ge(c_p, qt)
                    for h in range(NH):
                        lo = h % 2 * HD
                        ins = pe.matmul(ps[:, 5 + h % 2, h // 2 * 32:(h // 2 + 1) * 32], self.qT[lo:lo + HD, h // 2, qt * P:(qt + 1) * P],
                                        kc[lo:lo + HD, h // HPG, :], start=True, stop=True)
                    ins.then_inc(c_s, 1)
                    pe.wait_ge(c_p, qt + 1)
                    for h in range(NH):
                        if h == 0 and qt:
                            pe.wait_ge(c_tk, 2 * qt)
                        ins = pe.transpose(ps[0:32, h // HPG, h % HPG * P:(h % HPG + 1) * P], sc[:, h % 2 * HPG + h // 2, :], ident)
                        if h % HPG == HPG - 1:
                            ins.then_inc(c_t, 1)
                    pe.wait_ge(c_tk, 2 * qt + 2)
                    if qt:
                        pe.wait_ge(o_done, qt)
                    for h in range(NH):
                        g = h // HPG
                        ins = pe.matmul(ps[:, 7, h * HD:(h + 1) * HD], PTc[:, h, :], vc[:, g * HD:(g + 1) * HD], start=True, stop=True)
                    ins.then_inc(c_o, 1)
                pe.wait_ge(o_done, TT)

                def scores(u):
                    x = units[u]
                    if u >= 2:
                        pe.wait_ge(p_ready, u - 1)
                    pe.matmul(ps[:, u % 2, 0:x["n"] * P], x["q"], x["k"], start=True, stop=True).then_inc(s_ready, 1)

                def turn(u):
                    x = units[u]
                    pe.wait_ge(p_ready, u + 1)
                    if u >= 2:
                        pe.wait_ge(pt_kept, u - 1)
                    for c in range(x["n"]):
                        ins = pe.transpose(ps[:, 2 + u % 2, c * P:(c + 1) * P], Pb[u % 2][:, c * P:(c + 1) * P], ident)
                    ins.then_inc(pt_ready, 1)

                def values(u):
                    x = units[u]
                    pe.wait_ge(pt_kept, u + 1)
                    if u >= 2:
                        pe.wait_ge(o_done, TT + u - 1)
                    for c in range(x["n"]):
                        ins = pe.matmul(ps[:, 4 + u % 2, 0:x["N"]], PTb[u % 2][:, c * P:(c + 1) * P], x["v"][c], start=(c == 0), stop=(c == x["n"] - 1))
                    ins.then_inc(o_ready, 1)

                scores(0)
                for u in range(NU + 1):
                    if u + 1 < NU:
                        scores(u + 1)
                    if u < NU:
                        turn(u)
                    if u:
                        values(u - 1)

            @block.scalar
            def _(act):
                for t in range(TT + 1):
                    act.activation(self.gate[0:rows(t), t, :], proj[0:rows(t), t, C_GN:C_GN + 24], ACT.Sigmoid).then_inc(gates, 1)
                act.wait_ge(kept2, 1)
                for v in range(2):
                    act.wait_ge(self.hid_ready, hid0 + v + 1)
                    act.activation(HT[:, v, :, :], ps[:, 4 + v, 0:2 * PCMP].rearrange("p (g n) -> p g n", g=2),
                                   ACT.Gelu_apprx_tanh, bias=self.hbias[:, v:v + 1]).then_inc(gelu, 1)
                for qt in range(TT):
                    act.wait_ge(c_max, qt + 1)
                    act.activation(sc[:, :, :], sc[:, :, :], ACT.Exp).then_inc(c_exp, 1)
                    for i in range(2):
                        act.wait_ge(c_t, 2 * qt + i + 1)
                        if qt:
                            act.wait_ge(c_o, qt)
                        act.copy(PTc[:, HPG * i:HPG * i + HPG, :], ps[0:32, i, :].rearrange("p (h t) -> p h t", h=HPG)).then_inc(c_tk, 1)

                def exp(u):
                    x = units[u]
                    L = x["n"] * P
                    act.wait_ge(nmax, u + 1)
                    if u >= 2:
                        act.wait_ge(pt_ready, u - 1)
                    if u >= 4:
                        act.wait_ge(o_done, TT + u - 3)
                    act.activation(Pb[u % 2][:, 0:L], ps[:, u % 2, 0:L], ACT.Exp, bias=nm[:, u % 2:u % 2 + 1],
                                   accum_out=rs[:, u % 4:u % 4 + 1]).then_inc(p_ready, 1)

                def keep(u):
                    L = units[u]["n"] * P
                    act.wait_ge(pt_ready, u + 1)
                    if u >= 2:
                        act.wait_ge(o_ready, u - 1)
                    act.copy(PTb[u % 2][:, 0:L], ps[:, 2 + u % 2, 0:L]).then_inc(pt_kept, 1)

                for u in range(NU + 1):
                    if u < NU:
                        exp(u)
                    if u:
                        keep(u - 1)

            @block.vector
            def _(dve):
                for q in range(2):
                    dve.wait_ge(turned, q + 1)
                    for g in range(NG):
                        bank = ps[g * HD:(g + 1) * HD, q, :].rearrange("p (c v t e) -> p c v t e", c=2, v=2, e=2)
                        for e in range(2):
                            dst = XT.rearrange("p (v g) t -> p v g t", v=2)[e * HD:(e + 1) * HD, :, g, q * P:(q + 1) * P]
                            ins = dve.tensor_copy(dst.rearrange("p v (c t) -> p c v t", c=2), bank[:, :, :, :, e])
                        ins.then_inc(kept, 1)
                dve.wait_ge(turned, 3)
                dve.tensor_copy(self.hbias[:, :], ps[:, 2, 0:2]).then_inc(kept2, 1)
                dve.wait_ge(small_ready, 1)
                dve.wait_ge(zeroed, 2)
                dve.tensor_copy(kc[:, :, 0:PCMP], ps[:, 3, 0:64].rearrange("p (g n) -> p g n", g=2)[:, :, 0:PCMP]).then_inc(small_kept, 1)
                dve.tensor_copy(vc[0:PCMP, :], ps[0:PCMP, 2, 0:P]).then_inc(small_kept, 1)
                dve.wait_ge(gates, TT + 1)
                ch = Chain(c_chain, dve)
                over = lambda a: a.unsqueeze(1).broadcast_to([P, NH, 32])
                each = lambda a: a.unsqueeze(2).broadcast_to([P, NH, 32])
                for qt in range(TT):
                    dve.wait_ge(c_s, qt + 1)
                    ch.step(dve.tensor_tensor(sc.rearrange("p (e h) n -> p e h n", e=2), ps[:, 5:7, 0:HPG * 32].rearrange("p e (h n) -> p e h n", h=HPG),
                                              self.C("cmpbias", 32 * qt, 32 * qt + 32).unsqueeze(1).unsqueeze(1).broadcast_to([P, 2, HPG, 32]), ALU.add))
                    ch.step(dve.tensor_reduce(cs[:, 0, :], sc[:, :, :], AX, ALU.max))
                    dve.tensor_tensor(sc[:, :, :], sc[:, :, :], each(cs[:, 0, :]), ALU.subtract).then_inc(c_max, 1)
                    dve.wait_ge(c_exp, qt + 1)
                    ch.step(dve.tensor_reduce(cs[:, 1, :], sc[:, :, :], AX, ALU.add))
                    ch.step(dve.reciprocal(cs[:, 1, :], cs[:, 1, :]))
                    ch.step(dve.tensor_tensor(sc[:, :, :], sc[:, :, :], each(cs[:, 1, :]), ALU.mult))
                    dve.tensor_tensor(sc[:, :, :], sc[:, :, :], over(self.C("cmpok", 32 * qt, 32 * qt + 32)), ALU.mult).then_inc(c_p, 1)
                    dve.wait_ge(c_o, qt + 1)
                    g0 = self.gate[:, qt, 0:3 * NH:3].unsqueeze(2).broadcast_to([P, NH, HD])
                    dve.tensor_tensor(proj[:, qt, 0:NH * HD].rearrange("p (h d) -> p h d", d=HD), ps[:, 7, :].rearrange("p (h d) -> p h d", d=HD), g0, ALU.mult).then_inc(o_done, 1)
                dve.wait_ge(o_done, TT)
                vch = Chain(v_chain, dve)

                def biggest(u):
                    x = units[u]
                    L = x["n"] * P
                    dve.wait_ge(s_ready, u + 1)
                    if x["causal"]:
                        vch.step(dve.tensor_tensor(ps[:, u % 2, L - P:L], ps[:, u % 2, L - P:L], self.C("causal"), ALU.add))
                    dve.tensor_reduce(nm[:, u % 2:u % 2 + 1], ps[:, u % 2, 0:L], AX, ALU.max, negate=True).then_inc(nmax, 1)

                def finish(u):
                    x = units[u]
                    out, r = ps[:, 4 + u % 2, 0:x["N"]], rg[:, u % 2:u % 2 + 1]
                    dve.wait_ge(o_ready, u + 1)
                    vch.step(dve.reciprocal(r, rs[:, u % 4:u % 4 + 1]))
                    if x["gate"] is None:
                        dve.tensor_scalar(x["dst"], out, r, None, ALU.mult).then_inc(o_done, 1)
                    else:
                        vch.step(dve.tensor_tensor(r, r, x["gate"], ALU.mult))
                        dve.wait_ge(o_done, TT + u)
                        dve.scalar_tensor_tensor(x["dst"], out, r, x["dst"], ALU.mult, ALU.add).then_inc(o_done, 1)

                for u in range(NU + 2):
                    if u < NU:
                        biggest(u)
                    if u >= 2:
                        finish(u - 2)
        self.free("w1", "w2", "hbias", "XT", "HT", "kcp", "vcp", "sc", "cs", "PTc", "Pb0", "Pb1", "PTb0", "PTb1", "nm", "rs", "rg",
                  "qT", "kT", "qmT", "kmT", "mem_kv")

    def load_pages(self, eng, b, j):
        pool_kv = self.I["cache_sel_kv"].rearrange("n r v g d -> n r (v g d)")
        dst = self.slots[j].rearrange("p (t c) -> p t c", t=PAGES)
        with eng.Fori(0, PAGES) as p:
            page = eng.value_load(self.pt[0:1, bass.ds(p + b * PAGES, 1)], min_val=0, max_val=pool_kv.shape[0] - 1)
            eng.dma_start(dst[:, bass.ds(p, 1)], pool_kv[bass.ds(page, 1)].rearrange("a r c -> r a c")).then_inc(self.filled[j], 16)

    def stage_sample_attention(self):
        nc, I, O, ps, proj = self.nc, self.I, self.O, self.ps, self.proj
        ident = self.C("ident")
        R4 = NB // 4
        slots = self.slots
        slots.update({j: self.sb(f"slot{j}", [P, PAGES * 256]) for j in (1, 3)})
        KT = [self.sb(f"KT{i}", [P, PAST]) for i in range(2)]
        PT = self.sb("PT", [P, PAGES, P])
        PTn = self.sb("PTn", [1, P])
        Ss = self.sb("Ss", [P, PAST + 1])
        pc, PTc = self.sb("pc", [P, NCMP]), self.sb("PTc", [P, P])
        imp = self.sb("imp", [P, 4, NSEL])
        bias = self.sb("bias", [P, R4, NSEL])
        top = self.sb("top", [P, 2, 8])
        st = self.sb("st", [P, 4])
        osb = [self.sb(f"osb{i}", [P, 512]) for i in range(2)]
        obr = KT[0][0:NB, 0:3 * NH * HD].rearrange("b (i c) -> b i c", i=3)
        scr = {n: nc.dram_tensor("scratch_" + n, (NB, 32, w), F32, kind="Internal").ap()
               for n, w in (("cmp", P), ("sel", P), ("win", P), ("mem", 512))}

        jobs = [(br, r) for r in range(R4) for br in ("sel", "win", "mem")]
        NTL = {"sel": PAGES, "win": WIN // P, "mem": MT // P}
        KU = {"sel": 4, "win": 1, "mem": 2}
        PU = {"sel": 5, "win": 2, "mem": 1}
        base = [0]
        for br, _ in jobs:
            base.append(base[-1] + 4 * KU[br] + PU[br])
        loads = []
        at = [0] * 4
        for br, _ in jobs:
            at = [a + 16 * (PAGES if br == "sel" else 1) for a in at]
            loads.append(list(at))

        S = self.sem
        filled, slot_free = self.filled, S("e_slot_free")
        e_s, e_max, e_exp, e_pt, e_ptk, e_imp, e_o, chain = (S("e1_" + x) for x in ("s", "max", "exp", "pt", "ptk", "imp", "o", "chain"))
        turned, kept, s_done, s_read, nmax, p_ready, o_ready, o_read = (S("e_turned"), [S("e_kept0"), S("e_kept1")], S("e_scores"), S("e_sread"),
                                                                        S("e_max"), S("e_exp"), S("e_out"), S("e_oread"))
        imp_kept, o_scr, back, merged, j_chain = S("e_impk"), [S("e_scr0"), S("e_scr1")], S("e_back"), S("e_merged"), S("e_jchain")

        def kv(br, j):
            n = NTL[br]
            w = 2 * MH * MD if br == "mem" else 2 * P
            return slots[j][:, 0:n * w].rearrange("p (t c) -> p t c", t=n)

        def load(eng, n, j):
            br, r = jobs[n]
            b = 4 * r + j
            if n:
                eng.wait_ge(slot_free, 4 * (n - 1) + j + 1)
            if br == "sel":
                self.load_pages(eng, b, j)
            else:
                src = I["cache_win_kv" if br == "win" else "cache_mem_kv"][b].rearrange("(t p) v g d -> p t (v g d)", p=P)
                eng.dma_start(kv(br, j)[:, :, :], src).then_inc(filled[j], 16)

        with nc.Block() as block:
            @block.sync
            def _(sp):
                for n in range(len(jobs)):
                    for j in (0, 2):
                        if n:
                            load(sp, n, j)
                for k in range(2):
                    sp.wait_ge(o_scr[k], 16 * (R4 + len(jobs)) // 2)
                for i, br in enumerate(("cmp", "sel", "win")):
                    for g in range(NG):
                        sp.dma_start(obr[:, i, g * HPG * HD:(g + 1) * HPG * HD].rearrange("b (h d) -> b h d", d=HD),
                                     scr[br][:, g * HPG:(g + 1) * HPG, g * HD:(g + 1) * HD]).then_inc(back, 16)
                for h in range(MH):
                    c = tok_col(C_QM) + h * MD
                    sp.dma_start(proj[0:NB, TT, c:c + MD], scr["mem"][:, h, h * MD:(h + 1) * MD]).then_inc(back, 16)

            @block.gpsimd
            def _(pool):
                for n in range(len(jobs)):
                    for j in (1, 3):
                        load(pool, n, j)

            @block.tensor
            def _(pe):
                for r in range(R4):
                    if r:
                        pe.wait_ge(e_exp, r)
                    for j in range(4):
                        ins = pe.matmul(ps[32 * j:32 * j + 32, 0, 0:NCMP], self.qblk[:, 4 * r + j, :], self.kcT[:, 4 * r + j, 0:NCMP], start=True, stop=True)
                    ins.then_inc(e_s, 1)
                    pe.wait_ge(chain, 3 * r + 2)
                    pe.transpose(ps[0:NCMP, 1, 0:P], pc[:, :], ident).then_inc(e_pt, 1)
                    pe.wait_ge(e_ptk, r + 1)
                    pe.matmul(ps[:, 2, 0:NSEL], PTc[0:NCMP, :], self.C("cmp2sel")[0:NCMP, :], start=True, stop=True).then_inc(e_imp, 1)
                    for j in range(4):
                        ins = pe.matmul(ps[32 * j:32 * j + 32, 3, 0:P], PTc[0:NCMP, 32 * j:32 * j + 32], self.vc[0:NCMP, 4 * r + j, :], start=True, stop=True)
                    ins.then_inc(e_o, 1)
                    pe.wait_ge(imp_kept, r + 1)
                    pe.matmul(ps[:, 4, 0:NSEL], self.C("group"), imp[:, 0, :], start=True, stop=True).then_inc(e_imp, 1)
                    pe.wait_ge(chain, 3 * r + 3)

                def bank(u):
                    if u >= 2:
                        pe.wait_ge(kept[u % 2], u // 2)
                    return ps[:, 5 + u % 2]

                for n, (br, r) in enumerate(jobs):
                    T = NTL[br]
                    u = base[n]
                    for j in range(4):
                        b = 4 * r + j
                        pe.wait_ge(filled[j], loads[n][j])
                        K = kv(br, j)
                        for i in range(KU[br]):
                            o = bank(u)
                            for c in range(4):
                                blk = K[:, i, c * MD:(c + 1) * MD] if br == "mem" else K[:, 4 * i + c, 0:P]
                                ins = pe.transpose(o[:, c * P:(c + 1) * P], blk, ident)
                            ins.then_inc(turned, 1)
                            u += 1
                        pe.wait_ge(kept[0], (u + 1) // 2)
                        pe.wait_ge(kept[1], u // 2)
                        if j == 0 and n:
                            pe.wait_ge(s_read, n)
                        row = slice(32 * j, 32 * j + 32)
                        if br == "mem":
                            for h in range(MH):
                                ins = pe.matmul(ps[row, 0, 0:MT], self.qmpad[:, b, h, :], KT[j % 2][:, h * MT:(h + 1) * MT], start=(h == 0), stop=(h == MH - 1))
                        else:
                            for i in range(T // 4):
                                pe.matmul(ps[row, i, :], self.qblk[:, b, :], KT[j % 2][:, i * 512:(i + 1) * 512], start=True, stop=True)
                            ins = pe.matmul(ps[row, 4, 0:1], self.qblk[:, b, :], self.knT[:, 0 if br == "sel" else 1, b:b + 1], start=True, stop=True)
                        ins.then_inc(s_done, 1)
                    pe.wait_ge(p_ready, n + 1)
                    for i in range(-(-T // 4)):
                        o = bank(u)
                        for c in range(min(4, T)):
                            ins = pe.transpose(o[:, c * P:(c + 1) * P], Ss[:, (4 * i + c) * P:(4 * i + c + 1) * P], ident)
                        ins.then_inc(turned, 1)
                        u += 1
                    if br != "mem":
                        pe.transpose(bank(u)[0:1, 0:P], Ss[:, T * P:T * P + 1], ident).then_inc(turned, 1)
                        u += 1
                    pe.wait_ge(kept[0], (u + 1) // 2)
                    pe.wait_ge(kept[1], u // 2)
                    if n:
                        pe.wait_ge(o_read, n)
                    for j in range(4):
                        row, V = slice(32 * j, 32 * j + 32), kv(br, j)
                        for t in range(T):
                            v = V[:, t, MH * MD:] if br == "mem" else V[:, t, P:2 * P]
                            ins = pe.matmul(ps[row, 7, 0:v.shape[1]], PT[:, t, row], v, start=(t == 0), stop=(br == "mem" and t == T - 1))
                        if br != "mem":
                            ins = pe.matmul(ps[row, 7, 0:P], PTn[:, row], self.vnew[:, 0 if br == "sel" else 1, 4 * r + j, :], start=False, stop=True)
                        ins.then_inc(slot_free, 1)

            def keep_keys(eng, copy, k, n):
                br, r = jobs[n]
                u = base[n]
                for j in range(4):
                    for i in range(KU[br]):
                        if u % 2 == k:
                            eng.wait_ge(turned, u + 1)
                            if 4 * n + j >= 2:
                                eng.wait_ge(s_done, 4 * n + j - 1)
                            src = ps[:, 5 + u % 2, :]
                            if br == "mem":
                                dst = KT[j % 2][:, 0:MH * MT].rearrange("p (h t) -> p h t", h=MH)[:, :, i * P:(i + 1) * P]
                                src = src.rearrange("p (h t) -> p h t", h=MH)
                            else:
                                dst = KT[j % 2][:, i * 512:(i + 1) * 512]
                            copy(dst, src).then_inc(kept[k], 1)
                        u += 1

            def keep_probs(eng, copy, k, n):
                br, r = jobs[n]
                T = NTL[br]
                u = base[n] + 4 * KU[br]
                if n:
                    eng.wait_ge(slot_free, 4 * n)
                for i in range(PU[br]):
                    if u % 2 == k:
                        eng.wait_ge(turned, u + 1)
                        if i < -(-T // 4):
                            w = min(4, T)
                            copy(PT[:, 4 * i:4 * i + w, :], ps[:, 5 + u % 2, 0:w * P].rearrange("p (t q) -> p t q", t=w)).then_inc(kept[k], 1)
                        else:
                            copy(PTn[:, :], ps[0:1, 5 + u % 2, 0:P]).then_inc(kept[k], 1)
                    u += 1

            def width(n):
                br, _ = jobs[n]
                return NTL[br] * P + (br != "mem")

            @block.scalar
            def _(act):
                for r in range(R4):
                    act.wait_ge(e_max, r + 1)
                    act.activation(pc[:, :], ps[:, 0, 0:NCMP], ACT.Exp, bias=st[:, 0:1], accum_out=st[:, 1:2]).then_inc(e_exp, 1)
                    act.wait_ge(e_pt, r + 1)
                    act.copy(PTc[0:NCMP, :], ps[0:NCMP, 1, 0:P]).then_inc(e_ptk, 1)
                    act.wait_ge(chain, 3 * r + 3)
                    act.dma_start(scr["cmp"].rearrange("b h c -> (b h) c")[P * r:P * r + P], osb[r % 2][:, 0:P]).then_inc(o_scr[r % 2], 16)
                for n, (br, r) in enumerate(jobs):
                    keep_keys(act, act.copy, 1, n)
                    act.wait_ge(nmax, n + 1)
                    act.activation(Ss[:, 0:width(n)], Ss[:, 0:width(n)], ACT.Exp, bias=st[:, 0:1], accum_out=st[:, 1:2]).then_inc(p_ready, 1)
                    keep_probs(act, act.copy, 1, n)
                    w = 512 if br == "mem" else P
                    act.wait_ge(o_read, n + 1)
                    act.dma_start(scr[br].rearrange("b h c -> (b h) c")[P * r:P * r + P], osb[n % 2][:, 0:w]).then_inc(o_scr[n % 2], 16)

            @block.vector
            def _(dve):
                ch = Chain(j_chain, dve)
                dve.wait_ge(self.vecs_loaded, 16 * len(VECS))
                for r in range(R4):
                    dve.wait_ge(e_s, r + 1)
                    dve.tensor_reduce(st[:, 0:1], ps[:, 0, 0:NCMP], AX, ALU.max, negate=True).then_inc(e_max, 1)
                    dve.wait_ge(e_exp, r + 1)
                    dve.reciprocal(st[:, 2:3], st[:, 1:2]).then_inc(chain, 1)
                    dve.wait_ge(chain, 3 * r + 1)
                    dve.tensor_scalar(pc[:, :], pc[:, :], st[:, 2:3], None, ALU.mult).then_inc(chain, 1)
                    dve.wait_ge(e_imp, 2 * r + 1)
                    dve.tensor_copy(imp[:, 0, :], ps[:, 2, 0:NSEL]).then_inc(imp_kept, 1)
                    dve.wait_ge(e_imp, 2 * r + 2)
                    ch.step(dve.tensor_copy(imp[:, 1, :], ps[:, 4, 0:NSEL]))
                    ch.step(dve.memset(imp[:, 1, 0:NSEL:NSEL - 1], FORCE))
                    ch.step(dve.max(top[:, 0, :], imp[:, 1, :]))
                    ch.step(dve.match_replace(imp[:, 2, :], top[:, 0, :], imp[:, 1, :], NEG))
                    ch.step(dve.max(top[:, 1, :], imp[:, 2, :]))
                    ch.step(dve.match_replace(imp[:, 3, :], top[:, 1, :], imp[:, 2, :], NEG))
                    ch.step(dve.tensor_tensor(bias[:, r, :], imp[:, 3, :], imp[:, 1, :], ALU.not_equal))
                    ch.step(dve.tensor_scalar(bias[:, r, :], bias[:, r, :], -1.0, -NEG, ALU.add, ALU.mult))
                    dve.wait_ge(e_o, r + 1)
                    dve.tensor_copy(osb[r % 2][:, 0:P], ps[:, 3, 0:P]).then_inc(chain, 1)
                dve.wait_ge(e_exp, R4)
                for n, (br, r) in enumerate(jobs):
                    T = NTL[br]
                    L = T * P
                    keep_keys(dve, dve.tensor_copy, 0, n)
                    dve.wait_ge(s_done, 4 * n + 4)
                    if n:
                        dve.wait_ge(turned, base[n])
                    if br == "sel":
                        dve.tensor_tensor(Ss[:, 0:L].rearrange("p (s k) -> p s k", k=64), ps[:, 0:4, :].rearrange("p b (s k) -> p (b s) k", k=64),
                                          bias[:, r, 0:NSEL - 1].unsqueeze(2).broadcast_to([P, NSEL - 1, 64]), ALU.add).then_inc(j_chain, 1)
                    else:
                        dve.tensor_copy(Ss[:, 0:L], ps[:, 0, 0:L]).then_inc(j_chain, 1)
                    ch.n += 1
                    if br != "mem":
                        dve.tensor_copy(Ss[:, L:L + 1], ps[:, 4, 0:1]).then_inc(j_chain, 1)
                        ch.n += 1
                    dve.wait_ge(j_chain, ch.n)
                    dve.sem_inc(s_read, 1)
                    if br == "win":
                        ch.step(dve.memset(Ss[:, 0:1], NEG))
                    dve.tensor_reduce(st[:, 0:1], Ss[:, 0:width(n)], AX, ALU.max, negate=True).then_inc(nmax, 1)
                    dve.wait_ge(p_ready, n + 1)
                    ch.step(dve.reciprocal(st[:, 2:3], st[:, 1:2]))
                    keep_probs(dve, dve.tensor_copy, 0, n)
                    dve.wait_ge(slot_free, 4 * n + 4)
                    w = 512 if br == "mem" else P
                    dve.wait_ge(o_scr[n % 2], 16 * (1 + n // 2))
                    dve.tensor_scalar(osb[n % 2][:, 0:w], ps[:, 7, 0:w], st[:, 2:3], None, ALU.mult).then_inc(o_read, 1)
                dve.wait_ge(back, 160)
                g = lambda i: self.gate[0:NB, TT, i:3 * NH:3].unsqueeze(2).broadcast_to([NB, NH, HD])
                hd = lambda a: a.rearrange("b (h d) -> b h d", d=HD)
                for i in range(3):
                    ch.step(dve.tensor_tensor(hd(obr[:, i, :]), hd(obr[:, i, :]), g(i), ALU.mult))
                ch.step(dve.tensor_tensor(obr[:, 0, :], obr[:, 0, :], obr[:, 1, :], ALU.add))
                ch.step(dve.tensor_tensor(proj[0:NB, TT, 0:NH * HD], obr[:, 0, :], obr[:, 2, :], ALU.add))
        self.free("pt", "slot0", "slot1", "slot2", "slot3", "KT0", "KT1", "PT", "PTn", "Ss", "pc", "PTc", "imp", "bias", "top", "st", "osb0", "osb1",
                  "kcT", "vc", "qblk", "qmpad", "knT", "vnew", "gate")

    def stage_gdn_project(self):
        I = self.I
        self.graw = self.sb("graw", [P, CC, 3 + NT])
        self.weight_setup()
        self.uH = self.sbr("uH", [P, KC, NT])
        U = (self.uH, self.uL)
        tiles, units = [], []
        for n in range(CONV // WCOLS):
            tiles.append([I["w_in"][:, C_GDN + WCOLS * n:C_GDN + WCOLS * n + WCOLS]])
            for m, tok in self.tile_units():
                units.append((n, lambda w, i, c, m=m: w[i][:, c, m * P:(m + 1) * P], lambda w, i, c, tok=tok: U[i][:, c, tok],
                              P, HALF, self.graw[:, WM * n + m, 3 + tok.start:3 + tok.stop]))
        self.dense("gdn", tiles, units, tiles, (lambda dve: self.split_acts(dve, self.uT, self.uH, self.uL), 1))
        self.weight_free()

    def stage_gdn_conv(self):
        nc, I, O, ps, proj, graw = self.nc, self.I, self.O, self.ps, self.proj, self.graw
        ident = self.C("ident")
        cT = self.cT = self.sb("cT", [P, CC, NT])
        self.beta, self.g = self.sb("beta", [P, TT + 1, GH]), self.sb("g", [P, TT + 1, GH])
        buf, bufT = self.sb("buf", [3 * NB, CONV]), self.sb("bufT", [P, CC, 3 * NB])
        newc = self.sb("newc", [3 + NB, CONV])
        tmp, tmp2 = self.sb("ctmp", [P, 2, CC, NB]), self.sb("gtmp", [P, 3, (TT + 1) * GH])
        nega = self.sb("nega", [P, GH])
        S = self.sem
        buf_in, turned, kept, convd, silu, gates, gact, stored, zeroed = (S("f_" + x) for x in ("buf", "turned", "kept", "conv", "silu", "g", "gact", "stored", "zero"))
        chain = S("f_chain")
        w = lambda j, c: self.gcol[:, 24 + 12 * j + c:25 + 12 * j + c]
        x0 = (TT + 1) * GH
        with nc.Block() as block:
            @block.sync
            def _(sp):
                sp.dma_start(buf[:, :], I["state_gdn_conv"].rearrange("b j c -> (b j) c")).then_inc(buf_in, 16)
                sp.dma_start(O["s_conv"][:, 0:2], I["state_gdn_conv"][:, 1:3]).then_inc(stored, 16)
                sp.wait_ge(kept, 6)
                sp.dma_start(O["p_conv"][0], newc[0:3, :]).then_inc(stored, 16)
                sp.dma_start(O["s_conv"][:, 2], newc[3:3 + NB, :]).then_inc(stored, 16)
                sp.wait_ge(stored, 48)

            @block.tensor
            def _(pe):
                for i in range(3):
                    for c in range(4):
                        ins = pe.transpose(ps[0:3 + NB, i, c * P:(c + 1) * P], graw[:, 4 * i + c, SEQ:SEQ + 3 + NB], ident)
                    ins.then_inc(turned, 1)
                pe.wait_ge(buf_in, 16)
                for i in range(3):
                    for c in range(4):
                        ins = pe.transpose(ps[:, 3 + i, c * P:c * P + 3 * NB], buf[:, (4 * i + c) * P:(4 * i + c + 1) * P], ident[0:3 * NB, 0:3 * NB])
                    ins.then_inc(turned, 1)

            @block.scalar
            def _(act):
                for i in range(3):
                    act.wait_ge(turned, i + 1)
                    act.copy(newc[:, 512 * i:512 * i + 512], ps[0:3 + NB, i, :]).then_inc(kept, 1)
                for i in range(3):
                    act.wait_ge(turned, 4 + i)
                    act.copy(bufT[:, 4 * i:4 * i + 4, :], ps[:, 3 + i, :].rearrange("p (c t) -> p c t", c=4)[:, :, 0:3 * NB]).then_inc(kept, 1)
                act.wait_ge(gates, 1)
                act.activation(self.beta[:, :, :], self.beta[:, :, :], ACT.Sigmoid).then_inc(gact, 1)
                act.wait_ge(gates, 2)
                act.activation(tmp2[:, 1, :], tmp2[:, 1, :], ACT.Exp, scale=-1.0).then_inc(gact, 1)
                act.activation(nega[:, :], self.V("gdn_A_log"), ACT.Exp).then_inc(gact, 1)
                act.wait_ge(gates, 3)
                act.activation(tmp2[:, 1, :], tmp2[:, 1, :], ACT.Ln).then_inc(gact, 1)
                act.activation(proj[:, 0:TT, tok_col(C_Z):tok_col(C_Z) + 512], proj[:, 0:TT, tok_col(C_Z):tok_col(C_Z) + 512], ACT.Silu).then_inc(silu, 1)
                act.activation(proj[0:NB, TT, tok_col(C_Z):tok_col(C_Z) + 512], proj[0:NB, TT, tok_col(C_Z):tok_col(C_Z) + 512], ACT.Silu).then_inc(silu, 1)
                act.wait_ge(convd, 1)
                act.activation(cT[:, :, SEQ:NT], cT[:, :, SEQ:NT], ACT.Silu).then_inc(silu, 1)
                for i in range(3):
                    act.wait_ge(convd, 2 + i)
                    act.activation(cT[:, 4 * i:4 * i + 4, 0:SEQ], cT[:, 4 * i:4 * i + 4, 0:SEQ], ACT.Silu).then_inc(silu, 1)

            @block.vector
            def _(dve):
                ch = Chain(chain, dve)
                ch.step(dve.memset(self.beta[:, :, :], 0.0))
                ch.step(dve.memset(self.g[:, :, :], 0.0))
                ba = lambda c, t, R: proj[0:R, t, tok_col(c):tok_col(c) + GH]
                ch.inc(dve.tensor_copy(self.g[:, 0:TT, :], proj[:, 0:TT, tok_col(C_A):tok_col(C_A) + GH]))
                ch.inc(dve.tensor_copy(self.g[0:NB, TT, :], ba(C_A, TT, NB)))
                ch.step(dve.tensor_copy(self.beta[:, 0:TT, :], proj[:, 0:TT, tok_col(C_B):tok_col(C_B) + GH]))
                dve.tensor_copy(self.beta[0:NB, TT, :], ba(C_B, TT, NB)).then_inc(gates, 1)
                ch.step(dve.tensor_tensor(self.g[:, :, :], self.g[:, :, :], self.V("gdn_dt_bias").unsqueeze(1).broadcast_to([P, TT + 1, GH]), ALU.add))
                gf = self.g.rearrange("p t h -> p (t h)")
                ch.step(dve.tensor_scalar(tmp2[:, 0, :], gf, 0.0, None, ALU.max))
                dve.scalar_tensor_tensor(tmp2[:, 1, :], gf, -1.0, gf, ALU.mult, ALU.max).then_inc(gates, 1)
                dve.wait_ge(gact, 2)
                dve.tensor_scalar(tmp2[:, 1, :], tmp2[:, 1, :], 1.0, None, ALU.add).then_inc(gates, 1)
                dve.wait_ge(gact, 4)
                ch.step(dve.tensor_tensor(gf, tmp2[:, 0, :], tmp2[:, 1, :], ALU.add))
                ch.step(dve.tensor_scalar(nega[:, :], nega[:, :], -1.0, None, ALU.mult))
                ch.step(dve.tensor_tensor(self.g[:, :, :], self.g[:, :, :], nega.unsqueeze(1).broadcast_to([P, TT + 1, GH]), ALU.mult))
                dve.wait_ge(kept, 6)
                cs = cT[:, :, SEQ:NT]
                wj = lambda j: self.gcol[:, 24 + 12 * j:36 + 12 * j].unsqueeze(2).broadcast_to([P, CC, NB])
                ch.step(dve.tensor_tensor(cs, graw[:, :, 3 + SEQ:3 + NT], wj(3), ALU.mult))
                bT = bufT.rearrange("p c (b j) -> p c j b", j=3)
                for j in range(3):
                    ch.step(dve.tensor_tensor(tmp[:, j % 2], bT[:, :, j, :], wj(j), ALU.mult))
                    if j < 2:
                        ch.step(dve.tensor_tensor(cs, cs, tmp[:, j % 2], ALU.add))
                    else:
                        dve.tensor_tensor(cs, cs, tmp[:, j % 2], ALU.add).then_inc(convd, 1)
                for half in range(3):
                    dve.memset(graw[:, 4 * half:4 * half + 4, 0:3], 0.0).then_inc(zeroed, 1)
                dve.wait_ge(zeroed, 3)
                for i in range(3):
                    for j in range(4):
                        for c in range(4 * i, 4 * i + 4):
                            if j == 0:
                                ins = dve.tensor_scalar(cT[:, c, 0:SEQ], graw[:, c, 0:SEQ], w(0, c), None, ALU.mult)
                            else:
                                dve.wait_ge(chain, ch.n - 3)
                                ins = dve.scalar_tensor_tensor(cT[:, c, 0:SEQ], graw[:, c, j:j + SEQ], w(j, c), cT[:, c, 0:SEQ], ALU.mult, ALU.add)
                            if j == 3 and c == 4 * i + 3:
                                ins.then_inc(convd, 1)
                            else:
                                ch.inc(ins)
        self.free("graw", "buf", "bufT", "newc", "ctmp", "gtmp", "nega")

    def stage_gdn_prompt(self):
        nc, I, O, ps, proj = self.nc, self.I, self.O, self.ps, self.proj
        ident, cT = self.C("ident"), self.cT
        names = ("qn", "kn", "kb", "kbe", "kd", "qe", "vb", "qnT", "knT", "kbT", "qeT", "E", "AT", "attT", "X0", "X1", "XT0", "XT1",
                 "Am", "Y", "nWT", "vn", "state")
        B = {n: self.sb("g_" + n, [P, GH, P]) for n in names}
        B["sq"] = self.sb("g_sq", [P, 2 * GH, P])
        X, XT = [B["X0"], B["X1"]], [B["XT0"], B["XT1"]]
        sc = self.sb("g_sc", [P, 12, GH])
        DEC, DL, LAST, ED, EDL, EL, RQ, RK, RQE, RKB, RKBE, RKD = range(12)
        so = self.sb("g_so", [P, GH])
        S = self.sem
        L = 7
        p = Steps(S("gp_pe"), ["dec", "tq", "tk", "tv", "tqn", "tkn", "tkb", "tqe", "at", "att", "Y0"]
                  + [n + str(l) for l in range(1, L) for n in ("Y", "XY", "XYT") if n + str(l) != f"XY{L - 1}"] + ["wt", "vn", "o", "ds"])
        v = Steps(S("gp_dve"), ["sc", "e1", "ss", "rt", "qn", "qe", "kn", "kb", "kbe", "kd", "vb", "e2", "AT", "attT", "Am0", "XT0", "X0"]
                  + [n + str(l) for l in range(1, L) for n in ("Am", "X", "XT") if n + str(l) != f"X{L - 1}"] + ["so", "state", "out"])
        a = Steps(S("gp_act"), ["ed", "E", "sqq", "sqk", "rt", "qnT", "knT", "kbT", "qeT"] + [f"Y{l}" for l in range(1, L)] + ["nWT", "vn", "sqo", "ro"])
        stored = S("gp_stored")
        bank = lambda b: ps[:, b, :].rearrange("p (h d) -> p h d", h=GH)
        bc = lambda x: x.unsqueeze(2).broadcast_to([P, GH, P])
        heads = lambda x: x.unsqueeze(1).broadcast_to([P, GH, P])
        with nc.Block() as block:
            @block.sync
            def _(sp):
                v.wait(sp, "state", TT - 1)
                sp.dma_start(O["p_state"][0].rearrange("h k v -> k h v"), B["state"][:, :, :]).then_inc(stored, 16)
                sp.wait_ge(stored, 16)

            @block.tensor
            def _(pe):
                def product(b, lhsT, rhs, name, t, start=True, stop=True):
                    for h in range(GH):
                        ins = pe.matmul(ps[:, b, h * P:(h + 1) * P], lhsT[:, h, :], rhs[:, h, :], start=start, stop=stop)
                    p.done(ins, name, t)

                for t in range(TT):
                    s = slice(t * P, (t + 1) * P)
                    if t:
                        v.wait(pe, "out", t - 1)
                    g = self.g[:, t, :]
                    for h in range(GH):
                        pe.matmul(ps[:, 0, h * P:(h + 1) * P], g[:, h:h + 1].broadcast_to([P, P]), self.C("upper"), start=True, stop=True)
                    pe.matmul(ps[:, 1, 0:GH], self.C("upper"), g, start=True, stop=True)
                    p.done(pe.matmul(ps[:, 1, GH:2 * GH], self.C("ones"), g, start=True, stop=True), "dec", t)
                    for i, name in enumerate(("tq", "tk", "tv")):
                        for h in range(GH):
                            ins = pe.transpose(ps[:, 2 + i, h * P:(h + 1) * P], cT[:, GH * i + h, s], ident)
                        p.done(ins, name, t)
                    for name, b in (("qn", 5), ("kn", 6), ("kb", 7), ("qe", 0)):
                        v.wait(pe, name, t)
                        for h in range(GH):
                            ins = pe.transpose(ps[:, b, h * P:(h + 1) * P], B[name][:, h, :], ident)
                        p.done(ins, "t" + name, t)
                    a.wait(pe, "kbT", t)
                    product(1, B["knT"], B["kbT"], "at", t)
                    product(2, B["knT"], B["qnT"], "att", t)
                    v.wait(pe, "Am0", t)
                    for h in range(GH):
                        ins = pe.matmul(ps[:, 3, h * P:(h + 1) * P], B["Am"][:, h, :], ident, start=True, stop=True)
                    p.done(ins, "Y0", t)
                    for l in range(1, L):
                        x, xt = X[(l + 1) % 2], XT[(l + 1) % 2]
                        v.wait(pe, f"Am{l}", t)
                        v.wait(pe, f"X{l - 1}", t)
                        product(3, B["Am"], x, f"Y{l}", t)
                        v.wait(pe, f"XT{l - 1}", t)
                        a.wait(pe, f"Y{l}", t)
                        if l < L - 1:
                            product(4, xt, B["Y"], f"XY{l}", t)
                        product(5, B["Y"], xt, f"XYT{l}", t)
                    v.wait(pe, f"XT{L - 1}", t)
                    xt = XT[(L - 1) % 2]
                    product(6, B["kbe"], xt, "wt", t)
                    a.wait(pe, "nWT", t)
                    for h in range(GH):
                        ins = pe.matmul(ps[:, 7, h * P:(h + 1) * P], xt[:, h, :], B["vb"][:, h, :], start=True, stop=(t == 0))
                        if t:
                            ins = pe.matmul(ps[:, 7, h * P:(h + 1) * P], B["nWT"][:, h, :], B["state"][:, h, :], start=False, stop=True)
                    p.done(ins, "vn", t)
                    a.wait(pe, "vn", t)
                    a.wait(pe, "qeT", t)
                    v.wait(pe, "attT", t)
                    for h in range(GH):
                        if t:
                            pe.matmul(ps[:, 0, h * P:(h + 1) * P], B["qeT"][:, h, :], B["state"][:, h, :], start=True, stop=False)
                        ins = pe.matmul(ps[:, 0, h * P:(h + 1) * P], B["attT"][:, h, :], B["vn"][:, h, :], start=(t == 0), stop=True)
                    p.done(ins, "o", t)
                    product(1, B["kd"], B["vn"], "ds", t)

            @block.scalar
            def _(act):
                def keep(b, dst, name, t, src="t", scale=1.0):
                    p.wait(act, src + name if src == "t" else src, t)
                    a.done(act.activation(B[dst][:, :, :], bank(b), ACT.Copy, scale=scale), dst, t)

                for t in range(TT):
                    v.wait(act, "sc", t)
                    a.done(act.activation(sc[:, ED:EL + 1, :], sc[:, DEC:LAST + 1, :], ACT.Exp), "ed", t)
                    v.wait(act, "e1", t)
                    a.done(act.activation(B["E"][:, :, :], B["E"][:, :, :], ACT.Exp), "E", t)
                    p.wait(act, "tk", t)
                    a.done(act.activation(B["sq"][:, 0:GH, :], bank(2), ACT.Square), "sqq", t)
                    a.done(act.activation(B["sq"][:, GH:, :], bank(3), ACT.Square), "sqk", t)
                    v.wait(act, "ss", t)
                    a.done(act.activation(sc[:, RQ:RK + 1, :], sc[:, RQ:RK + 1, :], ACT.Sqrt), "rt", t)
                    for name, b in (("qn", 5), ("kn", 6), ("kb", 7), ("qe", 0)):
                        p.wait(act, "t" + name, t)
                        a.done(act.copy(B[name + "T"][:, :, :], bank(b)), name + "T", t)
                    for l in range(1, L):
                        p.wait(act, f"Y{l}", t)
                        if l > 1:
                            p.wait(act, f"XYT{l - 1}", t)
                        a.done(act.copy(B["Y"][:, :, :], bank(3)), f"Y{l}", t)
                    p.wait(act, "wt", t)
                    a.done(act.activation(B["nWT"][:, :, :], bank(6), ACT.Copy, scale=-1.0), "nWT", t)
                    p.wait(act, "vn", t)
                    a.done(act.copy(B["vn"][:, :, :], bank(7)), "vn", t)
                    p.wait(act, "o", t)
                    a.done(act.activation(B["sq"][:, 0:GH, :], bank(0), ACT.Square), "sqo", t)
                    v.wait(act, "so", t)
                    a.done(act.activation(so[:, :], so[:, :], ACT.Sqrt), "ro", t)

            @block.vector
            def _(dve):
                ch = Chain(S("gp_chain"), dve)
                for t in range(TT):
                    beta = self.beta[:, t, :]
                    p.wait(dve, "dec", t)
                    ch.step(dve.tensor_copy(sc[:, DEC, :], ps[:, 1, 0:GH]))
                    ch.step(dve.tensor_copy(sc[:, LAST, :], ps[:, 1, GH:2 * GH]))
                    v.done(dve.tensor_tensor(sc[:, DL, :], sc[:, LAST, :], sc[:, DEC, :], ALU.subtract), "sc", t)
                    for h in range(GH):
                        ins = dve.tensor_scalar(B["E"][:, h, :], ps[:, 0, h * P:(h + 1) * P], sc[:, DEC, h:h + 1], 0.0, ALU.subtract, ALU.min)
                        if h < GH - 1:
                            ch.inc(ins)
                    dve.wait_ge(ch.sem, ch.n)
                    v.done(ins, "e1", t)
                    a.wait(dve, "sqk", t)
                    ch.step(dve.tensor_reduce(sc[:, RQ:RK + 1, :].rearrange("p a h -> p (a h)"), B["sq"][:, :, :], AX, ALU.add))
                    v.done(dve.tensor_scalar(sc[:, RQ:RK + 1, :], sc[:, RQ:RK + 1, :], EPS, None, ALU.add), "ss", t)
                    a.wait(dve, "rt", t)
                    ch.step(dve.reciprocal(sc[:, RQ:RK + 1, :], sc[:, RQ:RK + 1, :]))
                    ch.step(dve.tensor_scalar(sc[:, RQ, :], sc[:, RQ, :], float(GD) ** -0.5, None, ALU.mult))
                    ch.step(dve.tensor_tensor(sc[:, RKB, :], sc[:, RK, :], beta, ALU.mult))
                    ch.step(dve.tensor_tensor(sc[:, RQE, :], sc[:, RQ, :], sc[:, ED, :], ALU.mult))
                    ch.step(dve.tensor_tensor(sc[:, RKBE, :], sc[:, RKB, :], sc[:, ED, :], ALU.mult))
                    v.done(dve.tensor_tensor(sc[:, RKD, :], sc[:, RK, :], sc[:, EDL, :], ALU.mult), "rt", t)
                    v.wait(dve, "rt", t)
                    for name, b, r in (("qn", 2, RQ), ("qe", 2, RQE), ("kn", 3, RK), ("kb", 3, RKB), ("kbe", 3, RKBE), ("kd", 3, RKD)):
                        v.done(dve.tensor_tensor(B[name][:, :, :], bank(b), bc(sc[:, r, :]), ALU.mult), name, t)
                    p.wait(dve, "tv", t)
                    v.done(dve.tensor_tensor(B["vb"][:, :, :], bank(4), bc(beta), ALU.mult), "vb", t)
                    a.wait(dve, "E", t)
                    v.done(dve.tensor_tensor(B["E"][:, :, :], B["E"][:, :, :], heads(self.C("upper")), ALU.mult), "e2", t)
                    v.wait(dve, "e2", t)
                    p.wait(dve, "at", t)
                    v.done(dve.tensor_tensor(B["AT"][:, :, :], bank(1), B["E"][:, :, :], ALU.mult), "AT", t)
                    p.wait(dve, "att", t)
                    v.done(dve.tensor_tensor(B["attT"][:, :, :], bank(2), B["E"][:, :, :], ALU.mult), "attT", t)
                    v.wait(dve, "AT", t)
                    level = lambda l: heads(self.C("levels", l * P, (l + 1) * P))
                    v.done(dve.tensor_tensor(B["Am"][:, :, :], B["AT"][:, :, :], level(0), ALU.mult), "Am0", t)
                    v.wait(dve, "Am0", t)
                    v.done(dve.tensor_tensor(XT[0][:, :, :], heads(ident), B["Am"][:, :, :], ALU.subtract), "XT0", t)
                    p.wait(dve, "Y0", t)
                    v.done(dve.scalar_tensor_tensor(X[0][:, :, :], bank(3), -1.0, heads(ident), ALU.mult, ALU.add), "X0", t)
                    for l in range(1, L):
                        x, xt, y, yt = X[(l + 1) % 2], XT[(l + 1) % 2], X[l % 2], XT[l % 2]
                        p.wait(dve, f"Y{l - 1}", t)
                        v.wait(dve, f"XT{l - 1}", t)
                        v.done(dve.tensor_tensor(B["Am"][:, :, :], B["AT"][:, :, :], level(l), ALU.mult), f"Am{l}", t)
                        if l < L - 1:
                            p.wait(dve, f"XY{l}", t)
                            v.done(dve.scalar_tensor_tensor(y[:, :, :], bank(4), -1.0, x[:, :, :], ALU.mult, ALU.add), f"X{l}", t)
                        p.wait(dve, f"XYT{l}", t)
                        v.done(dve.scalar_tensor_tensor(yt[:, :, :], bank(5), -1.0, xt[:, :, :], ALU.mult, ALU.add), f"XT{l}", t)
                    a.wait(dve, "sqo", t)
                    ch.step(dve.tensor_reduce(so[:, :], B["sq"][:, 0:GH, :], AX, ALU.add))
                    v.done(dve.tensor_scalar(so[:, :], so[:, :], 1.0 / GD, EPS, ALU.mult, ALU.add), "so", t)
                    p.wait(dve, "ds", t)
                    if t == 0:
                        v.done(dve.tensor_copy(B["state"][:, :, :], bank(1)), "state", t)
                    else:
                        ch.step(dve.tensor_tensor(B["state"][:, :, :], B["state"][:, :, :], bc(sc[:, EL, :]), ALU.mult))
                        v.done(dve.tensor_tensor(B["state"][:, :, :], B["state"][:, :, :], bank(1), ALU.add), "state", t)
                    z = proj[:, t, tok_col(C_Z):tok_col(C_Z) + GH * GD].rearrange("p (h d) -> p h d", d=GD)
                    dst = proj[:, t, 512:1024].rearrange("p (h d) -> p h d", d=GD)
                    a.wait(dve, "ro", t)
                    ch.step(dve.reciprocal(so[:, :], so[:, :]))
                    ch.step(dve.tensor_tensor(dst, bank(0), bc(so), ALU.mult))
                    ch.step(dve.tensor_tensor(dst, dst, heads(self.V("gdn_o_norm")), ALU.mult))
                    v.done(dve.tensor_tensor(dst, dst, z, ALU.mult), "out", t)
                    v.wait(dve, "out", t)
        self.free(*("g_" + n for n in names), "g_sq", "g_sc", "g_so")

    def stage_gdn_sample(self):
        nc, I, O, ps, proj = self.nc, self.I, self.O, self.ps, self.proj
        ident, cT = self.C("ident"), self.cT
        HB = GH * NB
        S0 = self.sb("s_S0", [P, GH, NB, P])
        self.wt = [self.sb(f"wt{i}", [P, KC, WCOLS]) for i in range(2)]
        sq, qkn = self.sb("s_sq", [P, 2 * HB]), self.sb("s_qkn", [P, 2 * HB])
        rn = self.sb("s_rn", [P, 2 * HB])
        pairs = self.sb("s_pairs", [P, HB, 2])
        prod = self.sb("s_prod", [P, HB])
        gb = self.sb("s_gb", [NB, 2, HB])
        bcs = self.sb("s_bcs", [P, 3, HB])
        vn, oT = self.sb("s_vn", [P, HB]), self.sb("s_oT", [P, HB])
        rows_kv = self.sb("s_rows", [HB, 2, P])
        Vm = self.sb("s_Vm", [HB, HB, P])
        eg = self.sb("s_eg", [NB, GH])
        tmp = self.sb("s_tmp", [P, HB])
        so, sqo = self.sb("s_so", [NB, GH]), self.sb("s_sqo", [NB, GH, GD])
        S = self.sem
        s_in, stored = S("s_in"), S("s_stored")
        p = Steps(S("s_pe"), ["sums", "bc", "qk", "read", "rows", "orow"] + [f"add{i}" for i in range(8)])
        a = Steps(S("s_act"), ["eg", "rt", "rows", "sqo", "ro"])
        v = Steps(S("s_dve"), ["sq", "mean", "gb", "prod", "pairs", "vn", "oT", "Vm", "so", "out"] + [f"add{i}" for i in range(8)])
        two = lambda x: x.rearrange("p c b -> p (c b)")
        with nc.Block() as block:
            @block.sync
            def _(sp):
                for h in range(GH):
                    sp.dma_start(S0[:, h], I["state_gdn"][:, h].rearrange("b k v -> k b v")).then_inc(s_in, 16)
                for srcs, chunks in self.merge_tiles()[0:2]:
                    self.load_tile(sp, srcs, chunks)
                for h in range(GH):
                    v.wait(sp, f"add{2 * h + 1}", 0)
                    sp.dma_start(O["s_state"][:, h].rearrange("b k v -> k b v"), S0[:, h]).then_inc(stored, 16)
                sp.wait_ge(stored, 64)

            @block.tensor
            def _(pe):
                v.wait(pe, "sq", 0)
                p.done(pe.matmul(ps[:, 0, 0:2 * HB], self.C("ones"), sq[:, :], start=True, stop=True), "sums", 0)
                v.wait(pe, "gb", 0)
                p.done(pe.matmul(ps[:, 1, 0:2 * HB], self.C("ones")[0:NB, :], gb.rearrange("b i c -> b (i c)"), start=True, stop=True), "bc", 0)
                v.wait(pe, "prod", 0)
                p.done(pe.matmul(ps[:, 2, 0:HB], self.C("ones"), prod[:, :], start=True, stop=True), "qk", 0)
                v.wait(pe, "pairs", 0)
                pe.wait_ge(s_in, 64)
                for i in range(HB):
                    ins = pe.matmul(ps[:, 3, 2 * i:2 * i + 2], S0[:, i // NB, i % NB, :], pairs[:, i, :], start=True, stop=True)
                p.done(ins, "read", 0)
                v.wait(pe, "vn", 0)
                pe.transpose(ps[0:HB, 4, 0:P], qkn[:, HB:], ident)
                p.done(pe.transpose(ps[0:HB, 4, P:2 * P], vn[:, :], ident), "rows", 0)
                v.wait(pe, "oT", 0)
                for h in range(GH):
                    ins = pe.transpose(ps[0:NB, 5, h * P:(h + 1) * P], oT[:, h * NB:(h + 1) * NB], ident)
                p.done(ins, "orow", 0)
                v.wait(pe, "Vm", 0)
                for i in range(8):
                    if i >= 2:
                        v.wait(pe, f"add{i - 2}", 0)
                    p.done(pe.matmul(ps[:, 6 + i % 2, :], rows_kv[:, 0, :], Vm[:, 4 * i:4 * i + 4, :], start=True, stop=True), f"add{i}", 0)

            @block.scalar
            def _(act):
                a.done(act.activation(eg[:, :], self.g[0:NB, TT, :], ACT.Exp), "eg", 0)
                v.wait(act, "mean", 0)
                a.done(act.activation(rn[:, :], rn[:, :], ACT.Sqrt), "rt", 0)
                p.wait(act, "rows", 0)
                a.done(act.copy(rows_kv[:, :, :], ps[0:HB, 4, 0:2 * P].rearrange("p (i d) -> p i d", i=2)), "rows", 0)
                p.wait(act, "orow", 0)
                a.done(act.activation(sqo[:, :, :], ps[0:NB, 5, :].rearrange("p (h d) -> p h d", h=GH), ACT.Square), "sqo", 0)
                v.wait(act, "so", 0)
                a.done(act.activation(so[:, :], so[:, :], ACT.Sqrt), "ro", 0)

            @block.vector
            def _(dve):
                ch = Chain(S("s_chain"), dve)
                qk = cT[:, 0:2 * GH, SEQ:NT]
                v3 = lambda x: x.rearrange("p (c b) -> p c b", b=NB)
                v.done(dve.tensor_tensor(v3(sq), qk, qk, ALU.mult), "sq", 0)
                p.wait(dve, "sums", 0)
                v.done(dve.tensor_scalar(rn[:, :], ps[:, 0, 0:2 * HB], EPS, None, ALU.add), "mean", 0)
                a.wait(dve, "eg", 0)
                own = ident[0:NB, 0:NB].unsqueeze(1).broadcast_to([NB, GH, NB])
                each = lambda x: x.unsqueeze(2).broadcast_to([NB, GH, NB])
                ch.step(dve.tensor_tensor(v3(gb[:, 0]), own, each(self.beta[0:NB, TT, :]), ALU.mult))
                v.done(dve.tensor_tensor(v3(gb[:, 1]), own, each(eg), ALU.mult), "gb", 0)
                a.wait(dve, "rt", 0)
                ch.step(dve.reciprocal(rn[:, :], rn[:, :]))
                ch.step(dve.tensor_tensor(v3(qkn), qk, v3(rn), ALU.mult))
                ch.step(dve.tensor_scalar(qkn[:, 0:HB], qkn[:, 0:HB], float(GD) ** -0.5, None, ALU.mult))
                v.done(dve.tensor_tensor(prod[:, :], qkn[:, 0:HB], qkn[:, HB:], ALU.mult), "prod", 0)
                ch.step(dve.tensor_copy(pairs[:, :, 0], qkn[:, HB:]))
                v.done(dve.tensor_copy(pairs[:, :, 1], qkn[:, 0:HB]), "pairs", 0)
                p.wait(dve, "qk", 0)
                ch.step(dve.tensor_copy(bcs[:, 0:2, :], ps[:, 1, 0:2 * HB].rearrange("p (i c) -> p i c", i=2)))
                ch.step(dve.tensor_copy(bcs[:, 2, :], ps[:, 2, 0:HB]))
                p.wait(dve, "read", 0)
                kS, qS = ps[:, 3, 0:2 * HB:2], ps[:, 3, 1:2 * HB:2]
                ch.step(dve.tensor_tensor(tmp[:, :], kS, bcs[:, 1, :], ALU.mult))
                ch.step(dve.tensor_tensor(v3(tmp), cT[:, 2 * GH:3 * GH, SEQ:NT], v3(tmp), ALU.subtract))
                v.done(dve.tensor_tensor(vn[:, :], tmp[:, :], bcs[:, 0, :], ALU.mult), "vn", 0)
                v.wait(dve, "vn", 0)
                ch.step(dve.tensor_tensor(tmp[:, :], vn[:, :], bcs[:, 2, :], ALU.mult))
                ch.step(dve.tensor_tensor(oT[:, :], qS, bcs[:, 1, :], ALU.mult))
                v.done(dve.tensor_tensor(oT[:, :], oT[:, :], tmp[:, :], ALU.add), "oT", 0)
                a.wait(dve, "rows", 0)
                v.done(dve.tensor_tensor(Vm[:, :, :], rows_kv[:, 1, :].unsqueeze(1).broadcast_to([HB, HB, P]),
                                         ident[0:HB, 0:HB].unsqueeze(2).broadcast_to([HB, HB, P]), ALU.mult), "Vm", 0)
                a.wait(dve, "sqo", 0)
                ch.step(dve.tensor_reduce(so[:, :], sqo[:, :, :], AX, ALU.add))
                v.done(dve.tensor_scalar(so[:, :], so[:, :], 1.0 / GD, EPS, ALU.mult, ALU.add), "so", 0)
                a.wait(dve, "ro", 0)
                ch.step(dve.reciprocal(so[:, :], so[:, :]))
                dst = proj[0:NB, TT, 512:1024].rearrange("p (h d) -> p h d", d=GD)
                z = proj[0:NB, TT, tok_col(C_Z):tok_col(C_Z) + GH * GD].rearrange("p (h d) -> p h d", d=GD)
                ch.step(dve.tensor_tensor(dst, ps[0:NB, 5, :].rearrange("p (h d) -> p h d", h=GH), so.unsqueeze(2).broadcast_to([NB, GH, GD]), ALU.mult))
                ch.step(dve.tensor_tensor(dst, dst, self.V("gdn_o_norm")[0:NB].unsqueeze(1).broadcast_to([NB, GH, GD]), ALU.mult))
                v.done(dve.tensor_tensor(dst, dst, z, ALU.mult), "out", 0)
                dve.wait_ge(s_in, 64)
                for i in range(8):
                    Si = S0[:, i // 2, 4 * (i % 2):4 * (i % 2) + 4, :]
                    ch.step(dve.tensor_tensor(Si, Si, bcs[:, 1, 4 * i:4 * i + 4].unsqueeze(2).broadcast_to([P, 4, P]), ALU.mult))
                    p.wait(dve, f"add{i}", 0)
                    v.done(dve.tensor_tensor(Si, Si, ps[:, 6 + i % 2, :].rearrange("p (s d) -> p s d", s=4), ALU.add), f"add{i}", 0)
        self.free("s_S0", "s_sq", "s_qkn", "s_rn", "s_pairs", "s_prod", "s_gb", "s_bcs", "s_vn", "s_oT", "s_rows", "s_Vm", "s_eg", "s_tmp",
                  "s_so", "s_sqo", "cT", "beta", "g")

    def merge_tiles(self):
        I, tiles = self.I, []
        for br, w in enumerate((I["w_br_nsa"], I["w_br_gdn"], I["w_br_mem"])):
            for a in range(0, DM, WCOLS):
                tiles.append(([I["w_in"][:, C_GB + DM * br + a:C_GB + DM * br + a + WCOLS]], KC))
                tiles.append(([w[:, a:a + WCOLS]], 4))
        return tiles

    def tile_units(self):
        return [(m, slice(HALF * h, HALF * h + HALF)) for m in range(WM) for h in range(2)]

    def out_tiles(self):
        return [[self.I["w_out"][:, a:a + WCOLS]] for a in range(0, DM, WCOLS)]

    def stage_turn(self):
        nc, ps, proj = self.nc, self.ps, self.proj
        ident = self.C("ident")
        self.oH, self.oL = oH, oL = self.sbr("oH", [P, 3, 4, NT]), self.sbr("oL", [P, 3, 4, NT])
        turned, oH_kept, oL_kept = (self.sem("t_" + x) for x in ("turned", "oH_kept", "oL_kept"))
        NO = 3 * (TT + 1)
        cols = (0, 512, tok_col(C_QM))
        with nc.Block() as block:
            @block.tensor
            def _(pe):
                for i in range(NO):
                    br, t = i // (TT + 1), i % (TT + 1)
                    if i >= 8:
                        pe.wait_ge(oL_kept, i - 7)
                    for c in range(4):
                        ins = pe.transpose(ps[:, i % 8, c * P:c * P + rows(t)], proj[0:rows(t), t, cols[br] + c * P:cols[br] + (c + 1) * P],
                                           ident[0:rows(t), 0:rows(t)])
                    ins.then_inc(turned, 1)

            @block.vector
            def _(dve):
                for i in range(NO):
                    br, t = i // (TT + 1), i % (TT + 1)
                    dve.wait_ge(turned, i + 1)
                    cut = lambda x: x[:, br, :, t * P:t * P + rows(t)]
                    src = ps[:, i % 8, :].rearrange("p (c t) -> p c t", c=4)[:, :, 0:rows(t)]
                    self.high_low(dve, src, cut(oH), cut(oL), oH_kept, i + 1).then_inc(oL_kept, 1)
                dve.wait_ge(oL_kept, NO)
        self.free("proj")

    def stage_merge(self):
        nc, ps, oH, oL = self.nc, self.ps, self.oH, self.oL
        self.weight_setup()
        self.mergedT = self.sb("mergedT", [P, KC, NT])
        self.mergedH, self.mergedL = self.sbr("mergedH", [P, KC, NT]), self.sbr("mergedT", [P, KC, NT])
        sig = self.sb("sig", [P, WM, NT])
        prod = [self.sb(f"m_prod{i}", [P, HALF]) for i in range(2)]
        S = self.sem
        gated, taken, added = (S("m_" + x) for x in ("gated", "taken", "added"))
        acc, u0 = self.acc, self.units
        tiles, U = self.merge_tiles(), self.tile_units()
        NU, PAIRS = len(U), len(tiles) // 2
        BP = PAIRS // 3
        for n in range(len(tiles)):
            self.tile_end.append(u0 + NU * (n + 1))
        self.units += NU * len(tiles)
        X, O3 = (self.uH, self.uL), (oH, oL)
        with nc.Block() as block:
            @block.sync
            def _(sp):
                for srcs, chunks in tiles[2:]:
                    self.load_tile(sp, srcs, chunks)
                for srcs in self.out_tiles()[0:2]:
                    self.load_tile(sp, srcs)

            @block.tensor
            def _(pe):
                for q in range(PAIRS):
                    w = self.tile_ready(pe)
                    for i, (m, tok) in enumerate(U):
                        u = q * NU + i
                        if u >= 4:
                            pe.wait_ge(gated, u - 3)
                        self.product3(pe, ps[:, u % 4, 0:HALF], lambda i, c: w[i][:, c, m * P:(m + 1) * P], lambda i, c: X[i][:, c, tok]).then_inc(acc, 1)
                    w = self.tile_ready(pe)
                    for i, (m, tok) in enumerate(U):
                        u = q * NU + i
                        if u >= 4:
                            pe.wait_ge(taken, u - 3)
                        self.product3(pe, ps[:, 4 + u % 4, 0:HALF], lambda i, c: w[i][:, c, m * P:(m + 1) * P],
                                      lambda i, c: O3[i][:, q // BP, c, tok], 4).then_inc(acc, 1)

            @block.scalar
            def _(act):
                for q in range(PAIRS):
                    for i, (m, tok) in enumerate(U):
                        u = q * NU + i
                        act.wait_ge(acc, u0 + 2 * q * NU + i + 1)
                        if q:
                            act.wait_ge(taken, u - NU + 1)
                        act.activation(sig[:, m, tok], ps[:, u % 4, 0:HALF], ACT.Sigmoid).then_inc(gated, 1)

            @block.vector
            def _(dve):
                self.split_tile(dve, chunks=tiles[0][1])
                self.split_tile(dve, chunks=tiles[1][1])
                for q in range(PAIRS):
                    for i, (m, tok) in enumerate(U):
                        u = q * NU + i
                        dst, high, low = (x[:, WM * (q % BP) + m, tok] for x in (self.mergedT, self.mergedH, self.mergedL))
                        if i == 0 and 2 * q + 2 < len(tiles):
                            self.split_tile(dve, chunks=tiles[2 * q + 2][1])
                        dve.wait_ge(gated, u + 1)
                        dve.wait_ge(acc, u0 + (2 * q + 1) * NU + i + 1)
                        if q < BP:
                            dve.tensor_tensor(dst, ps[:, 4 + u % 4, 0:HALF], sig[:, m, tok], ALU.mult).then_inc(taken, 1)
                            continue
                        v = u - BP * NU
                        if v >= 2:
                            dve.wait_ge(added, v - 1)
                        dve.tensor_tensor(prod[v % 2], ps[:, 4 + u % 4, 0:HALF], sig[:, m, tok], ALU.mult).then_inc(taken, 1)
                        dve.wait_ge(taken, u + 1)
                        dve.tensor_tensor(dst, dst, prod[v % 2], ALU.add).then_inc(added, 1)
                        if q >= 2 * BP:
                            dve.wait_ge(added, v + 1)
                            self.split_acts(dve, dst, high, low)
                    if 2 * q + 3 < len(tiles):
                        self.split_tile(dve, chunks=tiles[2 * q + 3][1])
                dve.wait_ge(self.x_split.sem, self.x_split.n)
        self.free("oH", "oL", "sig", "m_prod0", "m_prod1", "uT", "uH")

    def stage_out(self):
        nc, I, ps = self.nc, self.I, self.ps
        h = self.h = self.sb("h", [P, TT + 1, DM])
        self.hT = self.sb("hT", [P, KC, NT])
        self.hH, self.hL = self.sbr("hH", [P, KC, NT]), self.sbr("hT", [P, KC, NT])
        x_in, x_in_sample, h_ready = self.sem("o_x"), self.sem("o_xs"), self.sem("o_h")
        self.norm_stage_setup("o")
        srcs = [(h[0:rows(t), t, :], rows(t), self.hT[:, :, t * P:t * P + rows(t)], 16) for t in range(TT + 1)]
        acc, u0 = self.acc, self.units
        tiles, UN = self.out_tiles(), TT + 1
        for n in range(len(tiles)):
            self.tile_end.append(u0 + UN * (n + 1))
        self.units += len(tiles) * UN
        X = (self.mergedH, self.mergedL)
        with nc.Block() as block:
            @block.sync
            def _(sp):
                sp.dma_start(h[:, 0:TT, :], I["x_prompt"][0].rearrange("(t p) d -> p t d", p=P)).then_inc(x_in, 16)
                sp.dma_start(h[0:NB, TT, :], I["x_sample"][:, 0, :]).then_inc(x_in_sample, 16)
                for srcs in tiles[2:]:
                    self.load_tile(sp, srcs)
                for n in range(2):
                    self.load_tile(sp, [I["w_ff1"][:, WCOLS * n:WCOLS * (n + 1)]])

            @block.tensor
            def _(pe):
                for n in range(len(tiles)):
                    w = self.tile_ready(pe)
                    for t in range(UN):
                        u = n * UN + t
                        if u >= 4:
                            pe.wait_ge(h_ready, u - 3)
                        self.product3(pe, ps[0:rows(t), 4 + u % 4, 0:WCOLS], lambda i, c: X[i][:, c, t * P:t * P + rows(t)],
                                      lambda i, c: w[i][:, c, :]).then_inc(acc, 1)
                self.norm_pe(pe, srcs)

            @block.scalar
            def _(act):
                self.norm_act(act, srcs, {t: (h_ready, UN * (len(tiles) - 1) + t + 1) for t in range(UN)})

            @block.vector
            def _(dve):
                self.split_tile(dve)
                dve.wait_ge(x_in, 16)
                dve.wait_ge(x_in_sample, 16)
                for n in range(len(tiles)):
                    for t in range(UN):
                        if t == 0 and n + 1 < len(tiles):
                            self.split_tile(dve)
                        R, u = rows(t), n * UN + t
                        dve.wait_ge(acc, u0 + u + 1)
                        hh = h[0:R, t, WCOLS * n:WCOLS * n + WCOLS]
                        dve.tensor_tensor(hh, hh, ps[0:R, 4 + u % 4, 0:WCOLS], ALU.add).then_inc(h_ready, 1)
                self.norm_dve(dve, srcs, [[x[:, :, t * P:t * P + rows(t)] for x in (self.hH, self.hL)] for t in range(UN)])
                dve.wait_ge(self.x_split.sem, self.x_split.n)
        self.free("ss", "xn0", "xn1", "nj", "mergedT", "mergedH")

    def stage_ffn(self):
        nc, I, O, ps, h = self.nc, self.I, self.O, self.ps, self.h
        fT, fH, fL = self.sb("fT", [P, KC, NT]), self.sbr("fH", [P, KC, NT]), self.sbr("fT", [P, KC, NT])
        yT = self.sb("yT", [P, KC, NT])
        positive = self.sb("positive", [P, 4, HALF])
        relu, squared, high, low, summed, copied, turned, added, stored, zeroed = (
            self.sem("ff_" + x) for x in ("relu", "squared", "high", "low", "summed", "copied", "turned", "added", "stored", "zeroed"))
        acc, u0, first = self.acc, self.units, self.tiles
        U, QUARTERS, HT = self.tile_units(), DFF // DM, DM // WCOLS
        NU, QT = len(U), 2 * HT
        QU = NU * HT
        slot = lambda j: (first + j) % 2
        at = [self.loaded_at[first + j % 2] + 16 * (j // 2) for j in range(QT + 1)]
        per = 16 * (QT // 2)
        X, F = (self.hH, self.hL), (fH, fL)

        def source(q, j):
            if j < HT:
                return I["w_ff1"][:, bass.ds(q * DM + j * WCOLS, WCOLS)]
            return I["w_ff2"][bass.ds(q * DM, DM), WCOLS * (j - HT):WCOLS * (j - HT) + WCOLS]

        with nc.Block() as block:
            @block.sync
            def _(sp):
                def load(q, j):
                    sp.wait_ge(self.w_split, q * QT + (first + j - 1))
                    sp.dma_start(self.wt[slot(j)][:, :, :], source(q, j).rearrange("(c p) n -> p c n", p=P)).then_inc(self.w_loaded[slot(j)], 16)

                for j in range(2, QT):
                    load(0, j)
                with sp.Fori(1, QUARTERS) as q:
                    for j in range(QT):
                        load(q, j)
                for t in range(TT + 1):
                    sp.wait_ge(added, 2 * (t + 1))
                    dst = O["y_prompt"][0, t * P:(t + 1) * P, :] if t < TT else O["y_sample"][:, 0, :]
                    sp.dma_start(dst, h[0:rows(t), t, :]).then_inc(stored, 16)
                sp.wait_ge(stored, 16 * (TT + 1))

            @block.tensor
            def _(pe):
                def quarter(q, start):
                    for j in range(QT):
                        pe.wait_ge(self.w_split, q * QT + (first + j + 1))
                        w = self.wh[slot(j)], self.wl[slot(j)]
                        for i, (m, tok) in enumerate(U):
                            k = (j % HT) * NU + i
                            out = ps[:, 4 * (j // HT) + i % 4, 0:HALF]
                            lhsT = lambda i, c: w[i][:, c, m * P:(m + 1) * P]
                            if j < HT:
                                if not start or k >= 4:
                                    pe.wait_ge(squared, q * QU + (k - 3))
                                self.product3(pe, out, lhsT, lambda i, c: X[i][:, c, tok]).then_inc(acc, 1)
                            else:
                                if j == HT and i == 0:
                                    pe.wait_ge(low, q * QU + QU)
                                if not start or k >= 4:
                                    pe.wait_ge(summed, q * QU + (k - 3))
                                self.product3(pe, out, lhsT, lambda i, c: F[i][:, c, tok]).then_inc(acc, 1)

                quarter(0, True)
                with pe.Fori(1, QUARTERS) as q:
                    quarter(q, False)
                for u in range(2 * (TT + 1)):
                    t, half = u // 2, u % 2
                    if u == 0:
                        pe.wait_ge(summed, QU * QUARTERS)
                    if u >= 8:
                        pe.wait_ge(added, u - 7)
                    for c in range(4):
                        ins = pe.transpose(ps[0:rows(t), u % 8, c * P:(c + 1) * P], yT[:, 4 * half + c, t * P:t * P + rows(t)], self.C("ident"))
                    ins.then_inc(turned, 1)

            @block.scalar
            def _(act):
                with act.Fori(0, QUARTERS) as q:
                    for k in range(QU):
                        act.wait_ge(acc, q * (2 * QU) + (u0 + k + 1))
                        act.activation(positive[:, k % 4, :], ps[:, k % 4, 0:HALF], ACT.Relu).then_inc(relu, 1)

            @block.vector
            def _(dve):
                def split(q, j):
                    n = first + j
                    dve.wait_ge(self.w_loaded[slot(j)], q * per + at[j])
                    dve.wait_ge(acc, q * (2 * QU) + (u0 + NU * (j - 1)))
                    self.high_low(dve, self.wt[slot(j)][:, :, :], self.wh[slot(j)][:, :, :], self.wl[slot(j)][:, :, :],
                                  self.w_high, q * QT + (n + 1)).then_inc(self.w_split, 1)

                def quarter(q, more):
                    for j in range(QT):
                        if j + 1 < QT or more:
                            split(q, j + 1)
                        for i, (m, tok) in enumerate(U):
                            k = (j % HT) * NU + i
                            chunk = WM * (j % HT) + m
                            if j < HT:
                                x, f = ps[:, k % 4, 0:HALF], fT[:, chunk, tok]
                                dve.wait_ge(relu, q * QU + (k + 1))
                                dve.tensor_tensor(f, x, positive[:, k % 4, :], ALU.mult).then_inc(squared, 1)
                                dve.wait_ge(squared, q * QU + (k + 1))
                                self.high_low(dve, f, fH[:, chunk, tok], fL[:, chunk, tok], high, q * QU + (k + 1)).then_inc(low, 1)
                            else:
                                y = yT[:, chunk, tok]
                                dve.wait_ge(acc, q * (2 * QU) + (u0 + QU + k + 1))
                                dve.tensor_tensor(y, y, ps[:, 4 + k % 4, 0:HALF], ALU.add).then_inc(summed, 1)

                dve.memset(yT[:, :, :], 0.0).then_inc(zeroed, 1)
                split(0, 0)
                dve.wait_ge(zeroed, 1)
                with dve.Fori(0, QUARTERS - 1) as q:
                    quarter(q, True)
                quarter(QUARTERS - 1, False)
                for u in range(2 * (TT + 1)):
                    t, half = u // 2, u % 2
                    hh = h[0:rows(t), t, 512 * half:512 * half + 512]
                    dve.wait_ge(turned, u + 1)
                    dve.tensor_tensor(hh, hh, ps[0:rows(t), u % 8, :], ALU.add).then_inc(added, 1)
        self.free("yT", "fT", "fH", "h", "hT", "hH", "positive")

    def stages(self):
        return [self.stage_compress, self.stage_norms, self.stage_project, self.stage_qk, self.stage_prompt_attention,
                self.stage_sample_attention, self.stage_gdn_project, self.stage_gdn_conv, self.stage_gdn_prompt, self.stage_gdn_sample,
                self.stage_turn, self.stage_merge, self.stage_out, self.stage_ffn]


_INS = ["x_prompt", "x_sample", "cache_cmp_kv", "cache_sel_kv", "cache_win_kv", "state_gdn", "state_gdn_conv", "cache_mem_kv",
        "page_table", "mem_prompt", "g_mix", "w_in", "nsa_q_norm", "nsa_k_norm", "cmp_pe", "cmp_w1", "cmp_w2", "gdn_conv_w",
        "gdn_A_log", "gdn_dt_bias", "gdn_o_norm", "g_mem", "w_mem_kv", "mem_q_norm", "mem_k_norm", "w_br_nsa", "w_br_gdn",
        "w_br_mem", "w_out", "g_ffn", "w_ff1", "w_ff2"]
_OUTS = [("y_prompt", (1, SEQ, DM)), ("y_sample", (NB, 1, DM)), ("p_cmp", (1, SEQ, 2, NG, HD)), ("p_sel", (1, SEQ, 2, NG, HD)),
         ("p_win", (1, WIN, 2, NG, HD)), ("p_state", (1, GH, GD, GD)), ("p_conv", (1, 3, CONV)), ("p_mem", (1, MT, 2, MH, MD)),
         ("s_cmp", (NB, 1, 2, NG, HD)), ("s_sel", (NB, 1, 2, NG, HD)), ("s_win", (NB, WIN, 2, NG, HD)),
         ("s_state", (NB, GH, GD, GD)), ("s_conv", (NB, 3, CONV))]


def kernel(**inputs):
    from concourse import bacc
    from concourse.bass_utils import run_bass_kernel_spmd

    nc = bacc.Bacc("TRN2", target_bir_lowering=False, num_devices=1)
    arrays, ins = {}, {}
    table, at = shape_constants()
    for name in _INS:
        a = np.ascontiguousarray(inputs[name])
        arrays["in_" + name] = a
        ins[name] = nc.dram_tensor("in_" + name, a.shape, mybir.dt.from_np(a.dtype), kind="ExternalInput").ap()
    arrays["in_table"] = table
    const = nc.dram_tensor("in_table", table.shape, F32, kind="ExternalInput").ap()
    outs = {n: nc.dram_tensor("out_" + n, s, F32, kind="ExternalOutput").ap() for n, s in _OUTS}
    Kernel(nc, ins, outs, (const, at)).build()
    r = run_bass_kernel_spmd(nc, [arrays], core_ids=[0])
    return tuple(r.results[0]["out_" + n] for n, _ in _OUTS)
```
